# Optimizing a Trainium2 kernel written in Bass

```python
import math
import jax
import jax.numpy as jnp
from jax import lax
import numpy as np

D_MODEL = 1024
BATCH = 1
SEQ = 512
DEPTH = 2
DEC_BATCH = 8
DEC_SEQ = 4
PAST_LEN = 2048
PAGE_SIZE = 128

H_A = 4
DK_A = 64
DV_A = 128
GATE_RANK = 16
GATE_TAU = 16.0
CHUNK = 64
H_B = 8
P_B = 64
N_B = 64
G_B = 2
CONV_W = 4
D_B = H_B * P_B
CONV_DIM = D_B + 2 * G_B * N_B
POOL_WINDOWS = (2, 4, 8, 16)
POOL_GROUP = 128
D_C = len(POOL_WINDOWS) * POOL_GROUP
POOL_BUF = max(POOL_WINDOWS) - 1
H_D = 8
HD_D = 64
D_D = H_D * HD_D
MOBA_BLOCK = 256
MOBA_TOPK = 3
MOBA_QBLOCK = 32
ROT_DIM = HD_D // 4
ROPE_THETA = 500000.0
N_GROUPS = 4
EXP_PER_GROUP = 8
TOP_FINE = 2
D_EXPERT = 256
D_AB_OUT = H_A * DV_A + D_B
D_CD_OUT = D_C + D_D
DN_ALPHA = (2 * DEPTH) ** 0.25
DN_BETA = (8 * DEPTH) ** -0.25
LN_EPS = 1e-5
RMS_EPS = 1e-6

kernel_name = 'hybrid_gla_ssd_pool_moba_hmoe_step'

def _split(t, sizes):
    offs = np.cumsum(sizes)[:-1].tolist()
    return jnp.split(t, offs, axis=-1)

def _layer_norm(x, g, b):
    xf = x.astype(jnp.float32)
    mu = jnp.mean(xf, axis=-1, keepdims=True)
    var = jnp.mean(jnp.square(xf - mu), axis=-1, keepdims=True)
    return ((xf - mu) * lax.rsqrt(var + LN_EPS) * g.astype(jnp.float32) + b.astype(jnp.float32)).astype(x.dtype)

def _rms_norm(x, g):
    xf = x.astype(jnp.float32)
    return (xf * lax.rsqrt(jnp.mean(xf * xf, axis=-1, keepdims=True) + RMS_EPS) * g.astype(jnp.float32)).astype(x.dtype)

def _post_norm(x, sub, g, b):
    return _layer_norm(DN_ALPHA * x + sub, g, b)

def _chunk_len(t):
    return CHUNK if t % CHUNK == 0 else t

def _chunks(t, n, c):
    return jnp.moveaxis(t.reshape(t.shape[0], n, c, *t.shape[2:]), 1, 0)

def _unchunk(t):
    t = jnp.moveaxis(t, 0, 1)
    return t.reshape(t.shape[0], t.shape[1] * t.shape[2], *t.shape[3:])

def _gla(q, k, v, log_a, s0):
    bsz, t = q.shape[:2]
    c = _chunk_len(t)
    n = t // c
    causal = jnp.tril(jnp.ones((c, c), bool))
    f32 = jnp.float32
    xs = tuple(_chunks(a.astype(f32), n, c) for a in (q, k, v, log_a))

    def step(s, inp):
        qi, ki, vi, ai = inp
        b = jnp.cumsum(ai, axis=1)
        b_last = b[:, -1]
        q_dec = qi * jnp.exp(b)
        k_dec = ki * jnp.exp(-b)
        att = jnp.where(causal, jnp.einsum('bihk,bjhk->bhij', q_dec, k_dec), 0.0)
        o = jnp.einsum('bhij,bjhv->bihv', att, vi) + jnp.einsum('bihk,bhkv->bihv', q_dec, s)
        k_end = ki * jnp.exp(b_last[:, None] - b)
        s = s * jnp.exp(b_last)[..., None] + jnp.einsum('bjhk,bjhv->bhkv', k_end, vi)
        return s, o

    s, o = lax.scan(step, s0.astype(f32), xs)
    return _unchunk(o), s.astype(s0.dtype)

def _ssd(xs, dt, a, bm, cm, h0):
    bsz, t = xs.shape[:2]
    c = _chunk_len(t)
    n = t // c
    f32 = jnp.float32
    rep = H_B // G_B
    bh = jnp.repeat(bm.astype(f32), rep, axis=2)
    ch = jnp.repeat(cm.astype(f32), rep, axis=2)
    xdt = xs.astype(f32) * dt[..., None]
    la = dt * a
    causal = jnp.tril(jnp.ones((c, c), bool))[None, :, :, None]

    def step(h, inp):
        xi, lai, bi, ci = inp
        cum = jnp.cumsum(lai, axis=1)
        seg = jnp.where(causal, cum[:, :, None, :] - cum[:, None, :, :], -jnp.inf)
        w = jnp.einsum('bihn,bjhn->bijh', ci, bi) * jnp.exp(seg)
        y = jnp.einsum('bijh,bjhp->bihp', w, xi) + jnp.einsum('bihn,bhpn->bihp', ci, h) * jnp.exp(cum)[..., None]
        dec = jnp.exp(cum[:, -1:, :] - cum)
        h = h * jnp.exp(cum[:, -1, :])[..., None, None] + jnp.einsum('bjhp,bjhn->bhpn', xi * dec[..., None], bi)
        return h, y

    h, y = lax.scan(step, h0.astype(f32), tuple(_chunks(z, n, c) for z in (xdt, la, bh, ch)))
    return _unchunk(y), h.astype(h0.dtype)

def _causal_conv(u, buf, w, b):
    t = u.shape[1]
    ext = jnp.concatenate([buf, u], axis=1)
    y = sum(ext[:, i:i + t] * w[i] for i in range(CONV_W)) + b
    return y, ext[:, -(CONV_W - 1):]

def _mixer_ab(x, gla0, ssm0, conv0, w_in, w_gate2, b_gate, gla_norm, conv_w, conv_b, dt_bias, a_log, d_skip, ssm_norm, w_out):
    bsz, t, _ = x.shape
    q, k, v, r, g_lr, z, xbc, dtr = _split(x @ w_in, (H_A * DK_A, H_A * DK_A, H_A * DV_A, H_A * DV_A, GATE_RANK, D_B, CONV_DIM, H_B))
    q = q.reshape(bsz, t, H_A, DK_A) * (DK_A ** -0.5)
    k = k.reshape(bsz, t, H_A, DK_A)
    v = v.reshape(bsz, t, H_A, DV_A)
    log_a = jax.nn.log_sigmoid((g_lr @ w_gate2 + b_gate).astype(jnp.float32)).reshape(bsz, t, H_A, DK_A) / GATE_TAU
    o_a, gla_new = _gla(q, k, v, log_a, gla0)
    o_a = _rms_norm(o_a.astype(x.dtype), gla_norm).reshape(bsz, t, H_A * DV_A) * jax.nn.silu(r)
    xbc, conv_new = _causal_conv(xbc, conv0, conv_w, conv_b)
    xs, bm, cm = _split(jax.nn.silu(xbc), (D_B, G_B * N_B, G_B * N_B))
    dt = jax.nn.softplus(dtr.astype(jnp.float32) + dt_bias.astype(jnp.float32))
    a = -jnp.exp(a_log.astype(jnp.float32))
    xs = xs.reshape(bsz, t, H_B, P_B)
    y, ssm_new = _ssd(xs, dt, a, bm.reshape(bsz, t, G_B, N_B), cm.reshape(bsz, t, G_B, N_B), ssm0)
    y = (y + d_skip.astype(jnp.float32)[:, None] * xs.astype(jnp.float32)).astype(x.dtype).reshape(bsz, t, D_B)
    y = _rms_norm(y * jax.nn.silu(z), ssm_norm)
    out = jnp.concatenate([o_a, y], axis=-1) @ w_out
    return out, gla_new, ssm_new, conv_new

def _pool_mix(u, buf, start, w_pool, pool_scale):
    bsz, t, _ = u.shape
    ext = jnp.concatenate([buf, u], axis=1).astype(jnp.float32)
    cs = jnp.concatenate([jnp.zeros((bsz, 1, D_C), jnp.float32), jnp.cumsum(ext, axis=1)], axis=1)
    end = cs[:, POOL_BUF + 1:POOL_BUF + 1 + t]
    pos = start + jnp.arange(t)
    outs = []
    for gi, w in enumerate(POOL_WINDOWS):
        lo, hi = gi * POOL_GROUP, (gi + 1) * POOL_GROUP
        s = end[..., lo:hi] - cs[:, POOL_BUF + 1 - w:POOL_BUF + 1 - w + t, lo:hi]
        cnt = jnp.minimum(w, pos + 1).astype(jnp.float32)[None, :, None]
        outs.append(jnp.einsum('btc,cd->btd', s / cnt - ext[:, POOL_BUF:, lo:hi], w_pool[gi].astype(jnp.float32)))
    mixed = jnp.concatenate(outs, axis=-1) * pool_scale.astype(jnp.float32)
    return mixed.astype(u.dtype), ext[:, -POOL_BUF:].astype(u.dtype)

def _rope(t, pos):
    half = ROT_DIM // 2
    inv = ROPE_THETA ** (-jnp.arange(half, dtype=jnp.float32) / half)
    ang = pos.astype(jnp.float32)[:, None] * inv
    cos = jnp.cos(ang)[None, :, None, :]
    sin = jnp.sin(ang)[None, :, None, :]
    tr = t[..., :ROT_DIM].astype(jnp.float32)
    x1, x2 = tr[..., :half], tr[..., half:]
    rot = jnp.concatenate([x1 * cos - x2 * sin, x2 * cos + x1 * sin], axis=-1).astype(t.dtype)
    return jnp.concatenate([rot, t[..., ROT_DIM:]], axis=-1)

def _attend(s_sel, v_sel, s_own, v_own):
    lead = s_own.shape[:3]
    n_sel = s_sel.shape[3] * s_sel.shape[4]
    p = jax.nn.softmax(jnp.concatenate([s_sel.reshape(*lead, n_sel), s_own], axis=-1), axis=-1)
    return (jnp.einsum('bhqrk,bhqrkd->bqhd', p[..., :n_sel].reshape(s_sel.shape), v_sel)
            + jnp.einsum('bhqk,bkhd->bqhd', p[..., n_sel:], v_own))

def _moba_prompt(q, k, v):
    bsz, t, h, hd = q.shape
    f32 = jnp.float32
    n_blk = -(-t // MOBA_BLOCK)
    pad = n_blk * MOBA_BLOCK - t
    k_blk = jnp.pad(k, ((0, 0), (0, pad), (0, 0), (0, 0))).reshape(bsz, n_blk, MOBA_BLOCK, h, hd)
    v_blk = jnp.pad(v, ((0, 0), (0, pad), (0, 0), (0, 0))).reshape(bsz, n_blk, MOBA_BLOCK, h, hd)
    k_mean = k_blk.astype(f32).mean(axis=2)
    top = min(MOBA_TOPK, (t - 1) // MOBA_BLOCK)
    scale = hd ** -0.5
    b_i = jnp.arange(bsz)[:, None, None, None]
    h_i = jnp.arange(h)[None, :, None, None]

    def one_block(i):
        q0 = i * MOBA_QBLOCK
        qb = lax.dynamic_slice_in_dim(q, q0, MOBA_QBLOCK, axis=1).astype(f32)
        blk = q0 // MOBA_BLOCK
        own_k = lax.dynamic_index_in_dim(k_blk, blk, axis=1, keepdims=False).astype(f32)
        own_v = lax.dynamic_index_in_dim(v_blk, blk, axis=1, keepdims=False).astype(f32)
        q_pos = q0 + jnp.arange(MOBA_QBLOCK)
        k_pos = blk * MOBA_BLOCK + jnp.arange(MOBA_BLOCK)
        s_own = jnp.einsum('bqhd,bkhd->bhqk', qb, own_k) * scale
        s_own = jnp.where(k_pos[None, :] <= q_pos[:, None], s_own, -jnp.inf)
        if top == 0:
            return jnp.einsum('bhqk,bkhd->bqhd', jax.nn.softmax(s_own, axis=-1), own_v)
        gate = jnp.einsum('bqhd,bnhd->bhqn', qb, k_mean)
        gate = jnp.where(jnp.arange(n_blk) < blk, gate, -jnp.inf)
        _, idx = lax.top_k(gate, top)
        valid = jnp.arange(top) < blk
        idx = jnp.where(valid, idx, 0)
        k_sel = k_blk[b_i, idx, :, h_i].astype(f32)
        v_sel = v_blk[b_i, idx, :, h_i].astype(f32)
        s_sel = jnp.einsum('bqhd,bhqrkd->bhqrk', qb, k_sel) * scale
        s_sel = jnp.where(valid[:, None], s_sel, -jnp.inf)
        return _attend(s_sel, v_sel, s_own, own_v)

    o = lax.map(one_block, jnp.arange(t // MOBA_QBLOCK))
    return _unchunk(o).astype(q.dtype)

def _moba_sample(q, k, v, cache_k, cache_v, page_table):
    db, s, h, hd = q.shape
    f32 = jnp.float32
    n_pages = page_table.shape[1]
    past = n_pages * PAGE_SIZE
    ppb = MOBA_BLOCK // PAGE_SIZE
    n_full = past // MOBA_BLOCK
    own_pages = n_full * ppb
    n_own_past = past - n_full * MOBA_BLOCK
    scale = hd ** -0.5
    qf = q.astype(f32)
    tail = page_table[:, own_pages:]
    own_k = jnp.concatenate([cache_k[tail].reshape(db, n_own_past, h, hd), k], axis=1).astype(f32)
    own_v = jnp.concatenate([cache_v[tail].reshape(db, n_own_past, h, hd), v], axis=1).astype(f32)
    k_pos = jnp.arange(n_own_past + s)
    q_pos = n_own_past + jnp.arange(s)
    s_own = jnp.einsum('bqhd,bkhd->bhqk', qf, own_k) * scale
    s_own = jnp.where(k_pos[None, :] <= q_pos[:, None], s_own, -jnp.inf)
    top = min(MOBA_TOPK, n_full)
    if top == 0:
        return jnp.einsum('bhqk,bkhd->bqhd', jax.nn.softmax(s_own, axis=-1), own_v).astype(q.dtype)
    k_past = cache_k[page_table[:, :own_pages]].reshape(db, n_full, MOBA_BLOCK, h, hd)
    k_mean = k_past.astype(f32).mean(axis=2)
    gate = jnp.einsum('bqhd,bnhd->bhqn', qf, k_mean)
    _, idx = lax.top_k(gate, top)
    logical = idx[..., None] * ppb + jnp.arange(ppb)
    phys = page_table[jnp.arange(db)[:, None, None, None, None], logical]
    h_i = jnp.arange(h)[None, :, None, None, None]
    k_sel = cache_k[phys, :, h_i].reshape(db, h, s, top, MOBA_BLOCK, hd).astype(f32)
    v_sel = cache_v[phys, :, h_i].reshape(db, h, s, top, MOBA_BLOCK, hd).astype(f32)
    s_sel = jnp.einsum('bqhd,bhqrkd->bhqrk', qf, k_sel) * scale
    return _attend(s_sel, v_sel, s_own, own_v).astype(q.dtype)

def _cd_front(x, pool_buf, start, w_in, w_pool, pool_scale):
    bsz, t, _ = x.shape
    u, q, k, v = _split(x @ w_in, (D_C, D_D, D_D, D_D))
    pooled, pool_new = _pool_mix(u, pool_buf, start, w_pool, pool_scale)
    pos = start + jnp.arange(t)
    q = _rope(q.reshape(bsz, t, H_D, HD_D), pos)
    k = _rope(k.reshape(bsz, t, H_D, HD_D), pos)
    v = v.reshape(bsz, t, H_D, HD_D)
    return pooled, pool_new, q, k, v

def _mixer_cd_prompt(x, w_in, w_pool, pool_scale, w_out):
    bsz, t, _ = x.shape
    pooled, pool_new, q, k, v = _cd_front(x, jnp.zeros((bsz, POOL_BUF, D_C), x.dtype), 0, w_in, w_pool, pool_scale)
    o = _moba_prompt(q, k, v)
    out = jnp.concatenate([pooled, o.reshape(bsz, t, D_D)], axis=-1) @ w_out
    return out, pool_new, k, v

def _mixer_cd_sample(x, pool_buf, cache_k, cache_v, page_table, w_in, w_pool, pool_scale, w_out):
    bsz, t, _ = x.shape
    past = page_table.shape[1] * PAGE_SIZE
    pooled, pool_new, q, k, v = _cd_front(x, pool_buf, past, w_in, w_pool, pool_scale)
    o = _moba_sample(q, k, v, cache_k, cache_v, page_table)
    out = jnp.concatenate([pooled, o.reshape(bsz, t, D_D)], axis=-1) @ w_out
    return out, pool_new, k, v

def _hier_moe(x, w_coarse, b_coarse, w_fine, b_fine, w_gate_up, w_down):
    bsz, t, d = x.shape
    xt = x.reshape(bsz * t, d)
    lc = (xt @ w_coarse + b_coarse).astype(jnp.float32)
    grp = jnp.argmax(lc, axis=-1)
    p_grp = jnp.take_along_axis(jax.nn.softmax(lc, axis=-1), grp[:, None], axis=-1)
    lf = (jnp.einsum('nd,gde->nge', xt, w_fine) + b_fine).astype(jnp.float32)
    lf_sel = jnp.take_along_axis(lf, grp[:, None, None], axis=1)[:, 0]
    top_v, top_i = lax.top_k(lf_sel, TOP_FINE)
    w_top = jax.nn.softmax(top_v, axis=-1) * p_grp
    gates = (jax.nn.one_hot(top_i, EXP_PER_GROUP, dtype=jnp.float32) * w_top[..., None]).sum(axis=1)
    out = jnp.zeros_like(xt)
    for g in range(N_GROUPS):
        gate_g = jnp.where((grp == g)[:, None], gates, 0.0).astype(x.dtype)
        hg, hu = jnp.split(jnp.einsum('nd,edf->nef', xt, w_gate_up[g]), 2, axis=-1)
        out = out + jnp.einsum('nef,efd->nd', jax.nn.silu(hg) * hu * gate_g[..., None], w_down[g])
    return out.reshape(bsz, t, d)

def setup_inputs(seed: int = 0) -> dict:
    key = jax.random.key(seed)
    ks = jax.random.split(key, 40)

    def nrm(i, shape, scale):
        return jax.random.normal(ks[i], shape, jnp.float32) * scale

    n_pages = PAST_LEN // PAGE_SIZE
    n_phys = (DEC_BATCH * n_pages * 5) // 4
    d_ab_in = 2 * H_A * DK_A + 2 * H_A * DV_A + GATE_RANK + D_B + CONV_DIM + H_B
    d_cd_in = D_C + 3 * D_D
    page_table = jax.random.permutation(ks[8], n_phys)[:DEC_BATCH * n_pages].reshape(DEC_BATCH, n_pages).astype(jnp.int32)
    dt0 = jnp.exp(jax.random.uniform(ks[16], (H_B,), jnp.float32, math.log(1e-3), math.log(1e-1)))
    return {
        'x_prompt': nrm(0, (BATCH, SEQ, D_MODEL), 1.0),
        'x_sample': nrm(1, (DEC_BATCH, DEC_SEQ, D_MODEL), 1.0),
        'state_gla': nrm(2, (DEC_BATCH, H_A, DK_A, DV_A), 0.5),
        'state_ssm': nrm(3, (DEC_BATCH, H_B, P_B, N_B), 0.5),
        'state_conv': nrm(4, (DEC_BATCH, CONV_W - 1, CONV_DIM), 1.0),
        'state_pool': nrm(5, (DEC_BATCH, POOL_BUF, D_C), 1.0),
        'cache_k': nrm(6, (n_phys, PAGE_SIZE, H_D, HD_D), 1.0),
        'cache_v': nrm(7, (n_phys, PAGE_SIZE, H_D, HD_D), 1.0),
        'page_table': page_table,
        'ab_w_in': nrm(9, (D_MODEL, d_ab_in), D_MODEL ** -0.5),
        'ab_w_gate2': nrm(10, (GATE_RANK, H_A * DK_A), GATE_RANK ** -0.5),
        'ab_b_gate': nrm(11, (H_A * DK_A,), 0.1),
        'ab_gla_norm': 1.0 + nrm(12, (DV_A,), 0.02),
        'ab_conv_w': nrm(13, (CONV_W, CONV_DIM), CONV_W ** -0.5),
        'ab_conv_b': nrm(14, (CONV_DIM,), 0.02),
        'ab_dt_bias': dt0 + jnp.log(-jnp.expm1(-dt0)),
        'ab_a_log': jnp.log(jax.random.uniform(ks[15], (H_B,), jnp.float32, 1.0, 16.0)),
        'ab_d_skip': 1.0 + nrm(17, (H_B,), 0.02),
        'ab_ssm_norm': 1.0 + nrm(18, (D_B,), 0.02),
        'ab_w_out': nrm(19, (D_AB_OUT, D_MODEL), D_AB_OUT ** -0.5 * DN_BETA),
        'cd_w_in': nrm(20, (D_MODEL, d_cd_in), D_MODEL ** -0.5),
        'cd_w_pool': nrm(21, (len(POOL_WINDOWS), POOL_GROUP, POOL_GROUP), POOL_GROUP ** -0.5),
        'cd_pool_scale': 1.0 + nrm(22, (D_C,), 0.02),
        'cd_w_out': nrm(23, (D_CD_OUT, D_MODEL), D_CD_OUT ** -0.5 * DN_BETA),
        'moe_w_coarse': nrm(24, (DEPTH, D_MODEL, N_GROUPS), D_MODEL ** -0.5),
        'moe_b_coarse': nrm(25, (DEPTH, N_GROUPS), 0.01),
        'moe_w_fine': nrm(26, (DEPTH, N_GROUPS, D_MODEL, EXP_PER_GROUP), D_MODEL ** -0.5),
        'moe_b_fine': nrm(27, (DEPTH, N_GROUPS, EXP_PER_GROUP), 0.01),
        'moe_w_gate_up': nrm(28, (DEPTH, N_GROUPS, EXP_PER_GROUP, D_MODEL, 2 * D_EXPERT), D_MODEL ** -0.5),
        'moe_w_down': nrm(29, (DEPTH, N_GROUPS, EXP_PER_GROUP, D_EXPERT, D_MODEL), D_EXPERT ** -0.5 * DN_BETA),
        'ln_g': 1.0 + nrm(30, (DEPTH, 2, D_MODEL), 0.02),
        'ln_b': nrm(31, (DEPTH, 2, D_MODEL), 0.02),
    }

def reference(x_prompt, x_sample, state_gla, state_ssm, state_conv, state_pool, cache_k, cache_v, page_table,
              ab_w_in, ab_w_gate2, ab_b_gate, ab_gla_norm, ab_conv_w, ab_conv_b, ab_dt_bias, ab_a_log, ab_d_skip,
              ab_ssm_norm, ab_w_out, cd_w_in, cd_w_pool, cd_pool_scale, cd_w_out,
              moe_w_coarse, moe_b_coarse, moe_w_fine, moe_b_fine, moe_w_gate_up, moe_w_down, ln_g, ln_b):
    ab = (ab_w_in, ab_w_gate2, ab_b_gate, ab_gla_norm, ab_conv_w, ab_conv_b, ab_dt_bias, ab_a_log, ab_d_skip, ab_ssm_norm, ab_w_out)
    cd = (cd_w_in, cd_w_pool, cd_pool_scale, cd_w_out)
    xp, xs = x_prompt, x_sample
    bp = xp.shape[0]
    dtp = xp.dtype
    for l in range(DEPTH):
        if l % 2 == 0:
            mp, gla_p, ssm_p, conv_p = _mixer_ab(xp, jnp.zeros((bp, H_A, DK_A, DV_A), dtp), jnp.zeros((bp, H_B, P_B, N_B), dtp),
                                                 jnp.zeros((bp, CONV_W - 1, CONV_DIM), dtp), *ab)
            ms, gla_s, ssm_s, conv_s = _mixer_ab(xs, state_gla, state_ssm, state_conv, *ab)
        else:
            mp, pool_p, k_p, v_p = _mixer_cd_prompt(xp, *cd)
            ms, pool_s, k_s, v_s = _mixer_cd_sample(xs, state_pool, cache_k, cache_v, page_table, *cd)
        xp = _post_norm(xp, mp, ln_g[l, 0], ln_b[l, 0])
        xs = _post_norm(xs, ms, ln_g[l, 0], ln_b[l, 0])
        moe = (moe_w_coarse[l], moe_b_coarse[l], moe_w_fine[l], moe_b_fine[l], moe_w_gate_up[l], moe_w_down[l])
        xp = _post_norm(xp, _hier_moe(xp, *moe), ln_g[l, 1], ln_b[l, 1])
        xs = _post_norm(xs, _hier_moe(xs, *moe), ln_g[l, 1], ln_b[l, 1])
    return (xp, xs, gla_p, ssm_p, conv_p, pool_p, k_p, v_p, gla_s, ssm_s, conv_s, pool_s, k_s, v_s)


_drawn_inputs = setup_inputs


def setup_inputs(seed=0):
    import zlib

    import numpy as np

    out = dict(_drawn_inputs(seed))
    spreads = {}
    factors = {'cache_k': 3.236,
     'cache_v': 2.876,
     'ab_gla_norm': 22.183,
     'ab_d_skip': 200.0,
     'ab_ssm_norm': 11.826,
     'cd_pool_scale': 22.413,
     'moe_b_coarse': 14.018,
     'moe_b_fine': 11.57}
    for name, (base, spread) in spreads.items():
        noise = np.random.default_rng([zlib.crc32(name.encode()), seed]).standard_normal(out[name].shape)
        drawn = base * np.exp(spread * noise) if base else spread * noise
        out[name] = jnp.asarray(drawn.astype(out[name].dtype))
    for name, factor in factors.items():
        out[name] = (out[name] * factor).astype(out[name].dtype)
    return out
```

```python
from contextlib import ExitStack

import numpy as np

import concourse.bass as bass
from concourse import mybir

F32 = mybir.dt.float32
I32 = mybir.dt.int32
ALU = mybir.AluOpType
ACT = mybir.ActivationFunctionType
AX = mybir.AxisListType

D = 1024
KD = D // 128
SEQ, NB, NS = 512, 8, 4
NTOK = SEQ + NB * NS
TILES = [(t, 128) for t in range(4)] + [(4, NB * NS)]
ALPHA = 4 ** 0.25
LN_EPS, RMS_EPS = 1e-5, 1e-6
PAST, PAGE, NPG = 2048, 128, 16
WINDOWS = (2, 4, 8, 16)
PBUF = 15
NEG = -1e30
NE, SLOT, DE = 32, 64, 256
NPAIR = (NE + (2 * NTOK - NE) // SLOT + 1) // 2
NTILE = 2 * NPAIR
NROW = NTILE * SLOT


def constants():
    p = np.arange(128)
    j, i = p[:, None], p[None, :]
    parts = {}
    parts["ident"] = np.eye(128)
    for name, c in (("p", 64), ("s", NS)):
        same = j // c == i // c
        parts["tri_" + name] = same & (j <= i)
        parts["suf_" + name] = same & (j > i)
        parts["neg_" + name] = np.where(same & (j <= i), 0.0, NEG)
    parts["ones"] = np.ones((128, 128))
    parts["before"] = j < i
    parts["causal"] = np.where(i <= j, 0.0, NEG)
    parts["cmask"] = p[:, None] // 64 == np.arange(2)
    parts["bmask"] = p[:, None] // NS == np.arange(NB)
    parts["lt8"] = np.broadcast_to((np.arange(8)[:, None] > np.arange(8)[None, :]).reshape(1, 64), (128, 64))
    cnt = np.zeros((4, 16))
    for g, w in enumerate(WINDOWS):
        cnt[g, :PBUF] = 1.0 / np.minimum(w, np.arange(PBUF) + 1)
    parts["invcnt"] = np.broadcast_to(cnt.reshape(1, 64), (128, 64))
    parts["pidx"] = p[:, None]
    parts["p32"] = p[:, None] % 32
    parts["iota"] = np.broadcast_to(p[None, :], (128, 128))
    parts["m128"] = np.broadcast_to(128 * np.arange(NPAIR + 1)[None, :], (128, NPAIR + 1))
    tok = p[:, None] + 128 * np.arange(5)
    parts["valid"] = tok < NTOK
    parts["tokid"] = np.where(tok < NTOK, tok, 0)
    parts["m64"] = np.broadcast_to(SLOT * np.arange(9)[None, :], (128, 9))
    parts["tile"] = np.broadcast_to(np.arange(NTILE)[None, :], (128, NTILE))
    parts["ownneg"] = np.where(np.arange(NS)[None, :] <= p[:, None] % NS, 0.0, NEG)
    for g in range(2):
        parts[f"ownb{g}"] = np.repeat(p[:, None] // 32 + 4 * g == np.arange(NB)[None, :], NS, axis=1)
    parts["hmask"] = (p[:, None] // NS) % 8 == np.arange(8)
    parts["sumh"] = ((p[:, None] // 32) * NS + p[:, None] % NS) == np.arange(16)[None, :]
    half = 8
    inv = (np.float32(500000.0) ** (-np.arange(half, dtype=np.float32) / np.float32(half))).astype(np.float32)
    pos = np.concatenate([np.arange(SEQ), PAST + np.tile(np.arange(NS), NB), np.zeros(96)]).astype(np.float32)
    ang = (pos[:, None] * inv[None, :]).astype(np.float32)
    rope = np.concatenate([np.cos(ang), np.sin(ang)], axis=1).astype(np.float32)
    parts["rope"] = rope.reshape(5, 128, 16).transpose(1, 0, 2).reshape(128, 80)
    at, cols, out = 0, {}, []
    for name, a in parts.items():
        a = np.asarray(a, np.float32).reshape(128, -1)
        cols[name] = (at, at + a.shape[1])
        at += a.shape[1]
        out.append(a)
    return np.ascontiguousarray(np.concatenate(out, axis=1)), cols


class Count:

    def __init__(self, eng, sem):
        self.eng, self.sem, self.n = eng, sem, 0

    def add(self, ins):
        ins.then_inc(self.sem, 1)
        self.n += 1

    def wait(self):
        self.eng.wait_ge(self.sem, self.n)

    def step(self, ins):
        self.add(ins)
        self.wait()


class Scope(ExitStack):
    used, stores = [], {}

    def __init__(self, nc, name):
        super().__init__()
        self.nc, self.name = nc, name

    def sb(self, name, shape, dt=F32):
        return self.enter_context(self.nc.sbuf_tensor(f"{self.name}_{name}", shape, dt))

    def ps(self, name, cols=512):
        return self.enter_context(self.nc.psum_tensor(f"{self.name}_psum_{name}", [128, cols], F32))

    def sem(self, name):
        if name == "stored":
            return self.stores[self.name]
        sem = self.enter_context(self.nc.semaphore(f"{self.name}_{name}"))
        self.used.append(sem.num)
        return sem

    def block(self):
        return self.enter_context(self.nc.Block())


def tok0(t):
    return 128 * t


def reset_stage(nc):
    nums, Scope.used = sorted(set(Scope.used)), []
    with Scope(nc, "reset") as s:
        block = s.block()

        @block.sync
        def _(sp):
            start = nums[0]
            for a, b in zip(nums, nums[1:] + [None]):
                if b != a + 1:
                    sp.sem_clear(range(start, a + 1))
                    start = b


def transpose_stage(nc, name, C, src, dst, chunks=KD):
    units = [(t, P, h) for t, P in TILES for h in range(chunks // 4)]
    with Scope(nc, name) as s:
        ps = [s.ps(f"p{i}") for i in range(4)]
        transposed, by_act, by_dve = s.sem("transposed"), s.sem("by_act"), s.sem("by_dve")
        block = s.block()

        @block.tensor
        def _(pe):
            for u, (t, P, h) in enumerate(units):
                if u >= 4:
                    pe.wait_ge(by_dve if u % 2 else by_act, u // 2 - 1)
                for c in range(4):
                    last = nc.tensor.transpose(ps[u % 4][:, c * P:(c + 1) * P],
                                               src[:P, t, (4 * h + c) * 128:(4 * h + c + 1) * 128],
                                               C("ident")[:P, :P])
                last.then_inc(transposed, 1)

        def out_in(u):
            t, P, h = units[u]
            return (dst[:, 4 * h:4 * h + 4, tok0(t):tok0(t) + P],
                    ps[u % 4][:, :4 * P].rearrange("p (c n) -> p c n", c=4))

        @block.scalar
        def _(act):
            for u in range(0, len(units), 2):
                act.wait_ge(transposed, u + 1)
                o, i = out_in(u)
                nc.scalar.activation(o, i, ACT.Copy).then_inc(by_act, 1)

        @block.vector
        def _(dve):
            for u in range(1, len(units), 2):
                dve.wait_ge(transposed, u + 1)
                o, i = out_in(u)
                nc.vector.tensor_copy(o, i).then_inc(by_dve, 1)


class Job:

    def __init__(self, piece, M, N, lhsT, rhs, by, copy):
        self.piece, self.M, self.N, self.lhsT, self.rhs, self.by, self.copy = piece, M, N, lhsT, rhs, by, copy


def project_stage(nc, name, w_dram, pieces, width, xT, jobs_of, nbuf=3):
    with Scope(nc, name) as s:
        ring = [s.sb(f"w{i}", [128, KD, width]) for i in range(nbuf)]
        ps = [s.ps(f"p{i}") for i in range(8)]
        loaded = [s.sem(f"loaded{i}") for i in range(nbuf)]
        summed, by_act, by_dve = s.sem("summed"), s.sem("by_act"), s.sem("by_dve")
        jobs = [j for n in range(len(pieces)) for j in jobs_of(n, ring[n % nbuf])]
        done = {"act": by_act, "dve": by_dve}
        last_of = [max(i for i, j in enumerate(jobs) if j.piece == n) for n in range(len(pieces))]
        block = s.block()

        @block.sync
        def _(sp):
            for n, (a, b) in enumerate(pieces):
                if n >= nbuf:
                    sp.wait_ge(summed, last_of[n - nbuf] + 1)
                sp.dma_start(ring[n % nbuf][:, :, 0:b - a],
                             w_dram.rearrange("(k p) n -> p k n", p=128)[:, :, a:b]).then_inc(loaded[n % nbuf], 16)

        @block.tensor
        def _(pe):
            for i, j in enumerate(jobs):
                if i == 0 or jobs[i - 1].piece != j.piece:
                    pe.wait_ge(loaded[j.piece % nbuf], 16 * (j.piece // nbuf + 1))
                if i >= 8:
                    pe.wait_ge(done[jobs[i - 8].by], sum(q.by == jobs[i - 8].by for q in jobs[:i - 7]))
                for k in range(KD):
                    last = nc.tensor.matmul(ps[i % 8][:j.M, :j.N], j.lhsT(k), j.rhs(k),
                                            start=(k == 0), stop=(k == KD - 1))
                last.then_inc(summed, 1)

        @block.scalar
        def _(act):
            for i, j in enumerate(jobs):
                if j.by == "act":
                    act.wait_ge(summed, i + 1)
                    j.copy(ps[i % 8][:j.M, :j.N]).then_inc(by_act, 1)

        @block.vector
        def _(dve):
            for i, j in enumerate(jobs):
                if j.by == "dve":
                    dve.wait_ge(summed, i + 1)
                    j.copy(ps[i % 8][:j.M, :j.N]).then_inc(by_dve, 1)


def residual_norm_stage(nc, name, X, mv, lng, lnb, load, product=None):
    with Scope(nc, name) as s:
        stats = s.sb("stats", [128, 5, 2, 6])
        gb = s.sb("gb", [128, 2, D])
        rstd = s.sb("rstd", [128, 5])
        loaded, var_ready, root, dv, scaled, shifted = (s.sem(x) for x in (
            "loaded", "var_ready", "root", "dve_steps", "scaled", "shifted"))
        block = s.block()

        @block.sync
        def _(sp):
            sp.dma_start(gb[:, 0, :], lng.partition_broadcast(128)).then_inc(loaded, 16)
            sp.dma_start(gb[:, 1, :], lnb.partition_broadcast(128)).then_inc(loaded, 16)

        @block.vector
        def _(dve):
            c = Count(dve, dv)
            c.step(nc.vector.memset(mv[:, :, :], 1.0))
            for t, P in TILES:
                for h in range(2):
                    c.add(nc.vector.bn_stats(stats[:P, t, h, :], X[:P, t, h * 512:(h + 1) * 512]))
            c.wait()
            for t, P in TILES:
                c.add(nc.vector.bn_aggr(mv[:P, t, :], stats[:P, t, :, :].rearrange("p a b -> p (a b)")))
            c.wait()
            nc.vector.tensor_scalar(rstd[:, :], mv[:, :, 1], LN_EPS, None, ALU.add).then_inc(var_ready, 1)
            dve.wait_ge(root, 1)
            c.step(nc.vector.reciprocal(rstd[:, :], rstd[:, :]))
            for t, P in TILES:
                c.add(nc.vector.tensor_scalar(X[:P, t, :], X[:P, t, :], mv[:P, t, 0:1], rstd[:P, t:t + 1],
                                              ALU.subtract, ALU.mult))
            dve.wait_ge(loaded, 32)
            for t, P in TILES:
                dve.wait_ge(dv, c.n - 4 + t)
                nc.vector.tensor_tensor(X[:P, t, :], X[:P, t, :], gb[:P, 0, :], ALU.mult).then_inc(scaled, 1)

        @block.scalar
        def _(act):
            act.wait_ge(var_ready, 1)
            nc.scalar.activation(rstd[:, :], rstd[:, :], ACT.Sqrt).then_inc(root, 1)

        @block.gpsimd
        def _(pool):
            pool.wait_ge(loaded, 32)
            for t, P in TILES:
                pool.wait_ge(scaled, t + 1)
                nc.gpsimd.tensor_tensor(X[:P, t, :], X[:P, t, :], gb[:P, 1, :], ALU.add).then_inc(shifted, 1)


def out_jobs(nc, X, mixT):
    def jobs_of(n, w):
        out = []
        for t, P in TILES:
            def copy(src, t=t, P=P):
                cols = X[:P, t, n * 512:(n + 1) * 512]
                return nc.vector.scalar_tensor_tensor(out=cols, in0=cols, scalar=ALPHA, in1=src,
                                                      op0=ALU.mult, op1=ALU.add)
            out.append(Job(n, P, 512, lambda k, t=t, P=P: mixT[:, k, tok0(t):tok0(t) + P],
                           lambda k: w[:, k, 0:512], "dve", copy))
        return out
    return jobs_of


def mixer_ab(nc, A, X, C):
    with Scope(nc, "ab") as L:
        v = L.sb("v", [128, 5, 512])
        rs = L.sb("rs", [128, 5, 512])
        zs = L.sb("zs", [128, 5, 512])
        qT = L.sb("qT", [128, 2, NTOK])
        kT = L.sb("kT", [128, 2, NTOK])
        xbcP = L.sb("xbcP", [128, 6, 3 + SEQ])
        xbcS = L.sb("xbcS", [128, 6, NB, 3 + NS])
        gT = L.sb("gT", [16, NTOK])
        soft = L.sb("soft", [128, 5, 264])
        xbcC = L.sb("xbcC", [128, 6, NTOK])
        las = L.sb("las", [128, 5, 8])
        lam = L.sb("lam", [128, 4, 2, 8])
        lams = L.sb("lams", [32, NB, 8])
        yo = L.sb("yo", [128, 5, 1024])
        heads = L.sb("heads", [128, 16])
        norms = L.sb("norms", [128, 640])

        with Scope(nc, "abp") as s:
            xT = s.sb("xT", [128, KD, NTOK])
            transpose_stage(nc, "abt", C, X, xT)
            pieces = [(0, 512), (512, 1024), (1024, 1536), (1536, 2064), (2064, 2448), (2448, 2840)]

            def jobs_of(n, w):
                out = []

                def feat(c0, M, prompt, sample, scale=1.0):
                    out.append(Job(n, M, 512, lambda k: w[:, k, c0:c0 + M], lambda k: xT[:, k, 0:512], "act",
                                   lambda p: nc.scalar.activation(prompt, p, ACT.Copy, scale=scale)))
                    out.append(Job(n, M, 32, lambda k: w[:, k, c0:c0 + M], lambda k: xT[:, k, 512:544], "dve",
                                   lambda p: nc.vector.tensor_scalar(
                                       sample, p.rearrange("p (b s) -> p b s", s=NS) if len(sample.shape) == 3 else p,
                                       scale, None, ALU.mult)))

                def tok(c0, N, dst, func=None):
                    for t, P in TILES:
                        def copy(p, t=t, P=P):
                            if func is None:
                                return nc.vector.tensor_copy(dst[:P, t, :], p)
                            return nc.scalar.activation(dst[:P, t, :], p, func)
                        out.append(Job(n, P, N, lambda k, t=t, P=P: xT[:, k, tok0(t):tok0(t) + P],
                                       lambda k: w[:, k, c0:c0 + N], "dve" if func is None else "act", copy))

                if n == 0:
                    for f in range(2):
                        feat(f * 128, 128, qT[:, f, 0:512], qT[:, f, 512:544], 64 ** -0.5)
                        feat(256 + f * 128, 128, kT[:, f, 0:512], kT[:, f, 512:544])
                elif n == 1:
                    tok(0, 512, v)
                elif n == 2:
                    tok(0, 512, rs, ACT.Silu)
                elif n == 3:
                    feat(0, 16, gT[:, 0:512], gT[:, 512:544])
                    tok(16, 512, zs, ACT.Silu)
                else:
                    for f in range(3):
                        ff = 3 * (n - 4) + f
                        feat(f * 128, 128, xbcP[:, ff, 3:515], xbcS[:, ff, :, 3:7])
                    if n == 5:
                        tok(384, 8, soft[:, :, 256:264])
                return out

            project_stage(nc, "abi", A["ab_w_in"], pieces, 528, xT, jobs_of)

        with Scope(nc, "abg") as s:
            convst = s.sb("convst", [NB * 3, 768])
            wg2 = s.sb("wg2", [16, 256])
            bg = s.sb("bg", [128, 264])
            cwr = s.sb("cwr", [5, 768])
            cw = s.sb("cw", [128, 6, 5])
            nc_conv = s.sb("newconv", [128, 6, 3 + NB * 3])
            tmp = s.sb("tmp", [128, 5, 264])
            pg = [s.ps(f"pg{i}") for i in range(5)]
            pc = s.ps("pc")
            pn = [s.ps(f"pn{i}") for i in range(2)]
            names = ("loaded", "zeroed", "gate_sum", "states_T", "dve_steps", "ext_ready", "conv_ready",
                     "logit_ready", "act_steps", "log_ready", "newst_T", "newst_ready", "stored", "silu_done")
            (loaded, zeroed, gate_sum, states_T, dv, ext_ready, conv_ready, logit_ready, ac, log_ready, newst_T,
             newst_ready, stored, silu_done) = (s.sem(x) for x in names)
            newst = s.sb("newst", [32, 2, 768])
            block = s.block()

            @block.sync
            def _(sp):
                sp.dma_start(convst[:, :], A["state_conv"].rearrange("b i n -> (b i) n")).then_inc(loaded, 16)
                sp.dma_start(wg2[:, :], A["ab_w_gate2"]).then_inc(loaded, 16)
                sp.dma_start(bg[:, 0:256], A["ab_b_gate"].partition_broadcast(128)).then_inc(loaded, 16)
                sp.dma_start(bg[:, 256:264], A["ab_dt_bias"].partition_broadcast(128)).then_inc(loaded, 16)
                sp.dma_start(cwr[0:4, :], A["ab_conv_w"]).then_inc(loaded, 16)
                sp.dma_start(cwr[4:5, :], A["ab_conv_b"].rearrange("(a n) -> a n", a=1)).then_inc(loaded, 16)
                sp.dma_start(heads[:, 0:8], A["ab_a_log"].partition_broadcast(128)).then_inc(loaded, 16)
                sp.dma_start(heads[:, 8:16], A["ab_d_skip"].partition_broadcast(128)).then_inc(loaded, 16)
                sp.dma_start(norms[:, 0:128], A["ab_gla_norm"].partition_broadcast(128)).then_inc(loaded, 16)
                sp.dma_start(norms[:, 128:640], A["ab_ssm_norm"].partition_broadcast(128)).then_inc(loaded, 16)
                sp.wait_ge(newst_ready, 2)
                sp.dma_start(A["conv_p"][0, :, :], newst[0:3, 0, :]).then_inc(stored, 16)
                sp.dma_start(A["conv_s"].rearrange("b i n -> (b i) n"), newst[0:24, 1, :]).then_inc(stored, 16)
                sp.wait_ge(stored, 32)

            @block.tensor
            def _(pe):
                pe.wait_ge(loaded, 16 * 10)
                for f in range(6):
                    nc.tensor.transpose(pc[:, f * 24:(f + 1) * 24], convst[:, f * 128:(f + 1) * 128],
                                        C("ident")[:24, :24])
                    last = nc.tensor.transpose(pc[:, 144 + f * 5:149 + f * 5], cwr[:, f * 128:(f + 1) * 128],
                                               C("ident")[:5, :5])
                last.then_inc(states_T, 1)
                for t, P in TILES:
                    nc.tensor.matmul(pg[t][:P, 0:256], gT[:, tok0(t):tok0(t) + P], wg2[:, :],
                                     start=True, stop=True).then_inc(gate_sum, 1)
                pe.wait_ge(ext_ready, 2)
                for h in range(2):
                    for f in range(3):
                        last = nc.tensor.transpose(pn[h][0:3, f * 128:(f + 1) * 128],
                                                   nc_conv[:, 3 * h + f, 0:3], C("ident"))
                last.then_inc(newst_T, 1)
                pe.wait_ge(newst_ready, 1)
                for h in range(2):
                    for f in range(3):
                        last = nc.tensor.transpose(pn[h][0:24, f * 128:(f + 1) * 128],
                                                   nc_conv[:, 3 * h + f, 3:27], C("ident"))
                last.then_inc(newst_T, 1)

            @block.vector
            def _(dve):
                c = Count(dve, dv)
                c.step(nc.vector.memset(tmp[:, 4, :], 0.0))
                c.add(nc.vector.tensor_copy(tmp[:, 0:4, 256:264], soft[:, 0:4, 256:264]))
                c.add(nc.vector.tensor_copy(tmp[0:32, 4, 256:264], soft[0:32, 4, 256:264]))
                c.step(nc.vector.memset(xbcP[:, :, 0:3], 0.0))
                dve.wait_ge(states_T, 1)
                c.add(nc.vector.tensor_copy(cw[:, :, :], pc[:, 144:174].rearrange("p (f i) -> p f i", f=6)))
                c.step(nc.vector.tensor_copy(xbcS[:, :, :, 0:3],
                                             pc[:, 0:144].rearrange("p (f b i) -> p f b i", f=6, b=NB)))
                nc.vector.tensor_copy(nc_conv[:, :, 0:3], xbcP[:, :, 512:515]).then_inc(ext_ready, 1)
                nc.vector.tensor_copy(nc_conv[:, :, 3:27].rearrange("p f (b i) -> p f b i", b=NB),
                                      xbcS[:, :, :, 4:7]).then_inc(ext_ready, 1)
                dve.wait_ge(gate_sum, 5)
                for t, P in TILES:
                    c.add(nc.vector.tensor_copy(tmp[:P, t, 0:256], pg[t][:P, 0:256]))
                c.wait()
                dve.wait_ge(loaded, 16 * 10)
                bias = bg[:, :].unsqueeze(1).to_broadcast([128, 5, 264])
                c.step(nc.vector.tensor_tensor(tmp[:, :, :], tmp[:, :, :], bias, ALU.add))
                nc.vector.tensor_scalar(tmp[:, :, 0:256], tmp[:, :, 0:256], -1.0, None, ALU.mult).then_inc(logit_ready, 1)
                for f in range(6):
                    outs = [(xbcC[:, f, 0:512], lambda i: xbcP[:, f, i:i + 512]),
                            (xbcC[:, f, 512:544].rearrange("p (b s) -> p b s", s=NS), lambda i: xbcS[:, f, :, i:i + NS])]
                    for o, src in outs:
                        c.add(nc.vector.tensor_scalar(o, src(0), cw[:, f, 0:1], cw[:, f, 4:5],
                                                      ALU.mult, ALU.add))
                for i in range(1, 4):
                    for f in range(6):
                        outs = [(xbcC[:, f, 0:512], xbcP[:, f, i:i + 512]),
                                (xbcC[:, f, 512:544].rearrange("p (b s) -> p b s", s=NS), xbcS[:, f, :, i:i + NS])]
                        for o, src in outs:
                            dve.wait_ge(dv, c.n - 11)
                            last = nc.vector.scalar_tensor_tensor(out=o, in0=src, scalar=cw[:, f, i:i + 1], in1=o,
                                                                  op0=ALU.mult, op1=ALU.add)
                            if (i, f) != (3, 5) or o is outs[0][0]:
                                c.add(last)
                last.then_inc(conv_ready, 1)
                dve.wait_ge(newst_T, 1)
                for h in range(2):
                    last = nc.vector.tensor_copy(newst[0:3, 0, h * 384:(h + 1) * 384], pn[h][0:3, 0:384])
                last.then_inc(newst_ready, 1)
                dve.wait_ge(log_ready, 1)
                c.step(nc.vector.scalar_tensor_tensor(out=soft[:, :, :], in0=tmp[:, :, :], scalar=0.0,
                                                      in1=soft[:, :, :], op0=ALU.max, op1=ALU.add))
                c.step(nc.vector.tensor_scalar(soft[:, :, 0:256], soft[:, :, 0:256], -1.0 / 16, None, ALU.mult))
                c.step(nc.vector.tensor_tensor(las[:, :, :], soft[:, :, 256:264],
                                               heads[:, 0:8].unsqueeze(1).to_broadcast([128, 5, 8]), ALU.mult))
                c.step(nc.vector.tensor_scalar(las[:, :, :], las[:, :, :], -1.0, None, ALU.mult))
                for cc in range(2):
                    c.add(nc.vector.tensor_scalar(lam[:, :, cc, :], las[:, 0:4, :], C("cmask")[:, cc:cc + 1], None,
                                                  ALU.mult))
                for b in range(NB):
                    c.add(nc.vector.tensor_scalar(lams[:, b, :], las[0:32, 4, :], C("bmask")[0:32, b:b + 1], None,
                                                  ALU.mult))
                dve.wait_ge(newst_T, 2)
                for h in range(2):
                    last = nc.vector.tensor_copy(newst[0:24, 1, h * 384:(h + 1) * 384], pn[h][0:24, 0:384])
                last.then_inc(newst_ready, 1)

            @block.scalar
            def _(act):
                c = Count(act, ac)
                act.wait_ge(loaded, 16 * 10)
                c.add(nc.scalar.activation(heads[:, 0:8], heads[:, 0:8], ACT.Exp))
                act.wait_ge(logit_ready, 1)
                c.step(nc.scalar.activation(soft[:, :, :], tmp[:, :, :], ACT.Abs))
                c.step(nc.scalar.activation(soft[:, :, :], soft[:, :, :], ACT.Exp, scale=-1.0))
                nc.scalar.activation(soft[:, :, :], soft[:, :, :], ACT.Ln, bias=1.0).then_inc(log_ready, 1)
                act.wait_ge(conv_ready, 1)
                nc.scalar.activation(xbcC[:, :, :], xbcC[:, :, :], ACT.Silu).then_inc(silu_done, 1)

        with Scope(nc, "abz") as L2:
            scan_ab(nc, A, C, L2, yo, v, rs, zs, qT, kT, soft, xbcC, las, lam, lams, heads, norms)
        mix_out(nc, "abm", C, X, yo, A["ab_w_out"])


def scan_ab(nc, A, C, L, yo, v, rs, zs, qT, kT, soft, xbcC, las, lam, lams, heads, norms):
    eb = L.sb("eb", [128, 2, NTOK])
    kend = L.sb("kend", [128, 5, 256])
    xs = L.sb("xs", [128, 5, 512])
    btok = L.sb("btok", [128, 5, 128])
    xdd = L.sb("xdd", [128, 5, 512])
    ecum = L.sb("ecum", [128, 5, 16])
    elh = L.sb("elh", [128, 16, 4])
    ycs = L.sb("ycs", [128, 5, 512])
    BT, CT = xbcC[:, 4, :], xbcC[:, 5, :]

    with Scope(nc, "abs") as s:
        enb = s.sb("enb", [128, 2, 128])
        qd, kd = qT, kT
        ncum = s.sb("ncum", [128, 8])
        esuf = s.sb("esuf", [128, 256])
        el = s.sb("el", [128, 64])
        xdt = s.sb("xdt", [128, 512])
        W = s.sb("W", [128, 8, 128])
        At = s.sb("At", [128, 4, 128])
        pa, pb, px, pB, pr0, pr1, po, py = (s.ps(x) for x in ("pa", "pb", "px", "pB", "pr0", "pr1", "po", "py"))
        (summed, dv, ac, exps, cneg, wexp, ready, att, masked, outs, copied, zero) = (s.sem(x) for x in (
            "summed", "dve_steps", "act_steps", "exps", "cneg", "wexp", "ready", "att", "masked", "outs",
            "copied", "zeroed"))
        block = s.block()

        @block.tensor
        def _(pe):
            for t, P in TILES:
                m = "p" if t < 4 else "s"
                tri, suf, neg = C("tri_" + m)[:P, :P], C("suf_" + m)[:P, :P], C("neg_" + m)[:P, :P]
                tk = slice(tok0(t), tok0(t) + P)
                if t:
                    pe.wait_ge(ready, t)
                    pe.wait_ge(copied, t)
                for f in range(2):
                    nc.tensor.matmul(pa[:, f * 128:f * 128 + P], soft[:P, t, f * 128:(f + 1) * 128], tri,
                                     start=True, stop=True)
                nc.tensor.matmul(pa[:P, 256:512], suf, soft[:P, t, 0:256], start=True, stop=True)
                nc.tensor.matmul(pb[:P, 0:8], tri, las[:P, t, :], start=True, stop=True)
                nc.tensor.matmul(pb[:P, 8:16], suf, las[:P, t, :], start=True, stop=True)
                n = 16 if t < 4 else 64
                rhs = (lam[:, t, :, :] if t < 4 else lams[:, :, :]).rearrange("p c h -> p (c h)")
                nc.tensor.matmul(pb[:, 16:16 + n], C("ones")[:P, :], rhs, start=True, stop=True)
                for f in range(2):
                    nc.tensor.transpose(pb[:P, 256 + f * 128:256 + (f + 1) * 128], kT[:, f, tk], C("ident"))
                for f in range(4):
                    nc.tensor.transpose(px[:P, f * 128:(f + 1) * 128], xbcC[:, f, tk], C("ident"))
                nc.tensor.transpose(pB[:P, 256:384], BT[:, tk], C("ident"))
                for g in range(2):
                    nc.tensor.matmul((pB, po)[g][:P, 0:P], BT[64 * g:64 * g + 64, tk],
                                     CT[64 * g:64 * g + 64, tk], start=True, stop=True)
                for h in range(8):
                    pr = (pr0, pr1)[h // 4][:P, (h % 4) * 128:(h % 4) * 128 + P]
                    nc.tensor.matmul(pr, las[:P, t, h:h + 1].to_broadcast([P, P]), tri, start=True, stop=False)
                    last = nc.tensor.matmul(pr, C("ident")[:P, :P], neg, start=False, stop=True)
                last.then_inc(summed, 1)
                pe.wait_ge(ready, t + 1)
                for h in range(4):
                    r = slice(64 * (h % 2), 64 * (h % 2) + 64)
                    last = nc.tensor.matmul((pr0, pr1)[h % 2][:P, (h // 2) * 128:(h // 2) * 128 + P],
                                            kd[r, h // 2, tk], qd[r, h // 2, tk],
                                            start=True, stop=True)
                last.then_inc(att, 1)
                pe.wait_ge(masked, t + 1)
                for h in range(4):
                    last = nc.tensor.matmul(po[:P, h * 128:(h + 1) * 128], At[:P, h, :P], v[:P, t, h * 128:(h + 1) * 128],
                                            start=True, stop=True)
                for h in range(8):
                    last = nc.tensor.matmul(py[:P, h * 64:(h + 1) * 64], W[:P, h, :P], xdt[:P, h * 64:(h + 1) * 64],
                                            start=True, stop=True)
                last.then_inc(outs, 1)

        @block.scalar
        def _(act):
            for t, P in TILES:
                tk = slice(tok0(t), tok0(t) + P)
                if t:
                    act.wait_ge(masked, t)
                    act.wait_ge(outs, t)
                act.wait_ge(summed, t + 1)
                b = pa[:, 0:256].rearrange("p (f n) -> p f n", f=2)[:, :, :P]
                nc.scalar.activation(eb[:, :, tk], b, ACT.Exp)
                nc.scalar.activation(enb[:, :, :P], b, ACT.Exp, scale=-1.0)
                nc.scalar.activation(esuf[:P, :], pa[:P, 256:512], ACT.Exp)
                nc.scalar.activation(ecum[:P, t, :], pb[:P, 0:16], ACT.Exp)
                n = 16 if t < 4 else 64
                nc.scalar.activation(el[:, 0:n], pb[:, 16:16 + n], ACT.Exp).then_inc(exps, 1)
                act.wait_ge(cneg, t + 1)
                for h in range(8):
                    last = nc.scalar.activation(W[:P, h, :P], (pr0, pr1)[h // 4][:P, (h % 4) * 128:(h % 4) * 128 + P],
                                                ACT.Exp, bias=ncum[:P, h:h + 1])
                last.then_inc(wexp, 1)

        @block.vector
        def _(dve):
            c = Count(dve, dv)
            c.add(nc.vector.memset(yo[:, 4, :], 0.0))
            c.step(nc.vector.memset(ycs[:, 4, :], 0.0))
            c.add(nc.vector.memset(xs[:, 4, :], 0.0))
            c.step(nc.vector.memset(ecum[:, 4, :], 0.0))
            for t, P in TILES:
                tk = slice(tok0(t), tok0(t) + P)
                dve.wait_ge(summed, t + 1)
                c.add(nc.vector.tensor_copy(xs[:P, t, :], px[:P, :]))
                c.add(nc.vector.tensor_copy(btok[:P, t, :], pB[:P, 256:384]))
                c.wait()
                dt = soft[:P, t, 256:264].unsqueeze(2).to_broadcast([P, 8, 64])
                c.step(nc.vector.tensor_tensor(xdt[:P, :].rearrange("p (h d) -> p h d", h=8),
                                               xs[:P, t, :].rearrange("p (h d) -> p h d", h=8), dt, ALU.mult))
                dve.wait_ge(exps, t + 1)
                nc.vector.tensor_scalar(ncum[:P, :], pb[:P, 0:8], -1.0, None, ALU.mult).then_inc(cneg, 1)
                c.add(nc.vector.tensor_tensor(qd[:, :, tk], qT[:, :, tk], eb[:, :, tk], ALU.mult))
                c.add(nc.vector.tensor_tensor(kd[:, :, tk], kT[:, :, tk], enb[:, :, :P], ALU.mult))
                c.add(nc.vector.tensor_tensor(kend[:P, t, :], pb[:P, 256:512], esuf[:P, :], ALU.mult))
                c.add(nc.vector.tensor_tensor(xdd[:P, t, :].rearrange("p (h d) -> p h d", h=8),
                                              xdt[:P, :].rearrange("p (h d) -> p h d", h=8),
                                              ecum[:P, t, 8:16].unsqueeze(2).to_broadcast([P, 8, 64]), ALU.mult))
                for g in range(2):
                    n, at = (2, 2 * t) if t < 4 else (8, 8)
                    c.add(nc.vector.tensor_copy(elh[64 * g:64 * g + 64, at:at + n, :],
                                                el[64 * g:64 * g + 64, 0:8 * n]
                                                .rearrange("p (c h) -> p c h", h=8)[:, :, 4 * g:4 * g + 4]))
                dve.wait_ge(wexp, t + 1)
                for g in range(2):
                    last = nc.vector.tensor_tensor(W[:P, 4 * g:4 * g + 4, :P], W[:P, 4 * g:4 * g + 4, :P],
                                                   (pB, po)[g][:P, 0:P].unsqueeze(1).to_broadcast([P, 4, P]),
                                                   ALU.mult)
                last.then_inc(ready, 1)
                dve.wait_ge(att, t + 1)
                m = C("tri_p" if t < 4 else "tri_s")[:P, :P].unsqueeze(1).to_broadcast([P, 2, P])
                for hh in range(2):
                    last = nc.vector.tensor_tensor(At[:P, :, :P].rearrange("p (f h) n -> p h f n", h=2)[:, hh, :, :],
                                                   (pr0, pr1)[hh][:P, 0:256].rearrange("p (h n) -> p h n", h=2)[:, :, :P],
                                                   m, ALU.mult)
                last.then_inc(masked, 1)
                dve.wait_ge(outs, t + 1)
                c.add(nc.vector.tensor_copy(yo[:P, t, 0:512], po[:P, :]))
                nc.vector.tensor_copy(yo[:P, t, 512:1024], py[:P, :]).then_inc(copied, 1)

    qd = qT
    with Scope(nc, "abc") as s:
        Sg = s.sb("Sg", [128, 9, 256])
        Ss = s.sb("Ss", [128, 9, 256])
        stT = s.sb("stT", [128, 2, 128])
        pu = [s.ps(f"pu{i}") for i in range(4)]
        po = [s.ps(f"po{i}") for i in range(4)]
        upd, dv, states, inter, added, T_ready, T_done, stored = (s.sem(x) for x in (
            "upd", "dve_steps", "states", "inter", "added", "T_ready", "T_done", "stored"))
        block = s.block()

        @block.tensor
        def _(pe):
            for ch in range(8):
                t, r = ch // 2, slice(64 * (ch % 2), 64 * (ch % 2) + 64)
                if ch >= 4:
                    pe.wait_ge(states, ch - 3)
                for h in range(4):
                    nc.tensor.matmul(pu[ch % 4][64 * (h % 2):64 * (h % 2) + 64, (h // 2) * 128:(h // 2) * 128 + 128],
                                     kend[r, t, h * 64:(h + 1) * 64], v[r, t, h * 128:(h + 1) * 128],
                                     start=True, stop=True)
                for g in range(2):
                    last = nc.tensor.matmul(pu[ch % 4][64 * g:64 * g + 64, 256:512], btok[r, t, g * 64:(g + 1) * 64],
                                            xdd[r, t, g * 256:(g + 1) * 256], start=True, stop=True)
                last.then_inc(upd, 1)
            for t in range(4):
                pe.wait_ge(states, 2 * t + 1)
                if t >= 1:
                    pe.wait_ge(added, 2 * t)
                for ch in (2 * t, 2 * t + 1):
                    o = slice(64 * (ch % 2), 64 * (ch % 2) + 64)
                    tk = slice(64 * ch, 64 * ch + 64)
                    for h in range(4):
                        r = slice(64 * (h % 2), 64 * (h % 2) + 64)
                        nc.tensor.matmul(po[h % 2][o, (h // 2) * 128:(h // 2 + 1) * 128], qd[r, h // 2, tk],
                                         Sg[r, ch, (h // 2) * 128:(h // 2) * 128 + 128], start=True, stop=True)
                    for g in range(2):
                        r = slice(64 * g, 64 * g + 64)
                        last = nc.tensor.matmul(po[2 + g][o, 0:256], CT[r, tk], Ss[r, ch, :],
                                                start=True, stop=True)
                last.then_inc(inter, 1)
            pe.wait_ge(states, 8)
            for u in range(2):
                last = nc.tensor.transpose(pu[0][:, u * 128:(u + 1) * 128], Ss[:, 8, u * 128:(u + 1) * 128], C("ident"))
            last.then_inc(T_ready, 1)

        @block.vector
        def _(dve):
            c = Count(dve, dv)
            c.add(nc.vector.memset(Sg[:, 0, :], 0.0))
            c.step(nc.vector.memset(Ss[:, 0, :], 0.0))
            for ch in range(8):
                dve.wait_ge(upd, ch + 1)
                c.step(nc.vector.tensor_tensor(Ss[:, ch + 1, :].rearrange("p (h d) -> p h d", h=4),
                                               Ss[:, ch, :].rearrange("p (h d) -> p h d", h=4),
                                               elh[:, ch, :].unsqueeze(2).to_broadcast([128, 4, 64]), ALU.mult))
                c.add(nc.vector.tensor_tensor(Ss[:, ch + 1, :], Ss[:, ch + 1, :], pu[ch % 4][:, 256:512], ALU.add))
                for f in range(2):
                    col = slice(f * 128, f * 128 + 128)
                    last = nc.vector.scalar_tensor_tensor(out=Sg[:, ch + 1, col], in0=Sg[:, ch, col],
                                                          scalar=eb[:, f, 64 * ch + 63:64 * ch + 64],
                                                          in1=pu[ch % 4][:, col], op0=ALU.mult, op1=ALU.add)
                last.then_inc(states, 1)
                dve.wait_ge(states, ch + 1)
            for t in range(4):
                dve.wait_ge(inter, t + 1)
                for hh in range(2):
                    o3 = yo[:, t, 0:512].rearrange("p (f h d) -> p h f d", f=2, h=2)[:, hh, :, :]
                    last = nc.vector.tensor_tensor(o3, o3, po[hh][:, 0:256].rearrange("p (f d) -> p f d", f=2), ALU.add)
                last.then_inc(added, 1)
                for g in range(2):
                    last = nc.vector.tensor_copy(ycs[:, t, 256 * g:256 * g + 256], po[2 + g][:, 0:256])
                last.then_inc(added, 1)
            dve.wait_ge(T_ready, 1)
            nc.vector.tensor_copy(stT[:, :, :], pu[0][:, 0:256].rearrange("p (u n) -> p u n", u=2)).then_inc(T_done, 1)

        @block.sync
        def _(sp):
            sp.wait_ge(states, 8)
            for f in range(2):
                sp.dma_start(A["gla_p"][0, 2 * f:2 * f + 2, :, :].rearrange("h k v -> (h k) v"),
                             Sg[:, 8, f * 128:(f + 1) * 128]).then_inc(stored, 16)
            sp.wait_ge(T_done, 1)
            for g in range(2):
                for u in range(2):
                    h = 4 * g + 2 * u
                    sp.dma_start(A["ssm_p"][0, h:h + 2, :, :].rearrange("h p n -> (h p) n"),
                                 stT[:, u, 64 * g:64 * g + 64]).then_inc(stored, 16)
            sp.wait_ge(stored, 16 * 6)

    with Scope(nc, "abd") as s:
        G0 = s.sb("G0", [128, 2, NB, 128])
        S0 = s.sb("S0", [128, NB, 256])
        raw = s.sb("raw", [128, NB, 2, 128])
        vm = s.sb("vm", [32, NB, 512])
        oTs = s.sb("oTs", [128, 4, 32])
        yTs = s.sb("yTs", [128, 4, 32])
        ps = [s.ps(f"p{i}") for i in range(8)]
        (ld_g, ld_s, tr, tr_out, vmask, inter, evac, back, added, upd, dv, new_g, new_s, xmask, trb, fin, stored,
         mm) = (s.sem(x) for x in (
             "ld_g", "ld_s", "tr", "tr_out", "vmask", "inter", "evac", "back", "added", "upd", "dve_steps", "new_g",
             "new_s", "xmask", "trb", "fin", "stored", "updated_s"))
        block = s.block()

        @block.sync
        def _(sp):
            for f in range(2):
                sp.dma_start(G0[:, f, :, :], A["state_gla"][:, 2 * f:2 * f + 2, :, :].rearrange("b h k v -> (h k) b v"))\
                  .then_inc(ld_g, 16)
            for g in range(2):
                for u in range(2):
                    h = 4 * g + 2 * u
                    sp.dma_start(raw[:, :, u, 64 * g:64 * g + 64],
                                 A["state_ssm"][:, h:h + 2, :, :].rearrange("b h p n -> (h p) b n")).then_inc(ld_s, 16)
            sp.wait_ge(new_g, 1)
            for f in range(2):
                sp.dma_start(A["gla_s"][:, 2 * f:2 * f + 2, :, :].rearrange("b h k v -> (h k) b v"), G0[:, f, :, :])\
                  .then_inc(stored, 16)
            sp.wait_ge(fin, 4)
            for g in range(2):
                for u in range(2):
                    h = 4 * g + 2 * u
                    sp.dma_start(A["ssm_s"][:, h:h + 2, :, :].rearrange("b h p n -> (h p) b n"),
                                 raw[:, :, u, 64 * g:64 * g + 64]).then_inc(stored, 16)
            sp.wait_ge(stored, 16 * 6)

        @block.tensor
        def _(pe):
            pe.wait_ge(ld_s, 64)
            for i in range(4):
                for b in (2 * i, 2 * i + 1):
                    for u in range(2):
                        last = nc.tensor.transpose(ps[i][:, (b % 2) * 256 + u * 128:(b % 2) * 256 + (u + 1) * 128],
                                                   raw[:, b, u, :], C("ident"))
                last.then_inc(tr, 1)
            pe.wait_ge(ld_g, 32)
            for h in range(4):
                r = slice(64 * (h % 2), 64 * (h % 2) + 64)
                for b in range(NB):
                    nc.tensor.matmul(ps[4 + h % 2][:, (h // 2) * 32 + 4 * b:(h // 2) * 32 + 4 * b + 4], G0[r, h // 2, b, :],
                                     qd[r, h // 2, 512 + 4 * b:516 + 4 * b], start=True, stop=True)
            pe.wait_ge(tr_out, 4)
            for j in range(4):
                r = slice(64 * (j // 2), 64 * (j // 2) + 64)
                for b in range(NB):
                    last = nc.tensor.matmul(ps[6 + j // 2][:, (j % 2) * 32 + 4 * b:(j % 2) * 32 + 4 * b + 4],
                                            S0[r, b, (j % 2) * 128:(j % 2) * 128 + 128],
                                            CT[r, 512 + 4 * b:516 + 4 * b], start=True, stop=True)
            last.then_inc(inter, 1)
            pe.wait_ge(evac, 1)
            for h in range(4):
                nc.tensor.matmul(ps[6][:32, h * 128:(h + 1) * 128], oTs[:, h, :], C("ident"), start=True, stop=True)
            for h in range(4):
                last = nc.tensor.matmul(ps[7][:32, h * 128:(h + 1) * 128], yTs[:, h, :], C("ident"),
                                        start=True, stop=True)
            last.then_inc(back, 1)
            pe.wait_ge(vmask, 1)
            for h in range(4):
                for q in range(2):
                    last = nc.tensor.matmul(ps[2 * (h // 2) + q][64 * (h % 2):64 * (h % 2) + 64, :],
                                            kend[:32, 4, h * 64:(h + 1) * 64],
                                            vm[:, 4 * q:4 * q + 4, h * 128:(h + 1) * 128], start=True, stop=True)
            last.then_inc(upd, 1)
            pe.wait_ge(xmask, 1)
            for g in range(2):
                for q in range(4):
                    last = nc.tensor.matmul(ps[4 + q][64 * g:64 * g + 64, :], btok[:32, 4, g * 64:(g + 1) * 64],
                                            vm[:, 2 * q:2 * q + 2, g * 256:(g + 1) * 256], start=True, stop=True)
            last.then_inc(mm, 1)
            pe.wait_ge(new_s, 1)
            for i in range(4):
                for b in (2 * i, 2 * i + 1):
                    for u in range(2):
                        last = nc.tensor.transpose(ps[i][:, (b % 2) * 256 + u * 128:(b % 2) * 256 + (u + 1) * 128],
                                                   S0[:, b, u * 128:(u + 1) * 128], C("ident"))
                last.then_inc(trb, 1)

        @block.vector
        def _(dve):
            c = Count(dve, dv)
            for b in range(NB):
                last = nc.vector.tensor_scalar(vm[:, b, :], v[:32, 4, :], C("bmask")[:32, b:b + 1], None, ALU.mult)
            last.then_inc(vmask, 1)
            for i in range(4):
                dve.wait_ge(tr, i + 1)
                nc.vector.tensor_copy(S0[:, 2 * i:2 * i + 2, :], ps[i][:, :].rearrange("p (b n) -> p b n", b=2))\
                  .then_inc(tr_out, 1)
            dve.wait_ge(inter, 1)
            for q in range(2):
                nc.vector.tensor_copy(oTs[:, :, :].rearrange("p (f h) n -> p h f n", h=2)[:, q, :, :],
                                      ps[4 + q][:, 0:64].rearrange("p (h n) -> p h n", h=2))
                last = nc.vector.tensor_copy(yTs[:, 2 * q:2 * q + 2, :], ps[6 + q][:, 0:64].rearrange("p (h n) -> p h n", h=2))
            last.then_inc(evac, 1)
            dve.wait_ge(back, 1)
            c.add(nc.vector.tensor_tensor(yo[:32, 4, 0:512], yo[:32, 4, 0:512], ps[6][:32, :], ALU.add))
            c.step(nc.vector.tensor_copy(ycs[:32, 4, :], ps[7][:32, :]))
            for f in range(2):
                ebl = eb[:, f, 512:544].rearrange("p (b s) -> p b s", s=NS)[:, :, NS - 1:NS].to_broadcast([128, NB, 128])
                c.add(nc.vector.tensor_tensor(G0[:, f, :, :], G0[:, f, :, :], ebl, ALU.mult))
            c.add(nc.vector.tensor_tensor(S0[:, :, :].rearrange("p b (h d) -> p (b h) d", h=4),
                                          S0[:, :, :].rearrange("p b (h d) -> p (b h) d", h=4),
                                          elh[:, 8:16, :].rearrange("p b h -> p (b h)").unsqueeze(2)
                                          .to_broadcast([128, 32, 64]), ALU.mult))
            c.wait()
            dve.wait_ge(upd, 1)
            for b in range(NB):
                last = nc.vector.tensor_scalar(vm[:, b, :], xdd[:32, 4, :], C("bmask")[:32, b:b + 1], None, ALU.mult)
            last.then_inc(xmask, 1)
            for f in range(2):
                for q in range(2):
                    rows = G0[:, f, 4 * q:4 * q + 4, :].rearrange("p b n -> p (b n)")
                    last = nc.vector.tensor_tensor(rows, rows, ps[2 * f + q][:, :], ALU.add)
            last.then_inc(new_g, 1)
            dve.wait_ge(mm, 1)
            for q in range(4):
                rows = S0[:, 2 * q:2 * q + 2, :].rearrange("p b n -> p (b n)")
                last = nc.vector.tensor_tensor(rows, rows, ps[4 + q][:, :], ALU.add)
            last.then_inc(new_s, 1)
            for i in range(4):
                dve.wait_ge(trb, i + 1)
                nc.vector.tensor_copy(raw[:, 2 * i:2 * i + 2, :, :].rearrange("p b u n -> p (b u n)"), ps[i][:, :])\
                  .then_inc(fin, 1)

    with Scope(nc, "abe") as s:
        sq = s.sb("sq", [128, 5, 512])
        ms = s.sb("ms", [128, 5, 5])
        dv, var_ready, root, vm2 = (s.sem(x) for x in ("dve_steps", "var_ready", "root", "y_ready"))
        block = s.block()

        @block.vector
        def _(dve):
            c = Count(dve, dv)
            V = nc.vector
            c.step(V.memset(ms[:, :, :], 1.0))
            for t, P in TILES:
                o, y = yo[:P, t, 0:512], yo[:P, t, 512:1024]
                y3 = y.rearrange("p (h d) -> p h d", h=8)
                yc = ycs[:P, t, :].rearrange("p (h d) -> p h d", h=8)
                xs3 = xs[:P, t, :].rearrange("p (h d) -> p h d", h=8)
                c.add(V.tensor_tensor(yc, yc, ecum[:P, t, 0:8].unsqueeze(2).to_broadcast([P, 8, 64]), ALU.mult))
                c.step(V.tensor_tensor(xs3, xs3, heads[:P, 8:16].unsqueeze(2).to_broadcast([P, 8, 64]), ALU.mult))
                c.step(V.tensor_tensor(y, y, ycs[:P, t, :], ALU.add))
                c.step(V.tensor_tensor(y, y, xs[:P, t, :], ALU.add))
                c.step(V.tensor_tensor(y, y, zs[:P, t, :], ALU.mult))
                c.step(V.tensor_tensor(sq[:P, t, :], y, y, ALU.mult))
                c.step(V.tensor_reduce(ms[:P, t, 4:5], sq[:P, t, :], AX.X, ALU.add))
                c.step(V.tensor_tensor(sq[:P, t, :], o, o, ALU.mult))
                c.step(V.tensor_reduce(ms[:P, t, 0:4], sq[:P, t, :].rearrange("p (h d) -> p h d", h=4), AX.X, ALU.add))
            c.add(V.tensor_scalar(ms[:, :, 0:4], ms[:, :, 0:4], 1.0 / 128, RMS_EPS, ALU.mult, ALU.add))
            V.tensor_scalar(ms[:, :, 4:5], ms[:, :, 4:5], 1.0 / 512, RMS_EPS, ALU.mult, ALU.add).then_inc(var_ready, 1)
            dve.wait_ge(root, 1)
            c.step(V.reciprocal(ms[:, :, :], ms[:, :, :]))
            for t, P in TILES:
                o, y = yo[:P, t, 0:512], yo[:P, t, 512:1024]
                o3 = o.rearrange("p (h d) -> p h d", h=4)
                c.add(V.scalar_tensor_tensor(out=y, in0=y, scalar=ms[:P, t, 4:5], in1=norms[:P, 128:640],
                                             op0=ALU.mult, op1=ALU.mult))
                c.step(V.tensor_tensor(o3, o3, ms[:P, t, 0:4].unsqueeze(2).to_broadcast([P, 4, 128]), ALU.mult))
                c.step(V.tensor_tensor(o3, o3, norms[:P, 0:128].unsqueeze(1).to_broadcast([P, 4, 128]), ALU.mult))
                c.step(V.tensor_tensor(o, o, rs[:P, t, :], ALU.mult))

        @block.scalar
        def _(act):
            act.wait_ge(var_ready, 1)
            nc.scalar.activation(ms[:, :, :], ms[:, :, :], ACT.Sqrt).then_inc(root, 1)


def mix_out(nc, name, C, X, yo, w):
    with Scope(nc, name) as s:
        mT = s.sb("mT", [128, KD, NTOK])
        transpose_stage(nc, name + "t", C, yo, mT)
        project_stage(nc, name + "o", w, [(0, 512), (512, 1024)], 512, mT, out_jobs(nc, X, mT), nbuf=2)


def rank(V, c, dst, val, gt, eq, lt):
    lead, n = list(val.shape[:-1]), val.shape[-1]
    full = lead + [n, n]
    ax = len(lead)
    m_val, n_val = val.unsqueeze(ax).to_broadcast(full), val.unsqueeze(ax + 1).to_broadcast(full)
    c.add(V.tensor_tensor(gt, m_val, n_val, ALU.is_gt))
    c.step(V.tensor_tensor(eq, m_val, n_val, ALU.is_equal))
    c.step(V.tensor_tensor(eq, eq, lt, ALU.mult))
    c.step(V.tensor_tensor(gt, gt, eq, ALU.add))
    c.step(V.tensor_reduce(dst, gt, AX.X, ALU.add))


def moe(nc, A, X, C, l, xd, yd):
    name = f"m{l}"
    with Scope(nc, name) as M:
        posi = M.sb("posi", [128, 2, 5], I32)
        gate = M.sb("gate", [128, 2, 5])
        tokof = M.sb("tokof", [128, NPAIR], I32)
        widx = M.sb("widx", [128, NTILE], I32)

        with Scope(nc, name + "a") as s:
            xT = s.sb("xT", [128, KD, NTOK])
            wr = s.sb("wr", [128, KD, 36])
            br = s.sb("br", [128, 36])
            transpose_stage(nc, name + "t", C, X, xT)
            lg = s.sb("lg", [128, 5, 36])
            gt4, eq4 = s.sb("gt4", [128, 5, 4, 4]), s.sb("eq4", [128, 5, 4, 4])
            gt8, eq8 = s.sb("gt8", [128, 5, 8, 8]), s.sb("eq8", [128, 5, 8, 8])
            r4, r8 = s.sb("r4", [128, 5, 4]), s.sb("r8", [128, 5, 8])
            mx, dif, ssum, pgrp = s.sb("mx", [128, 5]), s.sb("dif", [128, 5, 5]), s.sb("ssum", [128, 5]), s.sb("pg", [128, 5])
            sel, sel4 = s.sb("sel", [128, 5, 8]), s.sb("sel4", [128, 5, 8, 4])
            oh = s.sb("oh", [128, 2, 5, 8])
            pick = s.sb("pick", [128, 5, 8])
            v2 = s.sb("v2", [128, 5])
            As = s.sb("As", [128, 2, 5, 32])
            A12 = s.sb("A12", [128, 5, 32])
            rk = s.sb("rk", [128, 6, 32])
            cmp9 = s.sb("cmp9", [128, 32, 9])
            tiles, sc = s.sb("tiles", [128, 32]), s.sb("sc", [128, 2, 32])
            pos = s.sb("pos", [128, 10])
            big = s.sb("big", [128, NTILE, 32])
            ex = s.sb("ex", [128, 2, NTILE])
            ge = s.sb("ge", [128, 10, NPAIR + 1])
            ci = s.sb("ci", [128, 10, NPAIR])
            rr = s.sb("rr", [128, 2, 10])
            ohr = s.sb("ohr", [128, 10, 128])
            pl = [s.ps(f"l{i}") for i in range(5)]
            pr, pt = s.ps("r"), s.ps("t")
            (loaded, logits, dv, ex_in, ex_out, asg, ranks, onehots, toks, xstored) = (s.sem(x) for x in (
                "loaded", "logits", "dve_steps", "exp_in", "exp_out", "assigned", "ranks", "onehots", "toks", "xstored"))
            block = s.block()

            @block.sync
            def _(sp):
                sp.dma_start(wr[:, :, 0:4], A["moe_w_coarse"][l].rearrange("(k p) g -> p k g", p=128)).then_inc(loaded, 16)
                for g in range(4):
                    sp.dma_start(wr[:, :, 4 + 8 * g:12 + 8 * g],
                                 A["moe_w_fine"][l, g].rearrange("(k p) e -> p k e", p=128)).then_inc(loaded, 16)
                sp.dma_start(br[:, 0:4], A["moe_b_coarse"][l].partition_broadcast(128)).then_inc(loaded, 16)
                sp.dma_start(br[:, 4:36], A["moe_b_fine"][l].rearrange("g e -> (g e)").partition_broadcast(128))\
                  .then_inc(loaded, 16)
                sp.dma_start(xd[0:512, :].rearrange("(t p) d -> p t d", p=128), X[:, 0:4, :]).then_inc(xstored, 16)
                sp.dma_start(xd[512:544, :], X[0:32, 4, :]).then_inc(xstored, 16)
                sp.wait_ge(xstored, 32)

            @block.tensor
            def _(pe):
                pe.wait_ge(loaded, 16 * 7)
                for t, P in TILES:
                    for k in range(KD):
                        last = nc.tensor.matmul(pl[t][:P, 0:36], xT[:, k, tok0(t):tok0(t) + P], wr[:, k, :],
                                                start=(k == 0), stop=(k == KD - 1))
                    last.then_inc(logits, 1)
                pe.wait_ge(asg, 1)
                for t in range(6):
                    for q in range(min(t, 4) + 1):
                        lhsT = C("before") if q == t else C("ones")
                        last = nc.tensor.matmul(pr[:, 32 * t:32 * t + 32], lhsT, A12[:, q, :],
                                                start=(q == 0), stop=(q == min(t, 4)))
                last.then_inc(ranks, 1)
                pe.wait_ge(onehots, 1)
                for n in range(10):
                    last = nc.tensor.matmul(pt[:, 0:NPAIR], ohr[:, n, :], ci[:, n, :], start=(n == 0), stop=(n == 9))
                last.then_inc(toks, 1)

            @block.scalar
            def _(act):
                act.wait_ge(ex_in, 1)
                nc.scalar.activation(dif[:, :, :], dif[:, :, :], ACT.Exp).then_inc(ex_out, 1)

            @block.vector
            def _(dve):
                c, V = Count(dve, dv), nc.vector
                lt8 = C("lt8").rearrange("p (n m) -> p n m", n=8)
                c.step(V.memset(lg[:, :, :], 0.0))
                dve.wait_ge(loaded, 16 * 7)
                for t, P in TILES:
                    dve.wait_ge(logits, t + 1)
                    c.add(V.tensor_tensor(lg[:P, t, :], pl[t][:P, 0:36], br[:P, :], ALU.add))
                c.wait()
                lc = lg[:, :, 0:4]
                rank(V, c, r4[:, :, :], lc, gt4[:, :, :, :], eq4[:, :, :, :],
                     lt8[:, 0:4, 0:4].unsqueeze(1).to_broadcast([128, 5, 4, 4]))
                c.add(V.tensor_scalar(r4[:, :, :], r4[:, :, :], 0.0, None, ALU.is_equal))
                c.step(V.tensor_reduce(mx[:, :], lc, AX.X, ALU.max))
                c.add(V.tensor_tensor(dif[:, :, 0:4], lc, mx[:, :].unsqueeze(2).to_broadcast([128, 5, 4]), ALU.subtract))
                c.step(V.tensor_tensor(sel4[:, :, :, :],
                                       lg[:, :, 4:36].rearrange("p t (g e) -> p t e g", g=4),
                                       r4[:, :, :].unsqueeze(2).to_broadcast([128, 5, 8, 4]), ALU.mult))
                c.step(V.tensor_reduce(sel[:, :, :], sel4[:, :, :, :], AX.X, ALU.add))
                rank(V, c, r8[:, :, :], sel[:, :, :], gt8[:, :, :, :], eq8[:, :, :, :],
                     lt8.unsqueeze(1).to_broadcast([128, 5, 8, 8]))
                for k in range(2):
                    c.add(V.tensor_scalar(oh[:, k, :, :], r8[:, :, :], float(k), None, ALU.is_equal))
                c.step(V.tensor_reduce(mx[:, :], sel[:, :, :], AX.X, ALU.max))
                c.step(V.tensor_tensor(pick[:, :, :], sel[:, :, :], oh[:, 1, :, :], ALU.mult))
                c.step(V.tensor_reduce(v2[:, :], pick[:, :, :], AX.X, ALU.add))
                V.tensor_tensor(dif[:, :, 4], v2[:, :], mx[:, :], ALU.subtract).then_inc(ex_in, 1)
                for k in range(2):
                    c.add(V.tensor_tensor(As[:, k, :, :].rearrange("p t (g e) -> p t g e", g=4),
                                          r4[:, :, :].unsqueeze(3).to_broadcast([128, 5, 4, 8]),
                                          oh[:, k, :, :].unsqueeze(2).to_broadcast([128, 5, 4, 8]), ALU.mult))
                c.wait()
                for k in range(2):
                    c.add(V.tensor_tensor(As[:, k, :, :], As[:, k, :, :],
                                          C("valid").unsqueeze(2).to_broadcast([128, 5, 32]), ALU.mult))
                c.wait()
                V.tensor_tensor(A12[:, :, :], As[:, 0, :, :], As[:, 1, :, :], ALU.add).then_inc(asg, 1)
                dve.wait_ge(ex_out, 1)
                c.add(V.tensor_reduce(ssum[:, :], dif[:, :, 0:4], AX.X, ALU.add))
                c.step(V.tensor_scalar(pgrp[:, :], dif[:, :, 4], 1.0, None, ALU.add))
                c.step(V.tensor_tensor(ssum[:, :], ssum[:, :], pgrp[:, :], ALU.mult))
                c.step(V.reciprocal(gate[:, 0, :], ssum[:, :]))
                c.add(V.tensor_tensor(gate[:, 1, :], gate[:, 0, :], dif[:, :, 4], ALU.mult))
                dve.wait_ge(ranks, 1)
                c.step(V.tensor_copy(rk[:, :, :], pr[:, 0:192].rearrange("p (t e) -> p t e", t=6)))
                c.step(V.tensor_tensor(cmp9[:, :, :], rk[:, 5, :].unsqueeze(2).to_broadcast([128, 32, 9]),
                                       C("m64").unsqueeze(1).to_broadcast([128, 32, 9]), ALU.is_gt))
                c.step(V.tensor_reduce(tiles[:, :], cmp9[:, :, :], AX.X, ALU.add))
                c.step(V.tensor_copy(sc[:, 0, :], tiles[:, :]))
                cur = 0
                for sh in (1, 2, 4, 8, 16):
                    c.add(V.tensor_copy(sc[:, 1 - cur, 0:sh], sc[:, cur, 0:sh]))
                    c.step(V.tensor_tensor(sc[:, 1 - cur, sh:32], sc[:, cur, sh:32], sc[:, cur, 0:32 - sh], ALU.add))
                    cur = 1 - cur
                ends = sc[:, cur, :]
                c.add(V.tensor_tensor(big[:, :, :], ends.unsqueeze(1).to_broadcast([128, NTILE, 32]),
                                      C("tile").unsqueeze(2).to_broadcast([128, NTILE, 32]), ALU.is_le))
                c.step(V.tensor_tensor(tiles[:, :], ends, tiles[:, :], ALU.subtract))
                c.add(V.tensor_reduce(ex[:, 0, :], big[:, :, :], AX.X, ALU.add))
                c.step(V.tensor_scalar(tiles[:, :], tiles[:, :], float(SLOT), None, ALU.mult))
                c.add(V.tensor_scalar(ex[:, 1, :], ex[:, 0, :], NE - 0.5, 1.0e6, ALU.is_gt, ALU.mult))
                c.step(V.tensor_scalar(ex[:, 0, :], ex[:, 0, :], 128.0, float(l * NE * 128), ALU.mult, ALU.add))
                c.step(V.tensor_tensor(ex[:, 0, :], ex[:, 0, :], ex[:, 1, :], ALU.add))
                c.add(V.tensor_scalar(widx[:, :], ex[:, 0, :], C("pidx"), None, ALU.add))
                c.step(V.tensor_tensor(rk[:, 0:5, :], rk[:, 0:5, :], tiles[:, :].unsqueeze(1).to_broadcast([128, 5, 32]),
                                       ALU.add))
                for k in range(2):
                    c.add(V.tensor_tensor(As[:, k, :, :], As[:, k, :, :], rk[:, 0:5, :], ALU.mult))
                c.wait()
                c.step(V.tensor_reduce(pos[:, :], As[:, :, :, :].rearrange("p k t e -> p (k t) e"), AX.X, ALU.add))
                c.add(V.tensor_copy(posi[:, :, :].rearrange("p k t -> p (k t)"), pos[:, :]))
                c.step(V.tensor_tensor(ge[:, :, :], pos[:, :].unsqueeze(2).to_broadcast([128, 10, NPAIR + 1]),
                                       C("m128").unsqueeze(1).to_broadcast([128, 10, NPAIR + 1]), ALU.is_ge))
                c.add(V.tensor_tensor(ci[:, :, :], ge[:, :, 0:NPAIR], ge[:, :, 1:NPAIR + 1], ALU.subtract))
                c.step(V.tensor_reduce(rr[:, 0, :], ge[:, :, 1:NPAIR + 1], AX.X, ALU.add))
                c.step(V.scalar_tensor_tensor(out=rr[:, 1, :], in0=rr[:, 0, :], scalar=-128.0, in1=pos[:, :],
                                              op0=ALU.mult, op1=ALU.add))
                for k in range(2):
                    c.add(V.tensor_tensor(ci[:, 5 * k:5 * k + 5, :], ci[:, 5 * k:5 * k + 5, :],
                                          C("tokid").unsqueeze(2).to_broadcast([128, 5, NPAIR]), ALU.mult))
                c.wait()
                V.tensor_tensor(ohr[:, :, :], rr[:, 1, :].unsqueeze(2).to_broadcast([128, 10, 128]),
                                C("iota").unsqueeze(1).to_broadcast([128, 10, 128]), ALU.is_equal).then_inc(onehots, 1)
                dve.wait_ge(toks, 1)
                c.step(V.tensor_copy(tokof[:, :], pt[:, 0:NPAIR]))

        with Scope(nc, name + "b") as s:
            NR = 3
            wg = [s.sb(f"wg{i}", [128, KD * 2 * DE]) for i in range(2 * NR)]
            wd = [s.sb(f"wd{i}", [128, 2 * D]) for i in range(2 * NR)]
            xg = [s.sb(f"xg{i}", [128, D]) for i in range(2)]
            xgT = [s.sb(f"xgT{i}", [128, KD, 128]) for i in range(2)]
            sg = s.sb("sg", [128, DE])
            hh = s.sb("hh", [128, DE])
            hT = s.sb("hT", [128, 2, 128])
            Y = [s.sb(f"Y{i}", [128, D]) for i in range(2)]
            px = [s.ps(f"x{i}") for i in range(2)]
            pg = [s.ps(f"g{i}") for i in range(2)]
            ph = s.ps("h")
            py = [s.ps(f"y{i}") for i in range(2)]
            wl = [s.sem(f"weights{i}") for i in range(NR)]
            xl = [s.sem(f"rows{i}") for i in range(2)]
            ys = [s.sem(f"stored{i}") for i in range(2)]
            (xt, xta, xtd, gu, sl, hr, ht, htc, dn, ya, ydv) = (s.sem(x) for x in (
                "x_T", "x_act", "x_dve", "gate_up", "silu", "hidden", "h_T", "h_copied", "down", "y_act", "y_dve"))
            w_gu = A["moe_w_gate_up"].rearrange("l g e (p j) f -> (l g e p) (j f)", p=128)
            w_dn = A["moe_w_down"].rearrange("l g e (p j) d -> (l g e p) (j d)", p=128)
            NWROW = 2 * NE * 128
            block = s.block()

            @block.gpsimd
            def _(pool):
                def rows(i):
                    if i >= 2:
                        pool.wait_ge(xt, i - 1)
                    nc.gpsimd.indirect_dma_start(out=xg[i % 2][:, :], out_offset=None, in_=xd,
                                                 in_offset=bass.IndirectOffsetOnAxis(ap=tokof[:, i:i + 1], axis=0))\
                        .then_inc(xl[i % 2], 16)

                rows(0)
                for i in range(NPAIR):
                    if i + 1 < NPAIR:
                        rows(i + 1)
                    if i >= NR:
                        pool.wait_ge(gu, i - NR + 1)
                        pool.wait_ge(dn, i - NR + 1)
                    for a in range(2):
                        at = bass.IndirectOffsetOnAxis(ap=widx[:, 2 * i + a:2 * i + a + 1], axis=0)
                        for dst, src in ((wg, w_gu), (wd, w_dn)):
                            nc.gpsimd.indirect_dma_start(out=dst[2 * (i % NR) + a][:, :], out_offset=None, in_=src,
                                                         in_offset=at, bounds_check=NWROW - 1, oob_is_err=False)\
                                .then_inc(wl[i % NR], 16)

            @block.tensor
            def _(pe):
                def x_T(i):
                    pe.wait_ge(xl[i % 2], 16 * (i // 2 + 1))
                    if i >= 1:
                        pe.wait_ge(xta, i)
                        pe.wait_ge(xtd, i)
                    xv = xg[i % 2][:, :].rearrange("r (p j) -> r j p", j=KD)
                    for j in range(KD):
                        last = nc.tensor.transpose(px[j // 4][:, (j % 4) * 128:(j % 4) * 128 + 128], xv[:, j, :],
                                                   C("ident"))
                    last.then_inc(xt, 1)

                def gate_up(i):
                    pe.wait_ge(wl[i % NR], 64 * (i // NR + 1))
                    pe.wait_ge(xta, i + 1)
                    pe.wait_ge(xtd, i + 1)
                    if i >= 2:
                        pe.wait_ge(hr, i - 1)
                    for j in range(KD):
                        for a in range(2):
                            last = nc.tensor.matmul(pg[i % 2][64 * a:64 * a + 64, :], xgT[i % 2][:, j, 64 * a:64 * a + 64],
                                                    wg[2 * (i % NR) + a][:, j * 512:(j + 1) * 512],
                                                    start=(j == 0), stop=(j == KD - 1))
                    last.then_inc(gu, 1)

                def h_T(i):
                    pe.wait_ge(hr, i + 1)
                    if i >= 1:
                        pe.wait_ge(htc, i)
                    hv = hh[:, :].rearrange("r (p j) -> r j p", j=2)
                    for j in range(2):
                        last = nc.tensor.transpose(ph[:, j * 128:(j + 1) * 128], hv[:, j, :], C("ident"))
                    last.then_inc(ht, 1)

                def down(i):
                    pe.wait_ge(htc, i + 1)
                    if i >= 1:
                        pe.wait_ge(ya, i)
                        pe.wait_ge(ydv, i)
                    for n in range(2):
                        for j in range(2):
                            for a in range(2):
                                last = nc.tensor.matmul(py[n][64 * a:64 * a + 64, :], hT[:, j, 64 * a:64 * a + 64],
                                                        wd[2 * (i % NR) + a][:, j * D + n * 512:j * D + (n + 1) * 512],
                                                        start=(j == 0), stop=(j == 1))
                    last.then_inc(dn, 1)

                x_T(0)
                for i in range(NPAIR + 1):
                    if i < NPAIR:
                        gate_up(i)
                    if i >= 1:
                        h_T(i - 1)
                    if i + 1 < NPAIR:
                        x_T(i + 1)
                    if i >= 1:
                        down(i - 1)

            def copy_x(i, half, eng, sem):
                eng.wait_ge(xt, i + 1)
                if i >= 2:
                    eng.wait_ge(gu, i - 1)
                dst = xgT[i % 2][:, 4 * half:4 * half + 4, :].rearrange("p j n -> p (j n)")
                ins = nc.scalar.activation(dst, px[half][:, :], ACT.Copy) if half == 0 else \
                    nc.vector.tensor_copy(dst, px[half][:, :])
                ins.then_inc(sem, 1)

            def copy_y(i, half, eng, sem):
                eng.wait_ge(dn, i + 1)
                if i >= 2:
                    eng.wait_ge(ys[i % 2], 16 * (i // 2))
                dst = Y[i % 2][:, 512 * half:512 * half + 512]
                ins = nc.scalar.activation(dst, py[half][:, :], ACT.Copy) if half == 0 else \
                    nc.vector.tensor_copy(dst, py[half][:, :])
                ins.then_inc(sem, 1)

            @block.scalar
            def _(act):
                copy_x(0, 0, act, xta)
                for i in range(NPAIR + 1):
                    if i < NPAIR:
                        act.wait_ge(gu, i + 1)
                        if i >= 1:
                            act.wait_ge(hr, i)
                        nc.scalar.activation(sg[:, :], pg[i % 2][:, 0:DE], ACT.Silu).then_inc(sl, 1)
                    if i >= 1:
                        act.wait_ge(ht, i)
                        if i >= 2:
                            act.wait_ge(dn, i - 1)
                        nc.scalar.activation(hT[:, :, :].rearrange("p j n -> p (j n)"), ph[:, 0:256], ACT.Copy)\
                            .then_inc(htc, 1)
                    if i + 1 < NPAIR:
                        copy_x(i + 1, 0, act, xta)
                    if i >= 1:
                        copy_y(i - 1, 0, act, ya)

            @block.vector
            def _(dve):
                copy_x(0, 1, dve, xtd)
                for i in range(NPAIR + 1):
                    if i < NPAIR:
                        dve.wait_ge(sl, i + 1)
                        if i >= 1:
                            dve.wait_ge(ht, i)
                        nc.vector.tensor_tensor(hh[:, :], sg[:, :], pg[i % 2][:, DE:2 * DE], ALU.mult).then_inc(hr, 1)
                    if i + 1 < NPAIR:
                        copy_x(i + 1, 1, dve, xtd)
                    if i >= 1:
                        copy_y(i - 1, 1, dve, ydv)

            @block.sync
            def _(sp):
                for i in range(NPAIR):
                    sp.wait_ge(ya, i + 1)
                    sp.wait_ge(ydv, i + 1)
                    sp.dma_start(yd[128 * i:128 * i + 128, :], Y[i % 2][:, :]).then_inc(ys[i % 2], 16)
                for i in range(2):
                    sp.wait_ge(ys[i], 16 * (NPAIR // 2))

        with Scope(nc, name + "c") as s:
            y = [s.sb(f"y{i}", [128, 2, D]) for i in range(5)]
            got, dv = [s.sem(f"got{i}") for i in range(5)], s.sem("dve_steps")
            block = s.block()

            @block.gpsimd
            def _(pool):
                for t, P in TILES:
                    for k in range(2):
                        nc.gpsimd.indirect_dma_start(out=y[t][:P, k, :], out_offset=None, in_=yd,
                                                     in_offset=bass.IndirectOffsetOnAxis(ap=posi[:P, k, t:t + 1], axis=0))\
                            .then_inc(got[t], 16)

            @block.vector
            def _(dve):
                c, V = Count(dve, dv), nc.vector
                for t, P in TILES:
                    c.step(V.tensor_scalar(X[:P, t, :], X[:P, t, :], ALPHA, None, ALU.mult))
                    dve.wait_ge(got[t], 32)
                    for k in range(2):
                        c.step(V.scalar_tensor_tensor(out=X[:P, t, :], in0=y[t][:P, k, :], scalar=gate[:P, k, t:t + 1],
                                                      in1=X[:P, t, :], op0=ALU.mult, op1=ALU.add))


def mixer_cd(nc, A, X, C):
    with Scope(nc, "cd") as L:
        mixT = L.sb("mixT", [128, KD, NTOK])
        vt = L.sb("vt", [128, 5, 512])
        qkT = L.sb("qkT", [128, KD, NTOK])
        with Scope(nc, "cdp") as F:
            qk = F.sb("qk", [128, 5, 1024])
            uP = F.sb("uP", [128, 4, PBUF + SEQ])
            uS = F.sb("uS", [128, 4, NB, PBUF + NS])
            with Scope(nc, "cdx") as s:
                xT = s.sb("xT", [128, KD, NTOK])
                transpose_stage(nc, "cdt", C, X, xT)

                def jobs_of(n, w):
                    out = []
                    if n == 0:
                        for f in range(4):
                            out.append(Job(n, 128, 512, lambda k, f=f: w[:, k, f * 128:f * 128 + 128],
                                           lambda k: xT[:, k, 0:512], "act",
                                           lambda p, f=f: nc.scalar.activation(uP[:, f, PBUF:], p, ACT.Copy)))
                            out.append(Job(n, 128, 32, lambda k, f=f: w[:, k, f * 128:f * 128 + 128],
                                           lambda k: xT[:, k, 512:544], "dve",
                                           lambda p, f=f: nc.vector.tensor_copy(
                                               uS[:, f, :, PBUF:], p.rearrange("p (b s) -> p b s", s=NS))))
                        return out
                    for t, P in TILES:
                        def copy(p, t=t, P=P):
                            dst = vt[:P, t, :] if n == 3 else qk[:P, t, (n - 1) * 512:n * 512]
                            if t % 2:
                                return nc.scalar.activation(dst, p, ACT.Copy)
                            return nc.vector.tensor_copy(dst, p)
                        out.append(Job(n, P, 512, lambda k, t=t, P=P: xT[:, k, tok0(t):tok0(t) + P],
                                       lambda k: w[:, k, 0:512], "act" if t % 2 else "dve", copy))
                    return out

                project_stage(nc, "cdi", A["cd_w_in"], [(512 * i, 512 * i + 512) for i in range(4)], 512, xT, jobs_of)
            rope_and_pool(nc, A, C, qk, vt, uP, uS, mixT)
            transpose_stage(nc, "cdq", C, qk, qkT)
        attend_prompt(nc, C, qkT, vt, mixT)
        attend_sample(nc, A, C, qkT, vt, mixT)
        project_stage(nc, "cdo", A["cd_w_out"], [(0, 512), (512, 1024)], 512, mixT, out_jobs(nc, X, mixT), nbuf=2)


def rope_and_pool(nc, A, C, qk, vt, uP, uS, mixT):
    with Scope(nc, "pl") as s:
        r1, r2 = s.sb("r1", [128, 5, 16, 8]), s.sb("r2", [128, 5, 16, 8])
        r3, r4 = s.sb("r3", [128, 5, 16, 8]), s.sb("r4", [128, 5, 16, 8])
        st = s.sb("st", [NB * PBUF, 512])
        wp = s.sb("wp", [128, 4, 128])
        pscr, psc = s.sb("pscr", [4, 128]), s.sb("psc", [128, 4])
        sP = [s.sb(f"sP{i}", [128, PBUF + SEQ]) for i in range(2)]
        sS = [s.sb(f"sS{i}", [128, NB, PBUF + NS]) for i in range(2)]
        Df = s.sb("Df", [128, 4, NTOK])
        newS = s.sb("newS", [128, 4, NB * PBUF])
        outs = s.sb("outs", [128, 2, 512])
        pst, pnp, pns = s.ps("st"), s.ps("np"), s.ps("ns")
        pm = [s.ps(f"m{i}") for i in range(4)]
        (loaded, st_T, dv, act_c, rot, stored, ext, new_c, new_T, new_o, dif, mixed) = (s.sem(x) for x in (
            "loaded", "st_T", "dve_steps", "act_c", "rotated", "stored", "ext", "new_c", "new_T", "new_o", "dif", "mixed"))
        block = s.block()

        @block.sync
        def _(sp):
            sp.dma_start(st[:, :], A["state_pool"].rearrange("b i c -> (b i) c")).then_inc(loaded, 16)
            sp.dma_start(wp[:, :, :], A["cd_w_pool"].rearrange("g c d -> c g d")).then_inc(loaded, 16)
            sp.dma_start(pscr[:, :], A["cd_pool_scale"].rearrange("(g d) -> g d", d=128)).then_inc(loaded, 16)
            sp.dma_start(A["v_p"][0].rearrange("(t p) h d -> p t (h d)", p=128), vt[:, 0:4, :]).then_inc(stored, 16)
            sp.dma_start(A["v_s"].rearrange("b s h d -> (b s) (h d)"), vt[0:32, 4, :]).then_inc(stored, 16)
            sp.wait_ge(rot, 1)
            sp.dma_start(A["k_p"][0].rearrange("(t p) h d -> p t (h d)", p=128), qk[:, 0:4, 512:1024]).then_inc(stored, 16)
            sp.dma_start(A["k_s"].rearrange("b s h d -> (b s) (h d)"), qk[0:32, 4, 512:1024]).then_inc(stored, 16)
            sp.wait_ge(new_o, 1)
            sp.dma_start(A["pool_p"][0], outs[0:PBUF, 0, :]).then_inc(stored, 16)
            sp.dma_start(A["pool_s"].rearrange("b i c -> (b i) c"), outs[0:NB * PBUF, 1, :]).then_inc(stored, 16)
            sp.wait_ge(stored, 16 * 6)

        @block.tensor
        def _(pe):
            pe.wait_ge(loaded, 48)
            for g in range(4):
                last = nc.tensor.transpose(pst[:, g * 120:(g + 1) * 120], st[:, g * 128:(g + 1) * 128],
                                           C("ident")[:120, :120])
            last = nc.tensor.transpose(pst[:, 480:484], pscr[:, :], C("ident")[:4, :4])
            last.then_inc(st_T, 1)
            pe.wait_ge(new_c, 1)
            for g in range(4):
                nc.tensor.transpose(pnp[:PBUF, g * 128:(g + 1) * 128], uP[:, g, SEQ:SEQ + PBUF], C("ident"))
            for g in range(4):
                last = nc.tensor.transpose(pns[:NB * PBUF, g * 128:(g + 1) * 128], newS[:, g, :], C("ident"))
            last.then_inc(new_T, 1)
            for g in range(4):
                pe.wait_ge(dif, g + 1)
                if g >= 2:
                    pe.wait_ge(mixed, g - 1)
                a, b = pm[2 * (g % 2)], pm[2 * (g % 2) + 1]
                nc.tensor.matmul(a[:, :], wp[:, g, :], Df[:, g, 0:512], start=True, stop=True)
                nc.tensor.matmul(b[:, 0:32], wp[:, g, :], Df[:, g, 512:544], start=True, stop=True).then_inc(act_c, 1)

        @block.scalar
        def _(act):
            for g in range(4):
                act.wait_ge(act_c, g + 1)
                a, b = pm[2 * (g % 2)], pm[2 * (g % 2) + 1]
                nc.scalar.activation(mixT[:, g, 0:512], a[:, :], ACT.Copy, scale=psc[:, g:g + 1])
                nc.scalar.activation(mixT[:, g, 512:544], b[:, 0:32], ACT.Copy, scale=psc[:, g:g + 1]).then_inc(mixed, 1)

        @block.vector
        def _(dve):
            c, V = Count(dve, dv), nc.vector
            halves = []
            for ts, P in (((0, 4), 128), ((4, 5), 32)):
                n = ts[1] - ts[0]
                sl = slice(ts[0], ts[1])
                w = qk[:P, sl, :].rearrange("p t (h d) -> p t h d", d=64)
                x1, x2 = w[:, :, :, 0:8], w[:, :, :, 8:16]
                table = C("rope")[:P, :].rearrange("p (t c) -> p t c", c=16)[:, sl, :]
                cos = table[:, :, 0:8].unsqueeze(2).to_broadcast([P, n, 16, 8])
                sin = table[:, :, 8:16].unsqueeze(2).to_broadcast([P, n, 16, 8])
                for dst, x, f in ((r1, x1, cos), (r2, x2, sin), (r3, x2, cos), (r4, x1, sin)):
                    c.add(V.tensor_tensor(dst[:P, sl, :, :], x, f, ALU.mult))
                halves.append((P, sl, x1, x2))
            c.wait()
            for P, sl, x1, x2 in halves:
                c.add(V.tensor_tensor(x1, r1[:P, sl, :, :], r2[:P, sl, :, :], ALU.subtract))
                last = V.tensor_tensor(x2, r3[:P, sl, :, :], r4[:P, sl, :, :], ALU.add)
                if P == 128:
                    c.add(last)
            last.then_inc(rot, 1)
            c.step(V.memset(uP[:, :, 0:PBUF], 0.0))
            dve.wait_ge(st_T, 1)
            c.add(V.tensor_copy(psc[:, :], pst[:, 480:484]))
            c.step(V.tensor_copy(uS[:, :, :, 0:PBUF], pst[:, 0:480].rearrange("p (g b i) -> p g b i", g=4, b=NB)))
            V.tensor_copy(newS[:, :, :].rearrange("p g (b i) -> p g b i", b=NB), uS[:, :, :, NS:]).then_inc(new_c, 1)
            for g, w in enumerate(WINDOWS):
                sp_, ss_ = uP[:, g, :], uS[:, g, :, :]
                width, i = 1, 0
                while width < w:
                    n = PBUF + SEQ - width
                    c.add(V.tensor_tensor(sP[i][:, width:], sp_[:, width:], sp_[:, 0:n], ALU.add))
                    c.add(V.tensor_copy(sP[i][:, 0:width], sp_[:, 0:width]))
                    c.add(V.tensor_tensor(sS[i][:, :, width:], ss_[:, :, width:], ss_[:, :, 0:PBUF + NS - width], ALU.add))
                    c.step(V.tensor_copy(sS[i][:, :, 0:width], ss_[:, :, 0:width]))
                    sp_, ss_ = sP[i], sS[i]
                    width, i = 2 * width, 1 - i
                inv = C("invcnt")[:, 16 * g:16 * g + PBUF]
                c.add(V.tensor_tensor(Df[:, g, 0:PBUF], sp_[:, PBUF:2 * PBUF], inv, ALU.mult))
                c.add(V.scalar_tensor_tensor(out=Df[:, g, PBUF:512], in0=sp_[:, 2 * PBUF:], scalar=1.0 / w,
                                             in1=uP[:, g, 2 * PBUF:], op0=ALU.mult, op1=ALU.subtract))
                c.add(V.scalar_tensor_tensor(out=Df[:, g, 512:544].rearrange("p (b s) -> p b s", s=NS),
                                             in0=ss_[:, :, PBUF:], scalar=1.0 / w, in1=uS[:, g, :, PBUF:],
                                             op0=ALU.mult, op1=ALU.subtract))
                c.wait()
                V.tensor_tensor(Df[:, g, 0:PBUF], Df[:, g, 0:PBUF], uP[:, g, PBUF:2 * PBUF], ALU.subtract)\
                 .then_inc(dif, 1)
            dve.wait_ge(new_T, 1)
            V.tensor_copy(outs[0:PBUF, 0, :], pnp[:PBUF, :])
            V.tensor_copy(outs[0:NB * PBUF, 1, :], pns[:NB * PBUF, :]).then_inc(new_o, 1)


def attend_prompt(nc, C, qkT, vt, mixT):
    units = [(h, t) for h in range(8) for t in range(4)]
    scale = 64 ** -0.5
    with Scope(nc, "ap") as s:
        Pm = [s.sb(f"P{i}", [128, 512]) for i in range(3)]
        PT = [s.sb(f"PT{i}", [128, 512]) for i in range(2)]
        nb = s.sb("nb", [128, len(units)])
        den = s.sb("den", [128, len(units)])
        ot = s.sb("ot", [128, 4, 512])
        psc = [s.ps(f"s{i}") for i in range(3)]
        ptr = [s.ps(f"t{i}") for i in range(2)]
        po = [s.ps(f"o{i}") for i in range(2)]
        (sc, dv, mxd, ex, tr, ptc, pv, od, o_T, o_c) = (s.sem(x) for x in (
            "scores", "dve_steps", "max_ready", "exps", "P_T", "P_copied", "pv", "o_ready", "o_T", "o_copied"))
        block = s.block()
        n = len(units)

        @block.tensor
        def _(pe):
            for u in range(n + 2):
                if u < n:
                    h, t = units[u]
                    r, w = slice(64 * (h % 2), 64 * (h % 2) + 64), (t + 1) * 128
                    if u >= 3:
                        pe.wait_ge(ex, u - 2)
                    nc.tensor.matmul(psc[u % 3][:, 0:w], qkT[r, h // 2, 128 * t:128 * t + 128],
                                     qkT[r, 4 + h // 2, 0:w], start=True, stop=True).then_inc(sc, 1)
                if 1 <= u <= n:
                    h, t = units[u - 1]
                    pe.wait_ge(ex, u)
                    if u >= 3:
                        pe.wait_ge(ptc, u - 2)
                    for k in range(t + 1):
                        last = nc.tensor.transpose(ptr[(u - 1) % 2][:, 128 * k:128 * k + 128],
                                                   Pm[(u - 1) % 3][:, 128 * k:128 * k + 128], C("ident"))
                    last.then_inc(tr, 1)
                if u >= 2:
                    h, t = units[u - 2]
                    pe.wait_ge(ptc, u - 1)
                    if u >= 4:
                        pe.wait_ge(od, u - 3)
                    for k in range(t + 1):
                        last = nc.tensor.matmul(po[u % 2][:, 0:64], PT[u % 2][:, 128 * k:128 * k + 128],
                                                vt[:, k, h * 64:(h + 1) * 64], start=(k == 0), stop=(k == t))
                    last.then_inc(pv, 1)
            pe.wait_ge(od, n)
            for t in range(4):
                for f in range(4):
                    last = nc.tensor.transpose((psc + ptr)[t][:, f * 128:(f + 1) * 128],
                                               ot[:, t, f * 128:(f + 1) * 128], C("ident"))
                last.then_inc(o_T, 1)

        @block.vector
        def _(dve):
            c, V = Count(dve, dv), nc.vector
            for u in range(n + 2):
                if u < n:
                    h, t = units[u]
                    w = (t + 1) * 128
                    dve.wait_ge(sc, u + 1)
                    c.step(V.tensor_tensor(psc[u % 3][:, 128 * t:w], psc[u % 3][:, 128 * t:w], C("causal"), ALU.add))
                    c.step(V.reduce_max(nb[:, u:u + 1], psc[u % 3][:, 0:w], AX.X))
                    V.tensor_scalar(nb[:, u:u + 1], nb[:, u:u + 1], -scale, None, ALU.mult).then_inc(mxd, 1)
                if u >= 2:
                    h, t = units[u - 2]
                    dve.wait_ge(ex, u - 1)
                    c.step(V.reciprocal(den[:, u - 2:u - 1], den[:, u - 2:u - 1]))
                    dve.wait_ge(pv, u - 1)
                    V.tensor_scalar(ot[:, t, h * 64:(h + 1) * 64], po[u % 2][:, 0:64], den[:, u - 2:u - 1], None,
                                    ALU.mult).then_inc(od, 1)
            for t in range(4):
                dve.wait_ge(o_T, t + 1)
                V.tensor_copy(mixT[:, 4:8, 128 * t:128 * t + 128],
                              (psc + ptr)[t][:, :].rearrange("p (f n) -> p f n", f=4)).then_inc(o_c, 1)

        @block.scalar
        def _(act):
            for u in range(n + 1):
                if u < n:
                    h, t = units[u]
                    w = (t + 1) * 128
                    act.wait_ge(mxd, u + 1)
                    if u >= 3:
                        act.wait_ge(tr, u - 2)
                    nc.scalar.activation(Pm[u % 3][:, 0:w], psc[u % 3][:, 0:w], ACT.Exp, bias=nb[:, u:u + 1],
                                         scale=scale, accum_out=den[:, u:u + 1]).then_inc(ex, 1)
                if u >= 1:
                    h, t = units[u - 1]
                    act.wait_ge(tr, u)
                    if u >= 3:
                        act.wait_ge(pv, u - 2)
                    nc.scalar.activation(PT[(u - 1) % 2][:, 0:(t + 1) * 128], ptr[(u - 1) % 2][:, 0:(t + 1) * 128],
                                         ACT.Copy).then_inc(ptc, 1)


def attend_sample(nc, A, C, qkT, vt, mixT):
    scale = 64 ** -0.5
    with Scope(nc, "as") as s:
        NBUF = 2
        ring = [[s.sb(f"kv{i}{b}", [128, 4 * 512]) for b in range(4)] for i in range(NBUF)]
        KT = [s.sb(f"KT{b}", [128, 4, 512]) for b in range(4)]
        pta = s.sb("pta", [128, NB * NPG], I32)
        pti, ptf = s.sb("pti", [128, 32], I32), s.sb("ptf", [128, 32])
        Q = s.sb("Q", [128, NB, 4, 32])
        S = s.sb("S", [128, 4 * 512 + NS])
        PT = s.sb("PT", [128, 16, 128])
        own, ownT = s.sb("own", [128, 32]), s.sb("ownT", [32, 128])
        gs, rk, gt8, eq8, pen = s.sb("gs", [128, 8]), s.sb("rk", [128, 8]), s.sb("gt8", [128, 8, 8]), s.sb("eq8", [128, 8, 8]), s.sb("pen", [128, 8])
        nb, den = s.sb("nb", [128, 1]), s.sb("den", [128, 1])
        Oh, wh = s.sb("Oh", [128, 512]), s.sb("wh", [128, 8])
        ptk = [s.ps(f"k{i}") for i in range(4)]
        pss = [s.ps(f"s{i}") for i in range(2)]
        po, pw = s.ps("o"), s.ps("w")
        (pt_l, dv, idx_r, k_T, kcp, kcp2, scored, sccp, q_r, soft, exs, pT, pTc, ownr, ownTr, ownc, pvd, oh_r, o_t,
         o_c, kvused) = (s.sem(x) for x in (
             "pages_loaded", "dve_steps", "index_ready", "K_T", "K_act", "K_dve", "scored", "s_copied", "Q_ready",
             "softmax_in", "exps", "P_T", "P_copied", "own_ready", "own_T", "own_copied", "pv", "O_ready", "O_T",
             "O_copied", "kv_used"))
        kvl = [s.sem(f"kv_loaded{i}") for i in range(NBUF)]
        loads = [(G, kind, pq) for G in range(2) for kind in "kv" for pq in range(4)]
        views = {k: A["cache_" + k].rearrange("n (c r) h d -> (n c) (r h d)", r=4) for k in "kv"}
        block = s.block()

        @block.sync
        def _(sp):
            sp.dma_start(pta[:, :], A["page_table"].rearrange("b n -> (b n)").partition_broadcast(128)).then_inc(pt_l, 16)

        @block.gpsimd
        def _(pool):
            pool.wait_ge(idx_r, 1)
            for n, (G, kind, pq) in enumerate(loads):
                if n >= NBUF:
                    m = n - NBUF + 1
                    if loads[n - NBUF][1] == "k":
                        pool.wait_ge(k_T, 4 * sum(q[1] == "k" for q in loads[:m]))
                    else:
                        pool.wait_ge(kvused, sum(q[1] == "v" for q in loads[:m]))
                for b in range(4):
                    at = (4 * G + b) * 4 + pq
                    nc.gpsimd.indirect_dma_start(out=ring[n % NBUF][b][:, :], out_offset=None, in_=views[kind],
                                                 in_offset=bass.IndirectOffsetOnAxis(ap=pti[:, at:at + 1], axis=0))\
                        .then_inc(kvl[n % NBUF], 16)

        @block.tensor
        def _(pe):
            pe.wait_ge(q_r, 1)
            nk = 0
            for n, (G, kind, pq) in enumerate(loads):
                pe.wait_ge(kvl[n % NBUF], 64 * (n // NBUF + 1))
                if kind == "k":
                    for b in range(4):
                        if nk:
                            pe.wait_ge(kcp, 2 * nk)
                            pe.wait_ge(kcp2, 2 * nk)
                        for r in range(4):
                            for c in range(4):
                                last = nc.tensor.transpose(ptk[c][:, r * 128:(r + 1) * 128],
                                                           ring[n % NBUF][b][:, r * 512 + c * 128:r * 512 + (c + 1) * 128],
                                                           C("ident"))
                        last.then_inc(k_T, 1)
                        nk += 1
                    pe.wait_ge(kcp, 2 * nk)
                    pe.wait_ge(kcp2, 2 * nk)
                    ns = G * 5 + pq
                    if ns >= 2:
                        pe.wait_ge(sccp, ns - 1)
                    for c in range(4):
                        for b in range(4):
                            last = nc.tensor.matmul(pss[ns % 2][32 * b:32 * b + 32, :], Q[:, 4 * G + b, c, :],
                                                    KT[b][:, c, :], start=(c == 0), stop=(c == 3),
                                                    tile_position=(0, 32 * b))
                    last.then_inc(scored, 1)
                    if pq == 3:
                        ns += 1
                        pe.wait_ge(sccp, ns - 1)
                        for b in range(4):
                            for c in range(4):
                                tok = 512 + 4 * (4 * G + b)
                                last = nc.tensor.matmul(pss[ns % 2][32 * b:32 * b + 32, 0:NS], Q[:, 4 * G + b, c, :],
                                                        qkT[:, 4 + c, tok:tok + NS], start=(c == 0), stop=(c == 3),
                                                        tile_position=(0, 32 * b))
                        last.then_inc(scored, 1)
                else:
                    if pq == 0:
                        pe.wait_ge(exs, G + 1)
                        for q in range(4):
                            for r in range(4):
                                last = nc.tensor.transpose(ptk[q][:, r * 128:(r + 1) * 128],
                                                           S[:, q * 512 + r * 128:q * 512 + (r + 1) * 128], C("ident"))
                            last.then_inc(pT, 1)
                        pe.wait_ge(ownr, G + 1)
                        if G:
                            pe.wait_ge(o_c, G)
                        nc.tensor.transpose(pw[0:32, 0:128], own[:, :], C("ident")).then_inc(ownTr, 1)
                        pe.wait_ge(pTc, 4 * G + 4)
                        if G:
                            pe.wait_ge(oh_r, G)
                    for r in range(4):
                        for b in range(4):
                            last = nc.tensor.matmul(po[32 * b:32 * b + 32, :], PT[:, 4 * pq + r, 32 * b:32 * b + 32],
                                                    ring[n % NBUF][b][:, r * 512:(r + 1) * 512],
                                                    start=(pq == 0 and r == 0), stop=False, tile_position=(0, 32 * b),
                                                    skip_group_check=True)
                    last.then_inc(kvused, 1)
                    if pq == 3:
                        pe.wait_ge(ownc, G + 1)
                        for b in range(4):
                            last = nc.tensor.matmul(po[32 * b:32 * b + 32, :], ownT[:, 32 * b:32 * b + 32],
                                                    vt[0:32, 4, :], start=False, stop=True, tile_position=(0, 32 * b),
                                                    skip_group_check=True)
                        last.then_inc(pvd, 1)
                        pe.wait_ge(oh_r, G + 1)
                        for c in range(4):
                            last = nc.tensor.matmul(pw[:, 128 + 16 * c:144 + 16 * c], Oh[:, c * 128:(c + 1) * 128],
                                                    C("sumh"), start=True, stop=True)
                        last.then_inc(o_t, 1)

        kvk = [(G, pq, b) for G in range(2) for pq in range(4) for b in range(4)]

        @block.scalar
        def _(act):
            for n, (G, pq, b) in enumerate(kvk):
                act.wait_ge(k_T, n + 1)
                if n >= 4:
                    act.wait_ge(scored, G * 5 + pq)
                for c in range(2):
                    ins = nc.scalar.activation(KT[b][:, c, :], ptk[c][:, :], ACT.Copy)
                    ins.then_inc(kcp, 1)
                if (pq, b) == (3, 3):
                    act.wait_ge(soft, G + 1)
                    nc.scalar.activation(S[:, :], S[:, :], ACT.Exp, bias=nb[:, 0:1], scale=scale,
                                         accum_out=den[:, 0:1]).then_inc(exs, 1)
                    for q in range(4):
                        act.wait_ge(pT, 4 * G + q + 1)
                        if G and q == 0:
                            act.wait_ge(pvd, G)
                        nc.scalar.activation(PT[:, 4 * q:4 * q + 4, :].rearrange("p r n -> p (r n)"), ptk[q][:, :],
                                             ACT.Copy).then_inc(pTc, 1)
                    act.wait_ge(ownTr, G + 1)
                    nc.scalar.activation(ownT[:, :], pw[0:32, 0:128], ACT.Copy).then_inc(ownc, 1)

        @block.vector
        def _(dve):
            c, V = Count(dve, dv), nc.vector
            dve.wait_ge(pt_l, 16)
            for g in range(4):
                r = slice(32 * g, 32 * g + 32)
                c.add(V.tensor_copy(ptf[r, :], pta[r, :].rearrange("p (n g) -> p n g", g=4)[:, :, g]))
            c.wait()
            c.step(V.tensor_scalar(ptf[:, :], ptf[:, :], 32.0, C("p32"), ALU.mult, ALU.add))
            V.tensor_copy(pti[:, :], ptf[:, :]).then_inc(idx_r, 1)
            c.step(V.memset(Q[:, :, :, :], 0.0))
            for f in range(4):
                for h in range(2):
                    r = slice(64 * h, 64 * h + 64)
                    last = V.tensor_copy(Q[r, :, f, 4 * (2 * f + h):4 * (2 * f + h) + 4],
                                         qkT[r, f, 512:544].rearrange("p (b s) -> p b s", s=NS))
            last.then_inc(q_r, 1)
            lt8 = C("lt8").rearrange("p (n m) -> p n m", n=8)
            for n, (G, pq, b) in enumerate(kvk):
                dve.wait_ge(k_T, n + 1)
                if n >= 4:
                    dve.wait_ge(scored, G * 5 + pq)
                for f in (2, 3):
                    V.tensor_copy(KT[b][:, f, :], ptk[f][:, :]).then_inc(kcp2, 1)
                if b < 3:
                    continue
                ns = G * 5 + pq
                dve.wait_ge(scored, ns + 1)
                if G and pq == 0:
                    dve.wait_ge(pT, 4)
                V.tensor_copy(S[:, 512 * pq:512 * pq + 512], pss[ns % 2][:, :]).then_inc(sccp, 1)
                dve.wait_ge(sccp, ns + 1)
                sv = S[:, 512 * pq:512 * pq + 512].rearrange("p (r b x) -> p b r x", r=4, b=2)
                c.step(V.tensor_reduce(gs[:, 2 * pq:2 * pq + 2], sv, AX.XY, ALU.add))
                if pq < 3:
                    continue
                dve.wait_ge(scored, ns + 2)
                V.tensor_tensor(S[:, 2048:2052], pss[(ns + 1) % 2][:, 0:NS], C("ownneg"), ALU.add).then_inc(sccp, 1)
                rank(V, c, rk[:, :], gs[:, :], gt8[:, :, :], eq8[:, :, :], lt8)
                c.step(V.tensor_scalar(pen[:, :], rk[:, :], 2.5, NEG, ALU.is_gt, ALU.mult))
                for q in range(4):
                    for bl in range(2):
                        v3 = S[:, 512 * q:512 * q + 512].rearrange("p (r b x) -> p b r x", r=4, b=2)[:, bl, :, :]
                        c.add(V.tensor_scalar(v3, v3, pen[:, 2 * q + bl:2 * q + bl + 1], None, ALU.add))
                c.wait()
                dve.wait_ge(sccp, ns + 2)
                c.step(V.reduce_max(nb[:, :], S[:, :], AX.X))
                V.tensor_scalar(nb[:, :], nb[:, :], -scale, None, ALU.mult).then_inc(soft, 1)
                dve.wait_ge(exs, G + 1)
                c.add(V.reciprocal(den[:, :], den[:, :]))
                V.tensor_tensor(own[:, :].rearrange("p (b k) -> p b k", k=NS),
                                S[:, 2048:2052].unsqueeze(1).to_broadcast([128, NB, NS]),
                                C(f"ownb{G}").rearrange("p (b k) -> p b k", k=NS), ALU.mult).then_inc(ownr, 1)
                c.wait()
                c.step(V.tensor_scalar(wh[:, :], C("hmask"), den[:, 0:1], None, ALU.mult))
                dve.wait_ge(pvd, G + 1)
                V.tensor_tensor(Oh[:, :].rearrange("p (h d) -> p h d", h=8), po[:, :].rearrange("p (h d) -> p h d", h=8),
                                wh[:, :].unsqueeze(2).to_broadcast([128, 8, 64]), ALU.mult).then_inc(oh_r, 1)
                dve.wait_ge(o_t, G + 1)
                V.tensor_copy(mixT[:, 4:8, 512 + 16 * G:528 + 16 * G],
                              pw[:, 128:192].rearrange("p (f n) -> p f n", f=4)).then_inc(o_c, 1)


IN = ["x_prompt", "x_sample", "state_gla", "state_ssm", "state_conv", "state_pool", "cache_k", "cache_v",
      "page_table", "ab_w_in", "ab_w_gate2", "ab_b_gate", "ab_gla_norm", "ab_conv_w", "ab_conv_b", "ab_dt_bias",
      "ab_a_log", "ab_d_skip", "ab_ssm_norm", "ab_w_out", "cd_w_in", "cd_w_pool", "cd_pool_scale", "cd_w_out",
      "moe_w_coarse", "moe_b_coarse", "moe_w_fine", "moe_b_fine", "moe_w_gate_up", "moe_w_down", "ln_g", "ln_b"]
OUT = [("y_p", (1, SEQ, D)), ("y_s", (NB, NS, D)), ("gla_p", (1, 4, 64, 128)), ("ssm_p", (1, 8, 64, 64)),
       ("conv_p", (1, 3, 768)), ("pool_p", (1, PBUF, 512)), ("k_p", (1, SEQ, 8, 64)), ("v_p", (1, SEQ, 8, 64)),
       ("gla_s", (NB, 4, 64, 128)), ("ssm_s", (NB, 8, 64, 64)), ("conv_s", (NB, 3, 768)),
       ("pool_s", (NB, PBUF, 512)), ("k_s", (NB, NS, 8, 64)), ("v_s", (NB, NS, 8, 64))]


def build(nc, A, cols, ncols):
    xd = nc.dram_tensor("token_rows", [NTOK, D], F32).ap()
    yd = [nc.dram_tensor(f"expert_rows{l}", [NROW, D], F32).ap() for l in range(2)]
    Scope.used, Scope.stores = [], {n: nc.alloc_semaphore(f"{n}_stored") for n in ("abg", "abc", "abd", "pl", "out")}
    with Scope(nc, "top") as S:
        X = S.sb("X", [128, 5, D])
        consts = S.sb("consts", [128, ncols])
        mv = S.sb("mv", [128, 5, 2])

        def C(name):
            return consts[:, cols[name][0]:cols[name][1]]

        with Scope(nc, "in") as s:
            loaded = s.sem("loaded")
            block = s.block()

            @block.sync
            def _(sp):
                sp.dma_start(X[:, 0:4, :], A["x_prompt"][0].rearrange("(t p) d -> p t d", p=128)).then_inc(loaded, 16)
                sp.dma_start(X[0:32, 4, :], A["x_sample"].rearrange("b s d -> (b s) d")).then_inc(loaded, 16)
                sp.dma_start(consts[:, :], A["consts"]).then_inc(loaded, 16)
                sp.wait_ge(loaded, 48)

        for l, mixer in enumerate((mixer_ab, mixer_cd)):
            if l:
                reset_stage(nc)
            mixer(nc, A, X, C)
            residual_norm_stage(nc, f"n{l}0", X, mv, A["ln_g"][l, 0], A["ln_b"][l, 0], None)
            moe(nc, A, X, C, l, xd, yd[l])
            residual_norm_stage(nc, f"n{l}1", X, mv, A["ln_g"][l, 1], A["ln_b"][l, 1], None)

        with Scope(nc, "out") as s:
            stored = s.sem("stored")
            block = s.block()

            @block.sync
            def _(sp):
                sp.dma_start(A["y_p"][0].rearrange("(t p) d -> p t d", p=128), X[:, 0:4, :]).then_inc(stored, 16)
                sp.dma_start(A["y_s"].rearrange("b s d -> (b s) d"), X[0:32, 4, :]).then_inc(stored, 16)
                sp.wait_ge(stored, 32)


def kernel(**inputs):
    import concourse.bacc as bacc
    import concourse.bass_utils as bass_utils

    nc = bacc.Bacc("TRN2", target_bir_lowering=False, num_devices=1)
    table, cols = constants()
    arrays = {n: np.ascontiguousarray(inputs[n]) for n in IN}
    arrays["consts"] = table
    A = {}
    feed = {}
    for n, a in arrays.items():
        A[n] = nc.dram_tensor("in_" + n, a.shape, mybir.dt.from_np(a.dtype), kind="ExternalInput").ap()
        feed["in_" + n] = a
    for n, shape in OUT:
        A[n] = nc.dram_tensor("out_" + n, shape, F32, kind="ExternalOutput").ap()
    build(nc, A, cols, table.shape[1])
    r = bass_utils.run_bass_kernel_spmd(nc, [feed], core_ids=[0])
    return tuple(r.results[0]["out_" + n] for n, _ in OUT)
```

```python
from contextlib import ExitStack

import numpy as np

import concourse.bass as bass
from concourse import mybir

F32 = mybir.dt.float32
I32 = mybir.dt.int32
ALU = mybir.AluOpType
ACT = mybir.ActivationFunctionType
AX = mybir.AxisListType

D = 1024
KD = D // 128
SEQ, NB, NS = 512, 8, 4
NTOK = SEQ + NB * NS
TILES = [(t, 128) for t in range(4)] + [(4, NB * NS)]
ALPHA = 4 ** 0.25
LN_EPS, RMS_EPS = 1e-5, 1e-6
PAST, PAGE, NPG = 2048, 128, 16
WINDOWS = (2, 4, 8, 16)
PBUF = 15
NEG = -1e30
NE, SLOT, DE = 32, 64, 256
NPAIR = (NE + (2 * NTOK - NE) // SLOT + 1) // 2
NTILE = 2 * NPAIR
NROW = NTILE * SLOT


def constants():
    p = np.arange(128)
    j, i = p[:, None], p[None, :]
    parts = {}
    parts["ident"] = np.eye(128)
    for name, c in (("p", 64), ("s", NS)):
        same = j // c == i // c
        parts["tri_" + name] = same & (j <= i)
        parts["suf_" + name] = same & (j > i)
        parts["neg_" + name] = np.where(same & (j <= i), 0.0, NEG)
    parts["ones"] = np.ones((128, 128))
    parts["before"] = j < i
    parts["causal"] = np.where(i <= j, 0.0, NEG)
    parts["cmask"] = p[:, None] // 64 == np.arange(2)
    parts["bmask"] = p[:, None] // NS == np.arange(NB)
    parts["lt8"] = np.broadcast_to((np.arange(8)[:, None] > np.arange(8)[None, :]).reshape(1, 64), (128, 64))
    cnt = np.zeros((4, 16))
    for g, w in enumerate(WINDOWS):
        cnt[g, :PBUF] = 1.0 / np.minimum(w, np.arange(PBUF) + 1)
    parts["invcnt"] = np.broadcast_to(cnt.reshape(1, 64), (128, 64))
    parts["pidx"] = p[:, None]
    parts["p32"] = p[:, None] % 32
    parts["iota"] = np.broadcast_to(p[None, :], (128, 128))
    parts["m128"] = np.broadcast_to(128 * np.arange(NPAIR + 1)[None, :], (128, NPAIR + 1))
    tok = p[:, None] + 128 * np.arange(5)
    parts["valid"] = tok < NTOK
    parts["tokid"] = np.where(tok < NTOK, tok, 0)
    parts["m64"] = np.broadcast_to(SLOT * np.arange(1, 9)[None, :], (128, 8))
    parts["e64"] = np.broadcast_to(SLOT * np.arange(NE)[None, :], (128, NE))
    parts["tile"] = np.broadcast_to(np.arange(NTILE - NE)[None, :], (128, NTILE - NE))
    parts["ownneg"] = np.where(np.arange(NS)[None, :] <= p[:, None] % NS, 0.0, NEG)
    for g in range(2):
        parts[f"ownb{g}"] = np.repeat(p[:, None] // 32 + 4 * g == np.arange(NB)[None, :], NS, axis=1)
    parts["hmask"] = (p[:, None] // NS) % 8 == np.arange(8)
    parts["sumh"] = ((p[:, None] // 32) * NS + p[:, None] % NS) == np.arange(16)[None, :]
    half = 8
    inv = (np.float32(500000.0) ** (-np.arange(half, dtype=np.float32) / np.float32(half))).astype(np.float32)
    pos = np.concatenate([np.arange(SEQ), PAST + np.tile(np.arange(NS), NB), np.zeros(96)]).astype(np.float32)
    ang = (pos[:, None] * inv[None, :]).astype(np.float32)
    rope = np.concatenate([np.cos(ang), np.sin(ang)], axis=1).astype(np.float32)
    parts["rope"] = rope.reshape(5, 128, 16).transpose(1, 0, 2).reshape(128, 80)
    at, cols, out = 0, {}, []
    for name, a in parts.items():
        a = np.asarray(a, np.float32).reshape(128, -1)
        cols[name] = (at, at + a.shape[1])
        at += a.shape[1]
        out.append(a)
    return np.ascontiguousarray(np.concatenate(out, axis=1)), cols


class Count:

    def __init__(self, eng, sem):
        self.eng, self.sem, self.n = eng, sem, 0

    def add(self, ins):
        ins.then_inc(self.sem, 1)
        self.n += 1

    def wait(self):
        self.eng.wait_ge(self.sem, self.n)

    def step(self, ins):
        self.add(ins)
        self.wait()


class Scope(ExitStack):
    used, kept = [], {}

    def __init__(self, nc, name):
        super().__init__()
        self.nc, self.name = nc, name

    def sb(self, name, shape, dt=F32):
        return self.enter_context(self.nc.sbuf_tensor(f"{self.name}_{name}", shape, dt))

    def ps(self, name, cols=512):
        return self.enter_context(self.nc.psum_tensor(f"{self.name}_psum_{name}", [128, cols], F32))

    def sem(self, name):
        if f"{self.name}_{name}" in self.kept:
            return self.kept[f"{self.name}_{name}"]
        sem = self.enter_context(self.nc.semaphore(f"{self.name}_{name}"))
        self.used.append(sem.num)
        return sem

    def block(self):
        return self.enter_context(self.nc.Block())


def tok0(t):
    return 128 * t


def reset_stage(nc):
    nums, Scope.used = sorted(set(Scope.used)), []
    with Scope(nc, "reset") as s:
        block = s.block()

        @block.sync
        def _(sp):
            start = nums[0]
            for a, b in zip(nums, nums[1:] + [None]):
                if b != a + 1:
                    sp.sem_clear(range(start, a + 1))
                    start = b


def transpose_stage(nc, name, C, src, dst, chunks=KD):
    units = [(t, P, h) for t, P in TILES for h in range(chunks // 4)]
    with Scope(nc, name) as s:
        ps = [s.ps(f"p{i}") for i in range(4)]
        transposed, by_act, by_dve = s.sem("transposed"), s.sem("by_act"), s.sem("by_dve")
        block = s.block()

        @block.tensor
        def _(pe):
            for u, (t, P, h) in enumerate(units):
                if u >= 4:
                    pe.wait_ge(by_dve if u % 2 else by_act, u // 2 - 1)
                for c in range(4):
                    last = nc.tensor.transpose(ps[u % 4][:, c * P:(c + 1) * P],
                                               src[:P, t, (4 * h + c) * 128:(4 * h + c + 1) * 128],
                                               C("ident")[:P, :P])
                last.then_inc(transposed, 1)

        def out_in(u):
            t, P, h = units[u]
            return (dst[:, 4 * h:4 * h + 4, tok0(t):tok0(t) + P],
                    ps[u % 4][:, :4 * P].rearrange("p (c n) -> p c n", c=4))

        @block.scalar
        def _(act):
            for u in range(0, len(units), 2):
                act.wait_ge(transposed, u + 1)
                o, i = out_in(u)
                nc.scalar.activation(o, i, ACT.Copy).then_inc(by_act, 1)

        @block.vector
        def _(dve):
            for u in range(1, len(units), 2):
                dve.wait_ge(transposed, u + 1)
                o, i = out_in(u)
                nc.vector.tensor_copy(o, i).then_inc(by_dve, 1)


class Job:

    def __init__(self, piece, M, N, lhsT, rhs, by, copy):
        self.piece, self.M, self.N, self.lhsT, self.rhs, self.by, self.copy = piece, M, N, lhsT, rhs, by, copy


def project_stage(nc, name, w_dram, pieces, width, xT, jobs_of, nbuf=3, ahead=None):
    with Scope(nc, name) as s:
        ring = [s.sb(f"w{i}", [128, KD, width]) for i in range(nbuf)]
        ps = [s.ps(f"p{i}") for i in range(8)]
        loaded = [s.sem(f"loaded{i}") for i in range(nbuf)]
        summed, by_act, by_dve = s.sem("summed"), s.sem("by_act"), s.sem("by_dve")
        jobs = [j for n in range(len(pieces)) for j in jobs_of(n, ring[n % nbuf])]
        done = {"act": by_act, "dve": by_dve}
        last_of = [max(i for i, j in enumerate(jobs) if j.piece == n) for n in range(len(pieces))]
        block = s.block()

        if ahead:
            @block.gpsimd
            def _(pool):
                ahead(pool)

        @block.sync
        def _(sp):
            for n, (a, b) in enumerate(pieces):
                if n >= nbuf:
                    sp.wait_ge(summed, last_of[n - nbuf] + 1)
                sp.dma_start(ring[n % nbuf][:, :, 0:b - a],
                             w_dram.rearrange("(k p) n -> p k n", p=128)[:, :, a:b]).then_inc(loaded[n % nbuf], 16)

        @block.tensor
        def _(pe):
            for i, j in enumerate(jobs):
                if i == 0 or jobs[i - 1].piece != j.piece:
                    pe.wait_ge(loaded[j.piece % nbuf], 16 * (j.piece // nbuf + 1))
                if i >= 8:
                    pe.wait_ge(done[jobs[i - 8].by], sum(q.by == jobs[i - 8].by for q in jobs[:i - 7]))
                for k in range(KD):
                    last = nc.tensor.matmul(ps[i % 8][:j.M, :j.N], j.lhsT(k), j.rhs(k),
                                            start=(k == 0), stop=(k == KD - 1))
                last.then_inc(summed, 1)

        @block.scalar
        def _(act):
            for i, j in enumerate(jobs):
                if j.by == "act":
                    act.wait_ge(summed, i + 1)
                    j.copy(ps[i % 8][:j.M, :j.N]).then_inc(by_act, 1)

        @block.vector
        def _(dve):
            for i, j in enumerate(jobs):
                if j.by == "dve":
                    dve.wait_ge(summed, i + 1)
                    j.copy(ps[i % 8][:j.M, :j.N]).then_inc(by_dve, 1)


def finish_stage(nc, name, C, X, lng, lnb, proj=None, experts=None, xT=None, router=None, rows=None, out=None,
                 ahead=None):
    with Scope(nc, name) as s:
        gb = s.sb("gb", [128, 2, D])
        st, mv = s.sb("st", [128, 5, 2, 6]), s.sb("mv", [128, 5, 2])
        rstd, nmr = s.sb("rstd", [128, 5]), s.sb("nmr", [128, 5])
        if proj:
            mixT, w_dram = proj
            w = ahead.w_out
            pp = [s.ps(f"p{i}") for i in range(4)]
        else:
            y_dram, E = experts
            y = [w[:, 0:2 * D].rearrange("p (k n) -> p k n", k=2) for w in E.wg[0:5]]
            tmp = E.wg[5][:, 0:D]
        if xT is not None:
            pt = [s.ps(f"t{i}") for i in range(2)]
        if router:
            wr, br, lg = router
            pl = [s.ps(f"l{i}") for i in range(2)]
        (gb_in, summed, added, dv, var_in, root, mean_in, normed, final, T_in, T_out, logits, logit_c) = (
            s.sem(x) for x in ("gb_in", "summed", "added", "dve_steps", "var_in", "root", "mean_in", "normed",
                               "final", "T_in", "T_out", "logits", "logits_copied"))
        w_in = [s.sem(f"w_in{h}") for h in range(2)] if proj else None
        y_in = [s.sem(f"y_in{i}") for i in range(5)] if experts else None
        stored = s.sem("stored") if out else s.sem("rows_stored")
        block = s.block()

        @block.sync
        def _(sp):
            if proj:
                for h in range(2):
                    sp.dma_start(w[h][:, :, :], w_dram.rearrange("(k p) n -> p k n", p=128)[:, :, 512 * h:512 * h + 512])\
                      .then_inc(w_in[h], 16)
            sp.dma_start(gb[:, 0, :], lng.partition_broadcast(128)).then_inc(gb_in, 16)
            sp.dma_start(gb[:, 1, :], lnb.partition_broadcast(128)).then_inc(gb_in, 16)
            if ahead:
                ahead.fill(sp, range(ahead.RING - 1))
            for t, P in TILES:
                if ahead and t == 3:
                    sp.wait_ge(summed, 5)
                    ahead.fill(sp, range(ahead.RING - 1, ahead.RING))
                if rows is not None:
                    sp.wait_ge(final, t + 1)
                    sp.dma_start(rows[tok0(t):tok0(t) + P, :], X[:P, t, :]).then_inc(stored, 16)
                elif out:
                    sp.wait_ge(final, t + 1)
                    dst = out[0][0, tok0(t):tok0(t) + P, :] if t < 4 else out[1].rearrange("b s d -> (b s) d")
                    sp.dma_start(dst, X[:P, t, :]).then_inc(stored, 16)
            if rows is not None or out:
                sp.wait_ge(stored, 16 * 5)

        if experts:
            @block.gpsimd
            def _(pool):
                for t, P in TILES:
                    for k in range(2):
                        nc.gpsimd.indirect_dma_start(out=y[t][:P, k, :], out_offset=None, in_=y_dram,
                                                     in_offset=bass.IndirectOffsetOnAxis(ap=E.posi[:P, k, t:t + 1], axis=0))\
                            .then_inc(y_in[t], 16)

        if proj or xT is not None:
            @block.tensor
            def _(pe):
                def project(t, P):
                    if t >= 2:
                        pe.wait_ge(added, t - 1)
                    for h in range(2):
                        if t == 0:
                            pe.wait_ge(w_in[h], 16)
                        for k in range(KD):
                            last = nc.tensor.matmul(pp[2 * (t % 2) + h][:P, :], mixT[:, k, tok0(t):tok0(t) + P],
                                                    w[h][:, k, :], start=(k == 0), stop=(k == KD - 1))
                    last.then_inc(summed, 1)

                def flip(t, P):
                    pe.wait_ge(final, t + 1)
                    if t >= 1:
                        pe.wait_ge(T_out, t)
                    for c in range(KD):
                        last = nc.tensor.transpose(pt[c // 4][:, (c % 4) * P:(c % 4 + 1) * P],
                                                   X[:P, t, c * 128:(c + 1) * 128], C("ident")[:P, :P])
                    last.then_inc(T_in, 1)

                def route(t, P):
                    pe.wait_ge(T_out, t + 1)
                    if t >= 2:
                        pe.wait_ge(logit_c, t - 1)
                    for k in range(KD):
                        last = nc.tensor.matmul(pl[t % 2][:P, 0:36], xT[:, k, tok0(t):tok0(t) + P], wr[:, k, :],
                                                start=(k == 0), stop=(k == KD - 1))
                    last.then_inc(logits, 1)

                for i in range(7):
                    if proj and i < 5:
                        project(*TILES[i])
                    if xT is not None and 1 <= i <= 5:
                        flip(*TILES[i - 1])
                    if router and i >= 2:
                        route(*TILES[i - 2])

        @block.vector
        def _(dve):
            c, V = Count(dve, dv), nc.vector

            def add(t, P):
                x = X[:P, t, :]
                if proj:
                    dve.wait_ge(summed, t + 1)
                    for h in range(2):
                        last = V.scalar_tensor_tensor(out=x[:, 512 * h:512 * h + 512], in0=x[:, 512 * h:512 * h + 512],
                                                      scalar=ALPHA, in1=pp[2 * (t % 2) + h][:P, :],
                                                      op0=ALU.mult, op1=ALU.add)
                else:
                    dve.wait_ge(y_in[t], 32)
                    c.step(V.tensor_scalar(tmp[:P, :], y[t][:P, 0, :], E.gate[:P, 0, t:t + 1], None, ALU.mult))
                    c.step(V.scalar_tensor_tensor(out=tmp[:P, :], in0=y[t][:P, 1, :], scalar=E.gate[:P, 1, t:t + 1],
                                                  in1=tmp[:P, :], op0=ALU.mult, op1=ALU.add))
                    last = V.scalar_tensor_tensor(out=x, in0=x, scalar=ALPHA, in1=tmp[:P, :], op0=ALU.mult, op1=ALU.add)
                last.then_inc(added, 1)
                dve.wait_ge(added, t + 1)
                for h in range(2):
                    c.add(V.bn_stats(st[:P, t, h, :], x[:, h * 512:(h + 1) * 512]))
                c.wait()
                c.step(V.bn_aggr(mv[:P, t, :], st[:P, t, :, :].rearrange("p a b -> p (a b)")))
                V.tensor_scalar(rstd[:P, t:t + 1], mv[:P, t, 1:2], LN_EPS, None, ALU.add).then_inc(var_in, 1)

            def scale(t, P):
                dve.wait_ge(root, t + 1)
                c.step(V.reciprocal(rstd[:P, t:t + 1], rstd[:P, t:t + 1]))
                V.tensor_scalar(nmr[:P, t:t + 1], mv[:P, t, 0:1], rstd[:P, t:t + 1], -1.0, ALU.mult, ALU.mult)\
                 .then_inc(mean_in, 1)

            def affine(t, P):
                dve.wait_ge(normed, t + 1)
                if t == 0:
                    dve.wait_ge(gb_in, 32)
                c.step(V.tensor_tensor(X[:P, t, :], X[:P, t, :], gb[:P, 0, :], ALU.mult))
                V.tensor_tensor(X[:P, t, :], X[:P, t, :], gb[:P, 1, :], ALU.add).then_inc(final, 1)

            def logit(t, P):
                dve.wait_ge(logits, t + 1)
                V.tensor_tensor(lg[:P, t, :], pl[t % 2][:P, 0:36], br[:P, :], ALU.add).then_inc(logit_c, 1)

            if router:
                c.step(V.memset(lg[:, :, :], 0.0))
            for i in range(6):
                if i < 5:
                    add(*TILES[i])
                if i >= 1:
                    affine(*TILES[i - 1])
                if i < 5:
                    scale(*TILES[i])
                if router and i >= 2:
                    logit(*TILES[i - 2])
            if router:
                logit(*TILES[4])

        @block.scalar
        def _(act):
            for i in range(6):
                if i < 5:
                    t, P = TILES[i]
                    act.wait_ge(var_in, t + 1)
                    nc.scalar.activation(rstd[:P, t:t + 1], rstd[:P, t:t + 1], ACT.Sqrt).then_inc(root, 1)
                    act.wait_ge(mean_in, t + 1)
                    nc.scalar.activation(X[:P, t, :], X[:P, t, :], ACT.Identity, bias=nmr[:P, t:t + 1],
                                         scale=rstd[:P, t:t + 1]).then_inc(normed, 1)
                if xT is not None and i >= 1:
                    t, P = TILES[i - 1]
                    act.wait_ge(T_in, t + 1)
                    for h in range(2):
                        last = nc.scalar.activation(xT[:, 4 * h:4 * h + 4, tok0(t):tok0(t) + P],
                                                    pt[h][:, :4 * P].rearrange("p (c n) -> p c n", c=4), ACT.Copy)
                    last.then_inc(T_out, 1)




def mixer_ab(nc, A, C, xT, yo, cleared):
    with Scope(nc, "ab") as L:
        v = L.sb("v", [128, 5, 512])
        rs = L.sb("rs", [128, 5, 512])
        zs = L.sb("zs", [128, 5, 512])
        qT = L.sb("qT", [128, 2, NTOK])
        kT = L.sb("kT", [128, 2, NTOK])
        soft = L.sb("soft", [128, 5, 264])
        xbcC = L.sb("xbcC", [128, 6, NTOK])
        las = L.sb("las", [128, 5, 8])
        lam = L.sb("lam", [128, 4, 2, 8])
        lams = L.sb("lams", [32, NB, 8])
        heads = L.sb("heads", [128, 16])
        norms = L.sb("norms", [128, 640])

        with Scope(nc, "abw") as W:
            xbcP = W.sb("xbcP", [128, 6, 3 + SEQ])
            xbcS = W.sb("xbcS", [128, 6, NB, 3 + NS])
            gT = W.sb("gT", [16, NTOK])
            pieces = [(0, 512), (512, 1024), (1024, 1536), (1536, 2064), (2064, 2448), (2448, 2840)]

            def jobs_of(n, w):
                out = []

                def feat(c0, M, prompt, sample, scale=1.0):
                    out.append(Job(n, M, 512, lambda k: w[:, k, c0:c0 + M], lambda k: xT[:, k, 0:512], "act",
                                   lambda p: nc.scalar.activation(prompt, p, ACT.Copy, scale=scale)))
                    out.append(Job(n, M, 32, lambda k: w[:, k, c0:c0 + M], lambda k: xT[:, k, 512:544], "dve",
                                   lambda p: nc.vector.tensor_scalar(
                                       sample, p.rearrange("p (b s) -> p b s", s=NS) if len(sample.shape) == 3 else p,
                                       scale, None, ALU.mult)))

                def tok(c0, N, dst, func=None):
                    for t, P in TILES:
                        def copy(p, t=t, P=P):
                            if func is None:
                                return nc.vector.tensor_copy(dst[:P, t, :], p)
                            return nc.scalar.activation(dst[:P, t, :], p, func)
                        out.append(Job(n, P, N, lambda k, t=t, P=P: xT[:, k, tok0(t):tok0(t) + P],
                                       lambda k: w[:, k, c0:c0 + N], "dve" if func is None else "act", copy))

                if n == 0:
                    for f in range(2):
                        feat(f * 128, 128, qT[:, f, 0:512], qT[:, f, 512:544], 64 ** -0.5)
                        feat(256 + f * 128, 128, kT[:, f, 0:512], kT[:, f, 512:544])
                elif n == 1:
                    tok(0, 512, v)
                elif n == 2:
                    tok(0, 512, rs, ACT.Silu)
                elif n == 3:
                    feat(0, 16, gT[:, 0:512], gT[:, 512:544])
                    tok(16, 512, zs, ACT.Silu)
                else:
                    for f in range(3):
                        ff = 3 * (n - 4) + f
                        feat(f * 128, 128, xbcP[:, ff, 3:515], xbcS[:, ff, :, 3:7])
                    if n == 5:
                        tok(384, 8, soft[:, :, 256:264])
                return out

            project_stage(nc, "abi", A["ab_w_in"], pieces, 528, xT, jobs_of)

            with Scope(nc, "abg") as s:
                convst = s.sb("convst", [NB * 3, 768])
                wg2 = s.sb("wg2", [16, 256])
                bg = s.sb("bg", [128, 264])
                cwr = s.sb("cwr", [5, 768])
                cw = s.sb("cw", [128, 6, 5])
                nc_conv = s.sb("newconv", [128, 6, 3 + NB * 3])
                tmp = s.sb("tmp", [128, 5, 264])
                pg = [s.ps(f"pg{i}") for i in range(5)]
                pc = s.ps("pc")
                pn = [s.ps(f"pn{i}") for i in range(2)]
                names = ("loaded", "zeroed", "gate_sum", "states_T", "dve_steps", "ext_ready", "conv_ready",
                         "logit_ready", "act_steps", "log_ready", "newst_T", "newst_ready", "stored", "silu_done")
                (loaded, zeroed, gate_sum, states_T, dv, ext_ready, conv_ready, logit_ready, ac, log_ready, newst_T,
                 newst_ready, stored, silu_done) = (s.sem(x) for x in names)
                newst = s.sb("newst", [32, 2, 768])
                block = s.block()

                @block.sync
                def _(sp):
                    sp.dma_start(convst[:, :], A["state_conv"].rearrange("b i n -> (b i) n")).then_inc(loaded, 16)
                    sp.dma_start(wg2[:, :], A["ab_w_gate2"]).then_inc(loaded, 16)
                    sp.dma_start(bg[:, 0:256], A["ab_b_gate"].partition_broadcast(128)).then_inc(loaded, 16)
                    sp.dma_start(bg[:, 256:264], A["ab_dt_bias"].partition_broadcast(128)).then_inc(loaded, 16)
                    sp.dma_start(cwr[0:4, :], A["ab_conv_w"]).then_inc(loaded, 16)
                    sp.dma_start(cwr[4:5, :], A["ab_conv_b"].rearrange("(a n) -> a n", a=1)).then_inc(loaded, 16)
                    sp.dma_start(heads[:, 0:8], A["ab_a_log"].partition_broadcast(128)).then_inc(loaded, 16)
                    sp.dma_start(heads[:, 8:16], A["ab_d_skip"].partition_broadcast(128)).then_inc(loaded, 16)
                    sp.dma_start(norms[:, 0:128], A["ab_gla_norm"].partition_broadcast(128)).then_inc(loaded, 16)
                    sp.dma_start(norms[:, 128:640], A["ab_ssm_norm"].partition_broadcast(128)).then_inc(loaded, 16)
                    sp.wait_ge(newst_ready, 2)
                    sp.dma_start(A["conv_p"][0, :, :], newst[0:3, 0, :]).then_inc(stored, 16)
                    sp.dma_start(A["conv_s"].rearrange("b i n -> (b i) n"), newst[0:24, 1, :]).then_inc(stored, 16)
                    sp.wait_ge(stored, 32)

                @block.tensor
                def _(pe):
                    pe.wait_ge(loaded, 16 * 10)
                    for f in range(6):
                        nc.tensor.transpose(pc[:, f * 24:(f + 1) * 24], convst[:, f * 128:(f + 1) * 128],
                                            C("ident")[:24, :24])
                        last = nc.tensor.transpose(pc[:, 144 + f * 5:149 + f * 5], cwr[:, f * 128:(f + 1) * 128],
                                                   C("ident")[:5, :5])
                    last.then_inc(states_T, 1)
                    for t, P in TILES:
                        nc.tensor.matmul(pg[t][:P, 0:256], gT[:, tok0(t):tok0(t) + P], wg2[:, :],
                                         start=True, stop=True).then_inc(gate_sum, 1)
                    pe.wait_ge(ext_ready, 2)
                    for h in range(2):
                        for f in range(3):
                            last = nc.tensor.transpose(pn[h][0:3, f * 128:(f + 1) * 128],
                                                       nc_conv[:, 3 * h + f, 0:3], C("ident"))
                    last.then_inc(newst_T, 1)
                    pe.wait_ge(newst_ready, 1)
                    for h in range(2):
                        for f in range(3):
                            last = nc.tensor.transpose(pn[h][0:24, f * 128:(f + 1) * 128],
                                                       nc_conv[:, 3 * h + f, 3:27], C("ident"))
                    last.then_inc(newst_T, 1)

                @block.vector
                def _(dve):
                    c = Count(dve, dv)
                    c.step(nc.vector.memset(tmp[:, 4, :], 0.0))
                    c.add(nc.vector.tensor_copy(tmp[:, 0:4, 256:264], soft[:, 0:4, 256:264]))
                    c.add(nc.vector.tensor_copy(tmp[0:32, 4, 256:264], soft[0:32, 4, 256:264]))
                    c.step(nc.vector.memset(xbcP[:, :, 0:3], 0.0))
                    dve.wait_ge(states_T, 1)
                    c.add(nc.vector.tensor_copy(cw[:, :, :], pc[:, 144:174].rearrange("p (f i) -> p f i", f=6)))
                    c.step(nc.vector.tensor_copy(xbcS[:, :, :, 0:3],
                                                 pc[:, 0:144].rearrange("p (f b i) -> p f b i", f=6, b=NB)))
                    nc.vector.tensor_copy(nc_conv[:, :, 0:3], xbcP[:, :, 512:515]).then_inc(ext_ready, 1)
                    nc.vector.tensor_copy(nc_conv[:, :, 3:27].rearrange("p f (b i) -> p f b i", b=NB),
                                          xbcS[:, :, :, 4:7]).then_inc(ext_ready, 1)
                    dve.wait_ge(gate_sum, 5)
                    for t, P in TILES:
                        c.add(nc.vector.tensor_copy(tmp[:P, t, 0:256], pg[t][:P, 0:256]))
                    c.wait()
                    dve.wait_ge(loaded, 16 * 10)
                    bias = bg[:, :].unsqueeze(1).to_broadcast([128, 5, 264])
                    c.step(nc.vector.tensor_tensor(tmp[:, :, :], tmp[:, :, :], bias, ALU.add))
                    nc.vector.tensor_scalar(tmp[:, :, 0:256], tmp[:, :, 0:256], -1.0, None, ALU.mult).then_inc(logit_ready, 1)
                    for f in range(6):
                        outs = [(xbcC[:, f, 0:512], lambda i: xbcP[:, f, i:i + 512]),
                                (xbcC[:, f, 512:544].rearrange("p (b s) -> p b s", s=NS), lambda i: xbcS[:, f, :, i:i + NS])]
                        for o, src in outs:
                            c.add(nc.vector.tensor_scalar(o, src(0), cw[:, f, 0:1], cw[:, f, 4:5],
                                                          ALU.mult, ALU.add))
                    for i in range(1, 4):
                        for f in range(6):
                            outs = [(xbcC[:, f, 0:512], xbcP[:, f, i:i + 512]),
                                    (xbcC[:, f, 512:544].rearrange("p (b s) -> p b s", s=NS), xbcS[:, f, :, i:i + NS])]
                            for o, src in outs:
                                dve.wait_ge(dv, c.n - 11)
                                last = nc.vector.scalar_tensor_tensor(out=o, in0=src, scalar=cw[:, f, i:i + 1], in1=o,
                                                                      op0=ALU.mult, op1=ALU.add)
                                if (i, f) != (3, 5) or o is outs[0][0]:
                                    c.add(last)
                    last.then_inc(conv_ready, 1)
                    dve.wait_ge(newst_T, 1)
                    for h in range(2):
                        last = nc.vector.tensor_copy(newst[0:3, 0, h * 384:(h + 1) * 384], pn[h][0:3, 0:384])
                    last.then_inc(newst_ready, 1)
                    dve.wait_ge(log_ready, 1)
                    c.step(nc.vector.scalar_tensor_tensor(out=soft[:, :, :], in0=tmp[:, :, :], scalar=0.0,
                                                          in1=soft[:, :, :], op0=ALU.max, op1=ALU.add))
                    c.step(nc.vector.tensor_scalar(soft[:, :, 0:256], soft[:, :, 0:256], -1.0 / 16, None, ALU.mult))
                    c.step(nc.vector.tensor_tensor(las[:, :, :], soft[:, :, 256:264],
                                                   heads[:, 0:8].unsqueeze(1).to_broadcast([128, 5, 8]), ALU.mult))
                    c.step(nc.vector.tensor_scalar(las[:, :, :], las[:, :, :], -1.0, None, ALU.mult))
                    for cc in range(2):
                        c.add(nc.vector.tensor_scalar(lam[:, :, cc, :], las[:, 0:4, :], C("cmask")[:, cc:cc + 1], None,
                                                      ALU.mult))
                    for b in range(NB):
                        c.add(nc.vector.tensor_scalar(lams[:, b, :], las[0:32, 4, :], C("bmask")[0:32, b:b + 1], None,
                                                      ALU.mult))
                    dve.wait_ge(newst_T, 2)
                    for h in range(2):
                        last = nc.vector.tensor_copy(newst[0:24, 1, h * 384:(h + 1) * 384], pn[h][0:24, 0:384])
                    last.then_inc(newst_ready, 1)

                @block.scalar
                def _(act):
                    c = Count(act, ac)
                    act.wait_ge(loaded, 16 * 10)
                    c.add(nc.scalar.activation(heads[:, 0:8], heads[:, 0:8], ACT.Exp))
                    act.wait_ge(logit_ready, 1)
                    c.step(nc.scalar.activation(soft[:, :, :], tmp[:, :, :], ACT.Abs))
                    c.step(nc.scalar.activation(soft[:, :, :], soft[:, :, :], ACT.Exp, scale=-1.0))
                    nc.scalar.activation(soft[:, :, :], soft[:, :, :], ACT.Ln, bias=1.0).then_inc(log_ready, 1)
                    act.wait_ge(conv_ready, 1)
                    nc.scalar.activation(xbcC[:, :, :], xbcC[:, :, :], ACT.Silu).then_inc(silu_done, 1)

        with Scope(nc, "abz") as L2:
            scan_ab(nc, A, C, L2, xT, yo, cleared, v, rs, zs, qT, kT, soft, xbcC, las, lam, lams, heads, norms)


def scan_ab(nc, A, C, L, xT, yo, cleared, v, rs, zs, qT, kT, soft, xbcC, las, lam, lams, heads, norms):
    eb = L.sb("eb", [128, 2, NTOK])
    kend = L.sb("kend", [128, 5, 256])
    xs = L.sb("xs", [128, 5, 512])
    btok = L.sb("btok", [128, 5, 128])
    xdd = L.sb("xdd", [128, 5, 512])
    ecum = L.sb("ecum", [128, 5, 16])
    elh = L.sb("elh", [128, 16, 4])
    ycs = L.sb("ycs", [128, 5, 512])
    BT, CT = xbcC[:, 4, :], xbcC[:, 5, :]

    with Scope(nc, "abs") as s:
        enb = s.sb("enb", [128, 2, 128])
        qd, kd = qT, kT
        ncum = s.sb("ncum", [128, 8])
        esuf = s.sb("esuf", [128, 256])
        el = s.sb("el", [128, 64])
        xdt = s.sb("xdt", [128, 512])
        W = s.sb("W", [128, 8, 128])
        At = s.sb("At", [128, 4, 128])
        pa, pb, px, pB, pr0, pr1, po, py = (s.ps(x) for x in ("pa", "pb", "px", "pB", "pr0", "pr1", "po", "py"))
        (summed, dv, ac, exps, cneg, wexp, ready, att, masked, outs, copied, zero) = (s.sem(x) for x in (
            "summed", "dve_steps", "act_steps", "exps", "cneg", "wexp", "ready", "att", "masked", "outs",
            "copied", "zeroed"))
        block = s.block()

        @block.tensor
        def _(pe):
            for t, P in TILES:
                m = "p" if t < 4 else "s"
                tri, suf, neg = C("tri_" + m)[:P, :P], C("suf_" + m)[:P, :P], C("neg_" + m)[:P, :P]
                tk = slice(tok0(t), tok0(t) + P)
                if t:
                    pe.wait_ge(ready, t)
                    pe.wait_ge(copied, t)
                for f in range(2):
                    nc.tensor.matmul(pa[:, f * 128:f * 128 + P], soft[:P, t, f * 128:(f + 1) * 128], tri,
                                     start=True, stop=True)
                nc.tensor.matmul(pa[:P, 256:512], suf, soft[:P, t, 0:256], start=True, stop=True)
                nc.tensor.matmul(pb[:P, 0:8], tri, las[:P, t, :], start=True, stop=True)
                nc.tensor.matmul(pb[:P, 8:16], suf, las[:P, t, :], start=True, stop=True)
                n = 16 if t < 4 else 64
                rhs = (lam[:, t, :, :] if t < 4 else lams[:, :, :]).rearrange("p c h -> p (c h)")
                nc.tensor.matmul(pb[:, 16:16 + n], C("ones")[:P, :], rhs, start=True, stop=True)
                for f in range(2):
                    nc.tensor.transpose(pb[:P, 256 + f * 128:256 + (f + 1) * 128], kT[:, f, tk], C("ident"))
                for f in range(4):
                    nc.tensor.transpose(px[:P, f * 128:(f + 1) * 128], xbcC[:, f, tk], C("ident"))
                nc.tensor.transpose(pB[:P, 256:384], BT[:, tk], C("ident"))
                for g in range(2):
                    nc.tensor.matmul((pB, po)[g][:P, 0:P], BT[64 * g:64 * g + 64, tk],
                                     CT[64 * g:64 * g + 64, tk], start=True, stop=True)
                for h in range(8):
                    pr = (pr0, pr1)[h // 4][:P, (h % 4) * 128:(h % 4) * 128 + P]
                    nc.tensor.matmul(pr, las[:P, t, h:h + 1].to_broadcast([P, P]), tri, start=True, stop=False)
                    last = nc.tensor.matmul(pr, C("ident")[:P, :P], neg, start=False, stop=True)
                last.then_inc(summed, 1)
                pe.wait_ge(ready, t + 1)
                for h in range(4):
                    r = slice(64 * (h % 2), 64 * (h % 2) + 64)
                    last = nc.tensor.matmul((pr0, pr1)[h % 2][:P, (h // 2) * 128:(h // 2) * 128 + P],
                                            kd[r, h // 2, tk], qd[r, h // 2, tk],
                                            start=True, stop=True)
                last.then_inc(att, 1)
                pe.wait_ge(masked, t + 1)
                for h in range(4):
                    last = nc.tensor.matmul(po[:P, h * 128:(h + 1) * 128], At[:P, h, :P], v[:P, t, h * 128:(h + 1) * 128],
                                            start=True, stop=True)
                for h in range(8):
                    last = nc.tensor.matmul(py[:P, h * 64:(h + 1) * 64], W[:P, h, :P], xdt[:P, h * 64:(h + 1) * 64],
                                            start=True, stop=True)
                last.then_inc(outs, 1)

        @block.scalar
        def _(act):
            for t, P in TILES:
                tk = slice(tok0(t), tok0(t) + P)
                if t:
                    act.wait_ge(masked, t)
                    act.wait_ge(outs, t)
                act.wait_ge(summed, t + 1)
                b = pa[:, 0:256].rearrange("p (f n) -> p f n", f=2)[:, :, :P]
                nc.scalar.activation(eb[:, :, tk], b, ACT.Exp)
                nc.scalar.activation(enb[:, :, :P], b, ACT.Exp, scale=-1.0)
                nc.scalar.activation(esuf[:P, :], pa[:P, 256:512], ACT.Exp)
                nc.scalar.activation(ecum[:P, t, :], pb[:P, 0:16], ACT.Exp)
                n = 16 if t < 4 else 64
                nc.scalar.activation(el[:, 0:n], pb[:, 16:16 + n], ACT.Exp).then_inc(exps, 1)
                act.wait_ge(cneg, t + 1)
                for h in range(8):
                    last = nc.scalar.activation(W[:P, h, :P], (pr0, pr1)[h // 4][:P, (h % 4) * 128:(h % 4) * 128 + P],
                                                ACT.Exp, bias=ncum[:P, h:h + 1])
                last.then_inc(wexp, 1)

        @block.vector
        def _(dve):
            c = Count(dve, dv)
            dve.wait_ge(cleared, 16 * (NROW - NE * SLOT) // 128)
            c.add(nc.vector.memset(yo[:, 4, :], 0.0))
            c.step(nc.vector.memset(ycs[:, 4, :], 0.0))
            c.add(nc.vector.memset(xs[:, 4, :], 0.0))
            c.step(nc.vector.memset(ecum[:, 4, :], 0.0))
            for t, P in TILES:
                tk = slice(tok0(t), tok0(t) + P)
                dve.wait_ge(summed, t + 1)
                c.add(nc.vector.tensor_copy(xs[:P, t, :], px[:P, :]))
                c.add(nc.vector.tensor_copy(btok[:P, t, :], pB[:P, 256:384]))
                c.wait()
                dt = soft[:P, t, 256:264].unsqueeze(2).to_broadcast([P, 8, 64])
                c.step(nc.vector.tensor_tensor(xdt[:P, :].rearrange("p (h d) -> p h d", h=8),
                                               xs[:P, t, :].rearrange("p (h d) -> p h d", h=8), dt, ALU.mult))
                dve.wait_ge(exps, t + 1)
                nc.vector.tensor_scalar(ncum[:P, :], pb[:P, 0:8], -1.0, None, ALU.mult).then_inc(cneg, 1)
                c.add(nc.vector.tensor_tensor(qd[:, :, tk], qT[:, :, tk], eb[:, :, tk], ALU.mult))
                c.add(nc.vector.tensor_tensor(kd[:, :, tk], kT[:, :, tk], enb[:, :, :P], ALU.mult))
                c.add(nc.vector.tensor_tensor(kend[:P, t, :], pb[:P, 256:512], esuf[:P, :], ALU.mult))
                c.add(nc.vector.tensor_tensor(xdd[:P, t, :].rearrange("p (h d) -> p h d", h=8),
                                              xdt[:P, :].rearrange("p (h d) -> p h d", h=8),
                                              ecum[:P, t, 8:16].unsqueeze(2).to_broadcast([P, 8, 64]), ALU.mult))
                for g in range(2):
                    n, at = (2, 2 * t) if t < 4 else (8, 8)
                    c.add(nc.vector.tensor_copy(elh[64 * g:64 * g + 64, at:at + n, :],
                                                el[64 * g:64 * g + 64, 0:8 * n]
                                                .rearrange("p (c h) -> p c h", h=8)[:, :, 4 * g:4 * g + 4]))
                dve.wait_ge(wexp, t + 1)
                for g in range(2):
                    last = nc.vector.tensor_tensor(W[:P, 4 * g:4 * g + 4, :P], W[:P, 4 * g:4 * g + 4, :P],
                                                   (pB, po)[g][:P, 0:P].unsqueeze(1).to_broadcast([P, 4, P]),
                                                   ALU.mult)
                last.then_inc(ready, 1)
                dve.wait_ge(att, t + 1)
                m = C("tri_p" if t < 4 else "tri_s")[:P, :P].unsqueeze(1).to_broadcast([P, 2, P])
                for hh in range(2):
                    last = nc.vector.tensor_tensor(At[:P, :, :P].rearrange("p (f h) n -> p h f n", h=2)[:, hh, :, :],
                                                   (pr0, pr1)[hh][:P, 0:256].rearrange("p (h n) -> p h n", h=2)[:, :, :P],
                                                   m, ALU.mult)
                last.then_inc(masked, 1)
                dve.wait_ge(outs, t + 1)
                c.add(nc.vector.tensor_copy(yo[:P, t, 0:512], po[:P, :]))
                nc.vector.tensor_copy(yo[:P, t, 512:1024], py[:P, :]).then_inc(copied, 1)

    qd = qT
    with Scope(nc, "abc") as s:
        Sg = s.sb("Sg", [128, 9, 256])
        Ss = s.sb("Ss", [128, 9, 256])
        stT = s.sb("stT", [128, 2, 128])
        pu = [s.ps(f"pu{i}") for i in range(4)]
        po = [s.ps(f"po{i}") for i in range(4)]
        upd, dv, states, inter, added, T_ready, T_done, stored = (s.sem(x) for x in (
            "upd", "dve_steps", "states", "inter", "added", "T_ready", "T_done", "stored"))
        block = s.block()

        @block.tensor
        def _(pe):
            for ch in range(8):
                t, r = ch // 2, slice(64 * (ch % 2), 64 * (ch % 2) + 64)
                if ch >= 4:
                    pe.wait_ge(states, ch - 3)
                for h in range(4):
                    nc.tensor.matmul(pu[ch % 4][64 * (h % 2):64 * (h % 2) + 64, (h // 2) * 128:(h // 2) * 128 + 128],
                                     kend[r, t, h * 64:(h + 1) * 64], v[r, t, h * 128:(h + 1) * 128],
                                     start=True, stop=True)
                for g in range(2):
                    last = nc.tensor.matmul(pu[ch % 4][64 * g:64 * g + 64, 256:512], btok[r, t, g * 64:(g + 1) * 64],
                                            xdd[r, t, g * 256:(g + 1) * 256], start=True, stop=True)
                last.then_inc(upd, 1)
            for t in range(4):
                pe.wait_ge(states, 2 * t + 1)
                if t >= 1:
                    pe.wait_ge(added, 2 * t)
                for ch in (2 * t, 2 * t + 1):
                    o = slice(64 * (ch % 2), 64 * (ch % 2) + 64)
                    tk = slice(64 * ch, 64 * ch + 64)
                    for h in range(4):
                        r = slice(64 * (h % 2), 64 * (h % 2) + 64)
                        nc.tensor.matmul(po[h % 2][o, (h // 2) * 128:(h // 2 + 1) * 128], qd[r, h // 2, tk],
                                         Sg[r, ch, (h // 2) * 128:(h // 2) * 128 + 128], start=True, stop=True)
                    for g in range(2):
                        r = slice(64 * g, 64 * g + 64)
                        last = nc.tensor.matmul(po[2 + g][o, 0:256], CT[r, tk], Ss[r, ch, :],
                                                start=True, stop=True)
                last.then_inc(inter, 1)
            pe.wait_ge(states, 8)
            for u in range(2):
                last = nc.tensor.transpose(pu[0][:, u * 128:(u + 1) * 128], Ss[:, 8, u * 128:(u + 1) * 128], C("ident"))
            last.then_inc(T_ready, 1)

        @block.vector
        def _(dve):
            c = Count(dve, dv)
            c.add(nc.vector.memset(Sg[:, 0, :], 0.0))
            c.step(nc.vector.memset(Ss[:, 0, :], 0.0))
            for ch in range(8):
                dve.wait_ge(upd, ch + 1)
                c.step(nc.vector.tensor_tensor(Ss[:, ch + 1, :].rearrange("p (h d) -> p h d", h=4),
                                               Ss[:, ch, :].rearrange("p (h d) -> p h d", h=4),
                                               elh[:, ch, :].unsqueeze(2).to_broadcast([128, 4, 64]), ALU.mult))
                c.add(nc.vector.tensor_tensor(Ss[:, ch + 1, :], Ss[:, ch + 1, :], pu[ch % 4][:, 256:512], ALU.add))
                for f in range(2):
                    col = slice(f * 128, f * 128 + 128)
                    last = nc.vector.scalar_tensor_tensor(out=Sg[:, ch + 1, col], in0=Sg[:, ch, col],
                                                          scalar=eb[:, f, 64 * ch + 63:64 * ch + 64],
                                                          in1=pu[ch % 4][:, col], op0=ALU.mult, op1=ALU.add)
                last.then_inc(states, 1)
                dve.wait_ge(states, ch + 1)
            for t in range(4):
                dve.wait_ge(inter, t + 1)
                for hh in range(2):
                    o3 = yo[:, t, 0:512].rearrange("p (f h d) -> p h f d", f=2, h=2)[:, hh, :, :]
                    last = nc.vector.tensor_tensor(o3, o3, po[hh][:, 0:256].rearrange("p (f d) -> p f d", f=2), ALU.add)
                last.then_inc(added, 1)
                for g in range(2):
                    last = nc.vector.tensor_copy(ycs[:, t, 256 * g:256 * g + 256], po[2 + g][:, 0:256])
                last.then_inc(added, 1)
            dve.wait_ge(T_ready, 1)
            nc.vector.tensor_copy(stT[:, :, :], pu[0][:, 0:256].rearrange("p (u n) -> p u n", u=2)).then_inc(T_done, 1)

        @block.sync
        def _(sp):
            sp.wait_ge(states, 8)
            for f in range(2):
                sp.dma_start(A["gla_p"][0, 2 * f:2 * f + 2, :, :].rearrange("h k v -> (h k) v"),
                             Sg[:, 8, f * 128:(f + 1) * 128]).then_inc(stored, 16)
            sp.wait_ge(T_done, 1)
            for g in range(2):
                for u in range(2):
                    h = 4 * g + 2 * u
                    sp.dma_start(A["ssm_p"][0, h:h + 2, :, :].rearrange("h p n -> (h p) n"),
                                 stT[:, u, 64 * g:64 * g + 64]).then_inc(stored, 16)
            sp.wait_ge(stored, 16 * 6)

    with Scope(nc, "abd") as s:
        G0 = s.sb("G0", [128, 2, NB, 128])
        S0 = s.sb("S0", [128, NB, 256])
        raw = s.sb("raw", [128, NB, 2, 128])
        vm = xT[0:32, :, 0:512]
        oTs = s.sb("oTs", [128, 4, 32])
        yTs = s.sb("yTs", [128, 4, 32])
        ps = [s.ps(f"p{i}") for i in range(8)]
        (ld_g, ld_s, tr, tr_out, vmask, inter, evac, back, added, upd, dv, new_g, new_s, xmask, trb, fin, stored,
         mm) = (s.sem(x) for x in (
             "ld_g", "ld_s", "tr", "tr_out", "vmask", "inter", "evac", "back", "added", "upd", "dve_steps", "new_g",
             "new_s", "xmask", "trb", "fin", "stored", "updated_s"))
        block = s.block()

        @block.sync
        def _(sp):
            for f in range(2):
                sp.dma_start(G0[:, f, :, :], A["state_gla"][:, 2 * f:2 * f + 2, :, :].rearrange("b h k v -> (h k) b v"))\
                  .then_inc(ld_g, 16)
            for g in range(2):
                for u in range(2):
                    h = 4 * g + 2 * u
                    sp.dma_start(raw[:, :, u, 64 * g:64 * g + 64],
                                 A["state_ssm"][:, h:h + 2, :, :].rearrange("b h p n -> (h p) b n")).then_inc(ld_s, 16)
            sp.wait_ge(new_g, 1)
            for f in range(2):
                sp.dma_start(A["gla_s"][:, 2 * f:2 * f + 2, :, :].rearrange("b h k v -> (h k) b v"), G0[:, f, :, :])\
                  .then_inc(stored, 16)
            sp.wait_ge(fin, 4)
            for g in range(2):
                for u in range(2):
                    h = 4 * g + 2 * u
                    sp.dma_start(A["ssm_s"][:, h:h + 2, :, :].rearrange("b h p n -> (h p) b n"),
                                 raw[:, :, u, 64 * g:64 * g + 64]).then_inc(stored, 16)
            sp.wait_ge(stored, 16 * 6)

        @block.tensor
        def _(pe):
            pe.wait_ge(ld_s, 64)
            for i in range(4):
                for b in (2 * i, 2 * i + 1):
                    for u in range(2):
                        last = nc.tensor.transpose(ps[i][:, (b % 2) * 256 + u * 128:(b % 2) * 256 + (u + 1) * 128],
                                                   raw[:, b, u, :], C("ident"))
                last.then_inc(tr, 1)
            pe.wait_ge(ld_g, 32)
            for h in range(4):
                r = slice(64 * (h % 2), 64 * (h % 2) + 64)
                for b in range(NB):
                    nc.tensor.matmul(ps[4 + h % 2][:, (h // 2) * 32 + 4 * b:(h // 2) * 32 + 4 * b + 4], G0[r, h // 2, b, :],
                                     qd[r, h // 2, 512 + 4 * b:516 + 4 * b], start=True, stop=True)
            pe.wait_ge(tr_out, 4)
            for j in range(4):
                r = slice(64 * (j // 2), 64 * (j // 2) + 64)
                for b in range(NB):
                    last = nc.tensor.matmul(ps[6 + j // 2][:, (j % 2) * 32 + 4 * b:(j % 2) * 32 + 4 * b + 4],
                                            S0[r, b, (j % 2) * 128:(j % 2) * 128 + 128],
                                            CT[r, 512 + 4 * b:516 + 4 * b], start=True, stop=True)
            last.then_inc(inter, 1)
            pe.wait_ge(evac, 1)
            for h in range(4):
                nc.tensor.matmul(ps[6][:32, h * 128:(h + 1) * 128], oTs[:, h, :], C("ident"), start=True, stop=True)
            for h in range(4):
                last = nc.tensor.matmul(ps[7][:32, h * 128:(h + 1) * 128], yTs[:, h, :], C("ident"),
                                        start=True, stop=True)
            last.then_inc(back, 1)
            pe.wait_ge(vmask, 1)
            for h in range(4):
                for q in range(2):
                    last = nc.tensor.matmul(ps[2 * (h // 2) + q][64 * (h % 2):64 * (h % 2) + 64, :],
                                            kend[:32, 4, h * 64:(h + 1) * 64],
                                            vm[:, 4 * q:4 * q + 4, h * 128:(h + 1) * 128], start=True, stop=True)
            last.then_inc(upd, 1)
            pe.wait_ge(xmask, 1)
            for g in range(2):
                for q in range(4):
                    last = nc.tensor.matmul(ps[4 + q][64 * g:64 * g + 64, :], btok[:32, 4, g * 64:(g + 1) * 64],
                                            vm[:, 2 * q:2 * q + 2, g * 256:(g + 1) * 256], start=True, stop=True)
            last.then_inc(mm, 1)
            pe.wait_ge(new_s, 1)
            for i in range(4):
                for b in (2 * i, 2 * i + 1):
                    for u in range(2):
                        last = nc.tensor.transpose(ps[i][:, (b % 2) * 256 + u * 128:(b % 2) * 256 + (u + 1) * 128],
                                                   S0[:, b, u * 128:(u + 1) * 128], C("ident"))
                last.then_inc(trb, 1)

        @block.vector
        def _(dve):
            c = Count(dve, dv)
            for b in range(NB):
                last = nc.vector.tensor_scalar(vm[:, b, :], v[:32, 4, :], C("bmask")[:32, b:b + 1], None, ALU.mult)
            last.then_inc(vmask, 1)
            for i in range(4):
                dve.wait_ge(tr, i + 1)
                nc.vector.tensor_copy(S0[:, 2 * i:2 * i + 2, :], ps[i][:, :].rearrange("p (b n) -> p b n", b=2))\
                  .then_inc(tr_out, 1)
            dve.wait_ge(inter, 1)
            for q in range(2):
                nc.vector.tensor_copy(oTs[:, :, :].rearrange("p (f h) n -> p h f n", h=2)[:, q, :, :],
                                      ps[4 + q][:, 0:64].rearrange("p (h n) -> p h n", h=2))
                last = nc.vector.tensor_copy(yTs[:, 2 * q:2 * q + 2, :], ps[6 + q][:, 0:64].rearrange("p (h n) -> p h n", h=2))
            last.then_inc(evac, 1)
            dve.wait_ge(back, 1)
            c.add(nc.vector.tensor_tensor(yo[:32, 4, 0:512], yo[:32, 4, 0:512], ps[6][:32, :], ALU.add))
            c.step(nc.vector.tensor_copy(ycs[:32, 4, :], ps[7][:32, :]))
            for f in range(2):
                ebl = eb[:, f, 512:544].rearrange("p (b s) -> p b s", s=NS)[:, :, NS - 1:NS].to_broadcast([128, NB, 128])
                c.add(nc.vector.tensor_tensor(G0[:, f, :, :], G0[:, f, :, :], ebl, ALU.mult))
            c.add(nc.vector.tensor_tensor(S0[:, :, :].rearrange("p b (h d) -> p (b h) d", h=4),
                                          S0[:, :, :].rearrange("p b (h d) -> p (b h) d", h=4),
                                          elh[:, 8:16, :].rearrange("p b h -> p (b h)").unsqueeze(2)
                                          .to_broadcast([128, 32, 64]), ALU.mult))
            c.wait()
            dve.wait_ge(upd, 1)
            for b in range(NB):
                last = nc.vector.tensor_scalar(vm[:, b, :], xdd[:32, 4, :], C("bmask")[:32, b:b + 1], None, ALU.mult)
            last.then_inc(xmask, 1)
            for f in range(2):
                for q in range(2):
                    rows = G0[:, f, 4 * q:4 * q + 4, :].rearrange("p b n -> p (b n)")
                    last = nc.vector.tensor_tensor(rows, rows, ps[2 * f + q][:, :], ALU.add)
            last.then_inc(new_g, 1)
            dve.wait_ge(mm, 1)
            for q in range(4):
                rows = S0[:, 2 * q:2 * q + 2, :].rearrange("p b n -> p (b n)")
                last = nc.vector.tensor_tensor(rows, rows, ps[4 + q][:, :], ALU.add)
            last.then_inc(new_s, 1)
            for i in range(4):
                dve.wait_ge(trb, i + 1)
                nc.vector.tensor_copy(raw[:, 2 * i:2 * i + 2, :, :].rearrange("p b u n -> p (b u n)"), ps[i][:, :])\
                  .then_inc(fin, 1)

    with Scope(nc, "abe") as s:
        sq = s.sb("sq", [128, 5, 512])
        ms = s.sb("ms", [128, 5, 5])
        dv, var_ready, root, vm2 = (s.sem(x) for x in ("dve_steps", "var_ready", "root", "y_ready"))
        block = s.block()

        @block.vector
        def _(dve):
            c = Count(dve, dv)
            V = nc.vector
            c.step(V.memset(ms[:, :, :], 1.0))
            for t, P in TILES:
                o, y = yo[:P, t, 0:512], yo[:P, t, 512:1024]
                y3 = y.rearrange("p (h d) -> p h d", h=8)
                yc = ycs[:P, t, :].rearrange("p (h d) -> p h d", h=8)
                xs3 = xs[:P, t, :].rearrange("p (h d) -> p h d", h=8)
                c.add(V.tensor_tensor(yc, yc, ecum[:P, t, 0:8].unsqueeze(2).to_broadcast([P, 8, 64]), ALU.mult))
                c.step(V.tensor_tensor(xs3, xs3, heads[:P, 8:16].unsqueeze(2).to_broadcast([P, 8, 64]), ALU.mult))
                c.step(V.tensor_tensor(y, y, ycs[:P, t, :], ALU.add))
                c.step(V.tensor_tensor(y, y, xs[:P, t, :], ALU.add))
                c.step(V.tensor_tensor(y, y, zs[:P, t, :], ALU.mult))
                c.step(V.tensor_tensor(sq[:P, t, :], y, y, ALU.mult))
                c.step(V.tensor_reduce(ms[:P, t, 4:5], sq[:P, t, :], AX.X, ALU.add))
                c.step(V.tensor_tensor(sq[:P, t, :], o, o, ALU.mult))
                c.step(V.tensor_reduce(ms[:P, t, 0:4], sq[:P, t, :].rearrange("p (h d) -> p h d", h=4), AX.X, ALU.add))
            c.add(V.tensor_scalar(ms[:, :, 0:4], ms[:, :, 0:4], 1.0 / 128, RMS_EPS, ALU.mult, ALU.add))
            V.tensor_scalar(ms[:, :, 4:5], ms[:, :, 4:5], 1.0 / 512, RMS_EPS, ALU.mult, ALU.add).then_inc(var_ready, 1)
            dve.wait_ge(root, 1)
            c.step(V.reciprocal(ms[:, :, :], ms[:, :, :]))
            for t, P in TILES:
                o, y = yo[:P, t, 0:512], yo[:P, t, 512:1024]
                o3 = o.rearrange("p (h d) -> p h d", h=4)
                c.add(V.scalar_tensor_tensor(out=y, in0=y, scalar=ms[:P, t, 4:5], in1=norms[:P, 128:640],
                                             op0=ALU.mult, op1=ALU.mult))
                c.step(V.tensor_tensor(o3, o3, ms[:P, t, 0:4].unsqueeze(2).to_broadcast([P, 4, 128]), ALU.mult))
                c.step(V.tensor_tensor(o3, o3, norms[:P, 0:128].unsqueeze(1).to_broadcast([P, 4, 128]), ALU.mult))
                c.step(V.tensor_tensor(o, o, rs[:P, t, :], ALU.mult))

        @block.scalar
        def _(act):
            act.wait_ge(var_ready, 1)
            nc.scalar.activation(ms[:, :, :], ms[:, :, :], ACT.Sqrt).then_inc(root, 1)


def rank(V, c, dst, val, gt, eq, lt):
    lead, n = list(val.shape[:-1]), val.shape[-1]
    full = lead + [n, n]
    ax = len(lead)
    m_val, n_val = val.unsqueeze(ax).to_broadcast(full), val.unsqueeze(ax + 1).to_broadcast(full)
    c.add(V.tensor_tensor(gt, m_val, n_val, ALU.is_gt))
    c.step(V.tensor_tensor(eq, m_val, n_val, ALU.is_equal))
    c.step(V.tensor_tensor(eq, eq, lt, ALU.mult))
    c.step(V.tensor_tensor(gt, gt, eq, ALU.add))
    c.step(V.tensor_reduce(dst, gt, AX.X, ALU.add))


class Experts:

    RING = 3

    def __init__(self, nc, A, M, l):
        self.posi = M.sb("posi", [128, 2, 5], I32)
        self.gate = M.sb("gate", [128, 2, 5])
        self.tokof = M.sb("tokof", [128, NPAIR], I32)
        self.widx = M.sb("widx", [128, NTILE - NE], I32)
        self.extra = M.sb("extra", [1, 1], I32)
        self.wg = [M.sb(f"wg{i}", [128, KD * 2 * DE]) for i in range(2 * self.RING)]
        self.wd = [M.sb(f"wd{i}", [128, 2 * D]) for i in range(2 * self.RING)]
        self.w_out = [w[:, :].rearrange("p (k n) -> p k n", k=KD) for w in self.wg[-2:]]
        self.loaded = [M.sem(f"weights{i}") for i in range(self.RING)]
        self.w_gu = A["moe_w_gate_up"].rearrange("l g e (p j) f -> (l g e p) (j f)", p=128)
        self.w_dn = A["moe_w_down"].rearrange("l g e (p j) d -> (l g e p) (j d)", p=128)
        self.l = l

    def load(self, eng, i):
        n = self.RING
        for a in range(2):
            row = (self.l * NE + 2 * i + a) * 128
            for dst, src in ((self.wg, self.w_gu), (self.wd, self.w_dn)):
                eng.dma_start(dst[2 * (i % n) + a][:, :], src[row:row + 128, :]).then_inc(self.loaded[i % n], 16)

    def fill(self, eng, pairs):
        for i in pairs:
            self.load(eng, i)


def route(nc, name, C, lg, xT, E):
    l, posi, gate, tokof, widx = E.l, E.posi, E.gate, E.tokof, E.widx
    if True:
        with Scope(nc, name + "a") as s:
            gt4, eq4 = s.sb("gt4", [128, 5, 4, 4]), s.sb("eq4", [128, 5, 4, 4])
            gt8, eq8 = s.sb("gt8", [128, 5, 8, 8]), s.sb("eq8", [128, 5, 8, 8])
            r4, r8 = s.sb("r4", [128, 5, 4]), s.sb("r8", [128, 5, 8])
            mx, dif, ssum, pgrp = s.sb("mx", [128, 5]), s.sb("dif", [128, 5, 5]), s.sb("ssum", [128, 5]), s.sb("pg", [128, 5])
            sel, sel4 = s.sb("sel", [128, 5, 8]), s.sb("sel4", [128, 5, 8, 4])
            oh = s.sb("oh", [128, 2, 5, 8])
            pick = s.sb("pick", [128, 5, 8])
            v2 = s.sb("v2", [128, 5])
            As = s.sb("As", [128, 2, 5, 32])
            A12 = s.sb("A12", [128, 5, 32])
            rk = s.sb("rk", [128, 6, 32])
            cmp8 = s.sb("cmp8", [128, 32, 8])
            tiles, sc = s.sb("tiles", [128, 32]), s.sb("sc", [128, 2, 32])
            pos = s.sb("pos", [128, 10])
            big = s.sb("big", [128, NTILE - NE, 32])
            ex = s.sb("ex", [128, NTILE - NE])
            low, away = s.sb("low", [128, 5, 32]), s.sb("away", [128, 2, 32])
            ge = s.sb("ge", [128, 10, NPAIR + 1])
            ci = s.sb("ci", [128, 10, NPAIR])
            rr = s.sb("rr", [128, 2, 10])
            ohr = xT[:, :, :].rearrange("p k n -> p (k n)")[:, 0:1280].rearrange("p (a n) -> p a n", a=10)
            pr, pt = s.ps("r"), s.ps("t")
            (dv, ex_in, ex_out, asg, ranks, onehots, toks) = (s.sem(x) for x in (
                "dve_steps", "exp_in", "exp_out", "assigned", "ranks", "onehots", "toks"))
            block = s.block()

            @block.tensor
            def _(pe):
                pe.wait_ge(asg, 1)
                for t in range(6):
                    for q in range(min(t, 4) + 1):
                        lhsT = C("before") if q == t else C("ones")
                        last = nc.tensor.matmul(pr[:, 32 * t:32 * t + 32], lhsT, A12[:, q, :],
                                                start=(q == 0), stop=(q == min(t, 4)))
                last.then_inc(ranks, 1)
                pe.wait_ge(onehots, 1)
                for n in range(10):
                    last = nc.tensor.matmul(pt[:, 0:NPAIR], ohr[:, n, :], ci[:, n, :], start=(n == 0), stop=(n == 9))
                last.then_inc(toks, 1)

            @block.scalar
            def _(act):
                act.wait_ge(ex_in, 1)
                nc.scalar.activation(dif[:, :, :], dif[:, :, :], ACT.Exp).then_inc(ex_out, 1)

            @block.vector
            def _(dve):
                c, V = Count(dve, dv), nc.vector
                lt8 = C("lt8").rearrange("p (n m) -> p n m", n=8)
                lc = lg[:, :, 0:4]
                rank(V, c, r4[:, :, :], lc, gt4[:, :, :, :], eq4[:, :, :, :],
                     lt8[:, 0:4, 0:4].unsqueeze(1).to_broadcast([128, 5, 4, 4]))
                c.add(V.tensor_scalar(r4[:, :, :], r4[:, :, :], 0.0, None, ALU.is_equal))
                c.step(V.tensor_reduce(mx[:, :], lc, AX.X, ALU.max))
                c.add(V.tensor_tensor(dif[:, :, 0:4], lc, mx[:, :].unsqueeze(2).to_broadcast([128, 5, 4]), ALU.subtract))
                c.step(V.tensor_tensor(sel4[:, :, :, :],
                                       lg[:, :, 4:36].rearrange("p t (g e) -> p t e g", g=4),
                                       r4[:, :, :].unsqueeze(2).to_broadcast([128, 5, 8, 4]), ALU.mult))
                c.step(V.tensor_reduce(sel[:, :, :], sel4[:, :, :, :], AX.X, ALU.add))
                rank(V, c, r8[:, :, :], sel[:, :, :], gt8[:, :, :, :], eq8[:, :, :, :],
                     lt8.unsqueeze(1).to_broadcast([128, 5, 8, 8]))
                for k in range(2):
                    c.add(V.tensor_scalar(oh[:, k, :, :], r8[:, :, :], float(k), None, ALU.is_equal))
                c.step(V.tensor_reduce(mx[:, :], sel[:, :, :], AX.X, ALU.max))
                c.step(V.tensor_tensor(pick[:, :, :], sel[:, :, :], oh[:, 1, :, :], ALU.mult))
                c.step(V.tensor_reduce(v2[:, :], pick[:, :, :], AX.X, ALU.add))
                V.tensor_tensor(dif[:, :, 4], v2[:, :], mx[:, :], ALU.subtract).then_inc(ex_in, 1)
                for k in range(2):
                    c.add(V.tensor_tensor(As[:, k, :, :].rearrange("p t (g e) -> p t g e", g=4),
                                          r4[:, :, :].unsqueeze(3).to_broadcast([128, 5, 4, 8]),
                                          oh[:, k, :, :].unsqueeze(2).to_broadcast([128, 5, 4, 8]), ALU.mult))
                c.wait()
                for k in range(2):
                    c.add(V.tensor_tensor(As[:, k, :, :], As[:, k, :, :],
                                          C("valid").unsqueeze(2).to_broadcast([128, 5, 32]), ALU.mult))
                c.wait()
                V.tensor_tensor(A12[:, :, :], As[:, 0, :, :], As[:, 1, :, :], ALU.add).then_inc(asg, 1)
                dve.wait_ge(ex_out, 1)
                c.add(V.tensor_reduce(ssum[:, :], dif[:, :, 0:4], AX.X, ALU.add))
                c.step(V.tensor_scalar(pgrp[:, :], dif[:, :, 4], 1.0, None, ALU.add))
                c.step(V.tensor_tensor(ssum[:, :], ssum[:, :], pgrp[:, :], ALU.mult))
                c.step(V.reciprocal(gate[:, 0, :], ssum[:, :]))
                c.add(V.tensor_tensor(gate[:, 1, :], gate[:, 0, :], dif[:, :, 4], ALU.mult))
                dve.wait_ge(ranks, 1)
                c.step(V.tensor_copy(rk[:, :, :], pr[:, 0:192].rearrange("p (t e) -> p t e", t=6)))
                c.step(V.tensor_tensor(cmp8[:, :, :], rk[:, 5, :].unsqueeze(2).to_broadcast([128, 32, 8]),
                                       C("m64").unsqueeze(1).to_broadcast([128, 32, 8]), ALU.is_gt))
                c.step(V.tensor_reduce(tiles[:, :], cmp8[:, :, :], AX.X, ALU.add))
                c.step(V.tensor_copy(sc[:, 0, :], tiles[:, :]))
                cur = 0
                for sh in (1, 2, 4, 8, 16):
                    c.add(V.tensor_copy(sc[:, 1 - cur, 0:sh], sc[:, cur, 0:sh]))
                    c.step(V.tensor_tensor(sc[:, 1 - cur, sh:32], sc[:, cur, sh:32], sc[:, cur, 0:32 - sh], ALU.add))
                    cur = 1 - cur
                ends = sc[:, cur, :]
                c.add(V.tensor_copy(E.extra[:, :], ends[0:1, 31:32]))
                c.add(V.tensor_tensor(big[:, :, :], ends.unsqueeze(1).to_broadcast([128, NTILE - NE, 32]),
                                      C("tile").unsqueeze(2).to_broadcast([128, NTILE - NE, 32]), ALU.is_le))
                c.step(V.tensor_tensor(tiles[:, :], ends, tiles[:, :], ALU.subtract))
                c.add(V.tensor_reduce(ex[:, :], big[:, :, :], AX.X, ALU.add))
                c.step(V.tensor_scalar(away[:, 0, :], tiles[:, :], float(SLOT), float(SLOT * (NE - 1)), ALU.mult, ALU.add))
                c.add(V.tensor_scalar(ex[:, :], ex[:, :], NE - 1.0, 128.0, ALU.min, ALU.mult))
                c.add(V.tensor_scalar(low[:, :, :], rk[:, 0:5, :], SLOT - 0.5, None, ALU.is_lt))
                c.step(V.tensor_tensor(away[:, 1, :], C("e64"), away[:, 0, :], ALU.subtract))
                c.add(V.tensor_scalar(widx[:, :], ex[:, :], C("pidx"), float(l * NE * 128), ALU.add, ALU.add))
                c.step(V.tensor_tensor(low[:, :, :], low[:, :, :], away[:, 1, :].unsqueeze(1).to_broadcast([128, 5, 32]),
                                       ALU.mult))
                c.step(V.tensor_tensor(rk[:, 0:5, :], rk[:, 0:5, :], away[:, 0, :].unsqueeze(1).to_broadcast([128, 5, 32]),
                                       ALU.add))
                c.step(V.tensor_tensor(rk[:, 0:5, :], rk[:, 0:5, :], low[:, :, :], ALU.add))
                for k in range(2):
                    c.add(V.tensor_tensor(As[:, k, :, :], As[:, k, :, :], rk[:, 0:5, :], ALU.mult))
                c.wait()
                c.step(V.tensor_reduce(pos[:, :], As[:, :, :, :].rearrange("p k t e -> p (k t) e"), AX.X, ALU.add))
                c.add(V.tensor_copy(posi[:, :, :].rearrange("p k t -> p (k t)"), pos[:, :]))
                c.step(V.tensor_tensor(ge[:, :, :], pos[:, :].unsqueeze(2).to_broadcast([128, 10, NPAIR + 1]),
                                       C("m128").unsqueeze(1).to_broadcast([128, 10, NPAIR + 1]), ALU.is_ge))
                c.add(V.tensor_tensor(ci[:, :, :], ge[:, :, 0:NPAIR], ge[:, :, 1:NPAIR + 1], ALU.subtract))
                c.step(V.tensor_reduce(rr[:, 0, :], ge[:, :, 1:NPAIR + 1], AX.X, ALU.add))
                c.step(V.scalar_tensor_tensor(out=rr[:, 1, :], in0=rr[:, 0, :], scalar=-128.0, in1=pos[:, :],
                                              op0=ALU.mult, op1=ALU.add))
                for k in range(2):
                    c.add(V.tensor_tensor(ci[:, 5 * k:5 * k + 5, :], ci[:, 5 * k:5 * k + 5, :],
                                          C("tokid").unsqueeze(2).to_broadcast([128, 5, NPAIR]), ALU.mult))
                c.wait()
                V.tensor_tensor(ohr[:, :, :], rr[:, 1, :].unsqueeze(2).to_broadcast([128, 10, 128]),
                                C("iota").unsqueeze(1).to_broadcast([128, 10, 128]), ALU.is_equal).then_inc(onehots, 1)
                dve.wait_ge(toks, 1)
                c.step(V.tensor_copy(tokof[:, :], pt[:, 0:NPAIR]))



def expert_stage(nc, name, C, E, xT, xd, yd, pairs):
    NR = E.RING
    n, first = len(pairs), 2 * pairs[0] - NE
    extra = first >= 0
    with Scope(nc, name) as s:
        wg, wd = E.wg, E.wd
        xg = [s.sb(f"xg{i}", [128, D]) for i in range(2)]
        xgT = [xT[:, :, 128 * i:128 * i + 128] for i in range(2)]
        sg, hh, hT = xT[:, 0, 256:256 + DE], xT[:, 1, 256:256 + DE], xT[:, 2:4, 256:384]
        Y = [s.sb(f"Y{i}", [128, D]) for i in range(2)]
        px = [s.ps(f"x{i}") for i in range(2)]
        pg = [s.ps(f"g{i}") for i in range(2)]
        ph = s.ps("h")
        py = [s.ps(f"y{i}") for i in range(2)]
        wl = [s.sem(f"gathered{i}") for i in range(NR)] if extra else E.loaded
        xl = [s.sem(f"rows{i}") for i in range(2)]
        ys = [s.sem(f"kept{i}") for i in range(2)]
        (xt, xta, xtd, gu, sl, hr, ht, htc, dn, ya, ydv) = (s.sem(x) for x in (
            "x_T", "x_act", "x_dve", "gate_up", "silu", "hidden", "h_T", "h_copied", "down", "y_act", "y_dve"))
        block = s.block()

        def when(eng, run):
            if not extra:
                return run(eng)
            tiles = eng.value_load(E.extra[0:1, 0:1], min_val=0, max_val=NTILE - NE)
            with eng.If(tiles > first):
                run(eng)

        def free(eng, i):
            if i >= NR:
                eng.wait_ge(gu, i - NR + 1)
                eng.wait_ge(dn, i - NR + 1)

        @block.gpsimd
        def _(pool):
            def rows(i):
                if i >= 2:
                    pool.wait_ge(xt, i - 1)
                at = pairs[i]
                nc.gpsimd.indirect_dma_start(out=xg[i % 2][:, :], out_offset=None, in_=xd,
                                             in_offset=bass.IndirectOffsetOnAxis(ap=E.tokof[:, at:at + 1], axis=0))\
                    .then_inc(xl[i % 2], 16)

            def run(pool):
                rows(0)
                for i in range(n):
                    if i + 1 < n:
                        rows(i + 1)
                    if extra:
                        free(pool, i)
                        for a in range(2):
                            at = bass.IndirectOffsetOnAxis(ap=E.widx[:, first + 2 * i + a:first + 2 * i + a + 1], axis=0)
                            for dst, src in ((wg, E.w_gu), (wd, E.w_dn)):
                                nc.gpsimd.indirect_dma_start(out=dst[2 * (i % NR) + a][:, :], out_offset=None,
                                                             in_=src, in_offset=at).then_inc(wl[i % NR], 16)
            when(pool, run)

        @block.sync
        def _(sp):
            def store(i):
                sp.wait_ge(ya, i + 1)
                sp.wait_ge(ydv, i + 1)
                at = 128 * pairs[i]
                sp.dma_start(yd[at:at + 128, :], Y[i % 2][:, :]).then_inc(ys[i % 2], 16)

            def run(sp):
                for i in range(n):
                    if not extra and i >= NR:
                        free(sp, i)
                        E.load(sp, i)
                    if i >= NR:
                        store(i - NR)
                for i in range(max(n - NR, 0), n):
                    store(i)
                for i in range(min(n, 2)):
                    sp.wait_ge(ys[i], 16 * ((n - i + 1) // 2))
            when(sp, run)

        @block.tensor
        def _(pe):
            def x_T(i):
                pe.wait_ge(xl[i % 2], 16 * (i // 2 + 1))
                if i >= 1:
                    pe.wait_ge(xta, i)
                    pe.wait_ge(xtd, i)
                xv = xg[i % 2][:, :].rearrange("r (p j) -> r j p", j=KD)
                for j in range(KD):
                    last = nc.tensor.transpose(px[j // 4][:, (j % 4) * 128:(j % 4) * 128 + 128], xv[:, j, :], C("ident"))
                last.then_inc(xt, 1)

            def gate_up(i):
                pe.wait_ge(wl[i % NR], 64 * (i // NR + 1))
                pe.wait_ge(xta, i + 1)
                pe.wait_ge(xtd, i + 1)
                if i >= 2:
                    pe.wait_ge(hr, i - 1)
                for j in range(KD):
                    for a in range(2):
                        last = nc.tensor.matmul(pg[i % 2][64 * a:64 * a + 64, :], xgT[i % 2][:, j, 64 * a:64 * a + 64],
                                                wg[2 * (i % NR) + a][:, j * 512:(j + 1) * 512],
                                                start=(j == 0), stop=(j == KD - 1))
                last.then_inc(gu, 1)

            def h_T(i):
                pe.wait_ge(hr, i + 1)
                if i >= 1:
                    pe.wait_ge(htc, i)
                hv = hh.rearrange("r (p j) -> r j p", j=2)
                for j in range(2):
                    last = nc.tensor.transpose(ph[:, j * 128:(j + 1) * 128], hv[:, j, :], C("ident"))
                last.then_inc(ht, 1)

            def down(i):
                pe.wait_ge(htc, i + 1)
                if i >= 1:
                    pe.wait_ge(ya, i)
                    pe.wait_ge(ydv, i)
                for n2 in range(2):
                    for j in range(2):
                        for a in range(2):
                            last = nc.tensor.matmul(py[n2][64 * a:64 * a + 64, :], hT[:, j, 64 * a:64 * a + 64],
                                                    wd[2 * (i % NR) + a][:, j * D + n2 * 512:j * D + (n2 + 1) * 512],
                                                    start=(j == 0), stop=(j == 1))
                last.then_inc(dn, 1)

            def run(pe):
                x_T(0)
                for i in range(n + 1):
                    if i < n:
                        gate_up(i)
                    if i >= 1:
                        h_T(i - 1)
                    if i + 1 < n:
                        x_T(i + 1)
                    if i >= 1:
                        down(i - 1)
            when(pe, run)

        def copy_x(i, half, eng, sem):
            eng.wait_ge(xt, i + 1)
            if i >= 2:
                eng.wait_ge(gu, i - 1)
            dst, src = xgT[i % 2][:, 4 * half:4 * half + 4, :], px[half][:, :].rearrange("p (j n) -> p j n", j=4)
            ins = nc.scalar.activation(dst, src, ACT.Copy) if half == 0 else nc.vector.tensor_copy(dst, src)
            ins.then_inc(sem, 1)

        def copy_y(i, half, eng, sem):
            eng.wait_ge(dn, i + 1)
            if i >= 2:
                eng.wait_ge(ys[i % 2], 16 * (i // 2))
            dst = Y[i % 2][:, 512 * half:512 * half + 512]
            ins = nc.scalar.activation(dst, py[half][:, :], ACT.Copy) if half == 0 else \
                nc.vector.tensor_copy(dst, py[half][:, :])
            ins.then_inc(sem, 1)

        @block.scalar
        def _(act):
            def run(act):
                copy_x(0, 0, act, xta)
                for i in range(n + 1):
                    if i < n:
                        act.wait_ge(gu, i + 1)
                        if i >= 1:
                            act.wait_ge(hr, i)
                        nc.scalar.activation(sg, pg[i % 2][:, 0:DE], ACT.Silu).then_inc(sl, 1)
                    if i >= 1:
                        act.wait_ge(ht, i)
                        if i >= 2:
                            act.wait_ge(dn, i - 1)
                        nc.scalar.activation(hT, ph[:, 0:256].rearrange("p (j n) -> p j n", j=2), ACT.Copy)\
                            .then_inc(htc, 1)
                    if i + 1 < n:
                        copy_x(i + 1, 0, act, xta)
                    if i >= 1:
                        copy_y(i - 1, 0, act, ya)
            when(act, run)

        @block.vector
        def _(dve):
            def run(dve):
                copy_x(0, 1, dve, xtd)
                for i in range(n + 1):
                    if i < n:
                        dve.wait_ge(sl, i + 1)
                        if i >= 1:
                            dve.wait_ge(ht, i)
                        nc.vector.tensor_tensor(hh, sg, pg[i % 2][:, DE:2 * DE], ALU.mult).then_inc(hr, 1)
                    if i + 1 < n:
                        copy_x(i + 1, 1, dve, xtd)
                    if i >= 1:
                        copy_y(i - 1, 1, dve, ydv)
            when(dve, run)


class Cache:

    LOADS = [(G, kind, pq) for kind in "kv" for G in range(2) for pq in range(4)]
    RING = 3

    def __init__(self, nc, A, L, pages):
        self.nc, self.pages = nc, pages
        self.ring = []
        self.grow(L, self.RING - 1)
        self.loaded = [L.kept[f"cache_loaded{i}"] for i in range(self.RING)]
        self.views = {k: A["cache_" + k].rearrange("n (c r) h d -> (n c) (r h d)", r=4) for k in "kv"}

    def grow(self, s, n):
        for i in range(len(self.ring), len(self.ring) + n):
            self.ring.append([s.sb(f"kv{i}{b}", [128, 4 * 512]) for b in range(4)])

    def load(self, n):
        G, kind, pq = self.LOADS[n]
        for b in range(4):
            at = (4 * G + b) * 4 + pq
            self.nc.gpsimd.indirect_dma_start(out=self.ring[n % self.RING][b][:, :], out_offset=None,
                                              in_=self.views[kind],
                                              in_offset=bass.IndirectOffsetOnAxis(ap=self.pages[:, at:at + 1], axis=0))\
                .then_inc(self.loaded[n % self.RING], 16)


def mixer_cd(nc, A, C, xT, pages):
    mixT = xT
    with Scope(nc, "cd") as L:
        vt = L.sb("vt", [128, 5, 512])
        qkT = L.sb("qkT", [128, KD, NTOK])
        cache = Cache(nc, A, L, pages)
        with Scope(nc, "cdp") as F:
            qk = F.sb("qk", [128, 5, 1024])
            uP = F.sb("uP", [128, 4, PBUF + SEQ])
            uS = F.sb("uS", [128, 4, NB, PBUF + NS])
            if True:
                def jobs_of(n, w):
                    out = []
                    if n == 0:
                        for f in range(4):
                            out.append(Job(n, 128, 512, lambda k, f=f: w[:, k, f * 128:f * 128 + 128],
                                           lambda k: xT[:, k, 0:512], "act",
                                           lambda p, f=f: nc.scalar.activation(uP[:, f, PBUF:], p, ACT.Copy)))
                            out.append(Job(n, 128, 32, lambda k, f=f: w[:, k, f * 128:f * 128 + 128],
                                           lambda k: xT[:, k, 512:544], "dve",
                                           lambda p, f=f: nc.vector.tensor_copy(
                                               uS[:, f, :, PBUF:], p.rearrange("p (b s) -> p b s", s=NS))))
                        return out
                    for t, P in TILES:
                        def copy(p, t=t, P=P):
                            dst = vt[:P, t, :] if n == 3 else qk[:P, t, (n - 1) * 512:n * 512]
                            if t % 2:
                                return nc.scalar.activation(dst, p, ACT.Copy)
                            return nc.vector.tensor_copy(dst, p)
                        out.append(Job(n, P, 512, lambda k, t=t, P=P: xT[:, k, tok0(t):tok0(t) + P],
                                       lambda k: w[:, k, 0:512], "act" if t % 2 else "dve", copy))
                    return out

                project_stage(nc, "cdi", A["cd_w_in"], [(512 * i, 512 * i + 512) for i in range(4)], 512, xT, jobs_of, nbuf=2,
                              ahead=lambda pool: [cache.load(n) for n in range(cache.RING - 1)])
            rope_and_pool(nc, A, C, qk, vt, uP, uS, mixT)
            transpose_stage(nc, "cdq", C, qk, qkT)
        cache.grow(L, 1)
        attend_prompt(nc, C, qkT, vt, mixT, cache)
        attend_sample(nc, C, qkT, vt, mixT, cache)


def rope_and_pool(nc, A, C, qk, vt, uP, uS, mixT):
    with Scope(nc, "pl") as s:
        r1, r2 = s.sb("r1", [128, 5, 16, 8]), s.sb("r2", [128, 5, 16, 8])
        r3, r4 = s.sb("r3", [128, 5, 16, 8]), s.sb("r4", [128, 5, 16, 8])
        st = s.sb("st", [NB * PBUF, 512])
        wp = s.sb("wp", [128, 4, 128])
        pscr, psc = s.sb("pscr", [4, 128]), s.sb("psc", [128, 4])
        sP = [s.sb(f"sP{i}", [128, PBUF + SEQ]) for i in range(2)]
        sS = [s.sb(f"sS{i}", [128, NB, PBUF + NS]) for i in range(2)]
        Df = s.sb("Df", [128, 4, NTOK])
        newS = s.sb("newS", [128, 4, NB * PBUF])
        outs = s.sb("outs", [128, 2, 512])
        pst, pnp, pns = s.ps("st"), s.ps("np"), s.ps("ns")
        pm = [s.ps(f"m{i}") for i in range(4)]
        (loaded, st_T, dv, act_c, rot, stored, ext, new_c, new_T, new_o, dif, mixed) = (s.sem(x) for x in (
            "loaded", "st_T", "dve_steps", "act_c", "rotated", "stored", "ext", "new_c", "new_T", "new_o", "dif", "mixed"))
        block = s.block()

        @block.sync
        def _(sp):
            sp.dma_start(st[:, :], A["state_pool"].rearrange("b i c -> (b i) c")).then_inc(loaded, 16)
            sp.dma_start(wp[:, :, :], A["cd_w_pool"].rearrange("g c d -> c g d")).then_inc(loaded, 16)
            sp.dma_start(pscr[:, :], A["cd_pool_scale"].rearrange("(g d) -> g d", d=128)).then_inc(loaded, 16)
            sp.dma_start(A["v_p"][0].rearrange("(t p) h d -> p t (h d)", p=128), vt[:, 0:4, :]).then_inc(stored, 16)
            sp.dma_start(A["v_s"].rearrange("b s h d -> (b s) (h d)"), vt[0:32, 4, :]).then_inc(stored, 16)
            sp.wait_ge(rot, 1)
            sp.dma_start(A["k_p"][0].rearrange("(t p) h d -> p t (h d)", p=128), qk[:, 0:4, 512:1024]).then_inc(stored, 16)
            sp.dma_start(A["k_s"].rearrange("b s h d -> (b s) (h d)"), qk[0:32, 4, 512:1024]).then_inc(stored, 16)
            sp.wait_ge(new_o, 1)
            sp.dma_start(A["pool_p"][0], outs[0:PBUF, 0, :]).then_inc(stored, 16)
            sp.dma_start(A["pool_s"].rearrange("b i c -> (b i) c"), outs[0:NB * PBUF, 1, :]).then_inc(stored, 16)
            sp.wait_ge(stored, 16 * 6)

        @block.tensor
        def _(pe):
            pe.wait_ge(loaded, 48)
            for g in range(4):
                last = nc.tensor.transpose(pst[:, g * 120:(g + 1) * 120], st[:, g * 128:(g + 1) * 128],
                                           C("ident")[:120, :120])
            last = nc.tensor.transpose(pst[:, 480:484], pscr[:, :], C("ident")[:4, :4])
            last.then_inc(st_T, 1)
            pe.wait_ge(new_c, 1)
            for g in range(4):
                nc.tensor.transpose(pnp[:PBUF, g * 128:(g + 1) * 128], uP[:, g, SEQ:SEQ + PBUF], C("ident"))
            for g in range(4):
                last = nc.tensor.transpose(pns[:NB * PBUF, g * 128:(g + 1) * 128], newS[:, g, :], C("ident"))
            last.then_inc(new_T, 1)
            for g in range(4):
                pe.wait_ge(dif, g + 1)
                if g >= 2:
                    pe.wait_ge(mixed, g - 1)
                a, b = pm[2 * (g % 2)], pm[2 * (g % 2) + 1]
                nc.tensor.matmul(a[:, :], wp[:, g, :], Df[:, g, 0:512], start=True, stop=True)
                nc.tensor.matmul(b[:, 0:32], wp[:, g, :], Df[:, g, 512:544], start=True, stop=True).then_inc(act_c, 1)

        @block.scalar
        def _(act):
            for g in range(4):
                act.wait_ge(act_c, g + 1)
                a, b = pm[2 * (g % 2)], pm[2 * (g % 2) + 1]
                nc.scalar.activation(mixT[:, g, 0:512], a[:, :], ACT.Copy, scale=psc[:, g:g + 1])
                nc.scalar.activation(mixT[:, g, 512:544], b[:, 0:32], ACT.Copy, scale=psc[:, g:g + 1]).then_inc(mixed, 1)

        @block.vector
        def _(dve):
            c, V = Count(dve, dv), nc.vector
            halves = []
            for ts, P in (((0, 4), 128), ((4, 5), 32)):
                n = ts[1] - ts[0]
                sl = slice(ts[0], ts[1])
                w = qk[:P, sl, :].rearrange("p t (h d) -> p t h d", d=64)
                x1, x2 = w[:, :, :, 0:8], w[:, :, :, 8:16]
                table = C("rope")[:P, :].rearrange("p (t c) -> p t c", c=16)[:, sl, :]
                cos = table[:, :, 0:8].unsqueeze(2).to_broadcast([P, n, 16, 8])
                sin = table[:, :, 8:16].unsqueeze(2).to_broadcast([P, n, 16, 8])
                for dst, x, f in ((r1, x1, cos), (r2, x2, sin), (r3, x2, cos), (r4, x1, sin)):
                    c.add(V.tensor_tensor(dst[:P, sl, :, :], x, f, ALU.mult))
                halves.append((P, sl, x1, x2))
            c.wait()
            for P, sl, x1, x2 in halves:
                c.add(V.tensor_tensor(x1, r1[:P, sl, :, :], r2[:P, sl, :, :], ALU.subtract))
                last = V.tensor_tensor(x2, r3[:P, sl, :, :], r4[:P, sl, :, :], ALU.add)
                if P == 128:
                    c.add(last)
            last.then_inc(rot, 1)
            c.step(V.memset(uP[:, :, 0:PBUF], 0.0))
            dve.wait_ge(st_T, 1)
            c.add(V.tensor_copy(psc[:, :], pst[:, 480:484]))
            c.step(V.tensor_copy(uS[:, :, :, 0:PBUF], pst[:, 0:480].rearrange("p (g b i) -> p g b i", g=4, b=NB)))
            V.tensor_copy(newS[:, :, :].rearrange("p g (b i) -> p g b i", b=NB), uS[:, :, :, NS:]).then_inc(new_c, 1)
            for g, w in enumerate(WINDOWS):
                sp_, ss_ = uP[:, g, :], uS[:, g, :, :]
                width, i = 1, 0
                while width < w:
                    n = PBUF + SEQ - width
                    c.add(V.tensor_tensor(sP[i][:, width:], sp_[:, width:], sp_[:, 0:n], ALU.add))
                    c.add(V.tensor_copy(sP[i][:, 0:width], sp_[:, 0:width]))
                    c.add(V.tensor_tensor(sS[i][:, :, width:], ss_[:, :, width:], ss_[:, :, 0:PBUF + NS - width], ALU.add))
                    c.step(V.tensor_copy(sS[i][:, :, 0:width], ss_[:, :, 0:width]))
                    sp_, ss_ = sP[i], sS[i]
                    width, i = 2 * width, 1 - i
                inv = C("invcnt")[:, 16 * g:16 * g + PBUF]
                c.add(V.tensor_tensor(Df[:, g, 0:PBUF], sp_[:, PBUF:2 * PBUF], inv, ALU.mult))
                c.add(V.scalar_tensor_tensor(out=Df[:, g, PBUF:512], in0=sp_[:, 2 * PBUF:], scalar=1.0 / w,
                                             in1=uP[:, g, 2 * PBUF:], op0=ALU.mult, op1=ALU.subtract))
                c.add(V.scalar_tensor_tensor(out=Df[:, g, 512:544].rearrange("p (b s) -> p b s", s=NS),
                                             in0=ss_[:, :, PBUF:], scalar=1.0 / w, in1=uS[:, g, :, PBUF:],
                                             op0=ALU.mult, op1=ALU.subtract))
                c.wait()
                V.tensor_tensor(Df[:, g, 0:PBUF], Df[:, g, 0:PBUF], uP[:, g, PBUF:2 * PBUF], ALU.subtract)\
                 .then_inc(dif, 1)
            dve.wait_ge(new_T, 1)
            V.tensor_copy(outs[0:PBUF, 0, :], pnp[:PBUF, :])
            V.tensor_copy(outs[0:NB * PBUF, 1, :], pns[:NB * PBUF, :]).then_inc(new_o, 1)


def attend_prompt(nc, C, qkT, vt, mixT, cache):
    units = [(h, t) for h in range(8) for t in range(4)]
    scale = 64 ** -0.5
    with Scope(nc, "ap") as s:
        Pm = [s.sb(f"P{i}", [128, 512]) for i in range(3)]
        PT = [s.sb(f"PT{i}", [128, 512]) for i in range(2)]
        nb = s.sb("nb", [128, len(units)])
        den = s.sb("den", [128, len(units)])
        ot = s.sb("ot", [128, 4, 512])
        psc = [s.ps(f"s{i}") for i in range(3)]
        ptr = [s.ps(f"t{i}") for i in range(2)]
        po = [s.ps(f"o{i}") for i in range(2)]
        (sc, dv, mxd, ex, tr, ptc, pv, od, o_T, o_c) = (s.sem(x) for x in (
            "scores", "dve_steps", "max_ready", "exps", "P_T", "P_copied", "pv", "o_ready", "o_T", "o_copied"))
        block = s.block()
        n = len(units)

        @block.gpsimd
        def _(pool):
            cache.load(cache.RING - 1)

        @block.tensor
        def _(pe):
            for u in range(n + 2):
                if u < n:
                    h, t = units[u]
                    r, w = slice(64 * (h % 2), 64 * (h % 2) + 64), (t + 1) * 128
                    if u >= 3:
                        pe.wait_ge(ex, u - 2)
                    nc.tensor.matmul(psc[u % 3][:, 0:w], qkT[r, h // 2, 128 * t:128 * t + 128],
                                     qkT[r, 4 + h // 2, 0:w], start=True, stop=True).then_inc(sc, 1)
                if 1 <= u <= n:
                    h, t = units[u - 1]
                    pe.wait_ge(ex, u)
                    if u >= 3:
                        pe.wait_ge(ptc, u - 2)
                    for k in range(t + 1):
                        last = nc.tensor.transpose(ptr[(u - 1) % 2][:, 128 * k:128 * k + 128],
                                                   Pm[(u - 1) % 3][:, 128 * k:128 * k + 128], C("ident"))
                    last.then_inc(tr, 1)
                if u >= 2:
                    h, t = units[u - 2]
                    pe.wait_ge(ptc, u - 1)
                    if u >= 4:
                        pe.wait_ge(od, u - 3)
                    for k in range(t + 1):
                        last = nc.tensor.matmul(po[u % 2][:, 0:64], PT[u % 2][:, 128 * k:128 * k + 128],
                                                vt[:, k, h * 64:(h + 1) * 64], start=(k == 0), stop=(k == t))
                    last.then_inc(pv, 1)
            pe.wait_ge(od, n)
            for t in range(4):
                for f in range(4):
                    last = nc.tensor.transpose((psc + ptr)[t][:, f * 128:(f + 1) * 128],
                                               ot[:, t, f * 128:(f + 1) * 128], C("ident"))
                last.then_inc(o_T, 1)

        @block.vector
        def _(dve):
            c, V = Count(dve, dv), nc.vector
            for u in range(n + 2):
                if u < n:
                    h, t = units[u]
                    w = (t + 1) * 128
                    dve.wait_ge(sc, u + 1)
                    c.step(V.tensor_tensor(psc[u % 3][:, 128 * t:w], psc[u % 3][:, 128 * t:w], C("causal"), ALU.add))
                    c.step(V.reduce_max(nb[:, u:u + 1], psc[u % 3][:, 0:w], AX.X))
                    V.tensor_scalar(nb[:, u:u + 1], nb[:, u:u + 1], -scale, None, ALU.mult).then_inc(mxd, 1)
                if u >= 2:
                    h, t = units[u - 2]
                    dve.wait_ge(ex, u - 1)
                    c.step(V.reciprocal(den[:, u - 2:u - 1], den[:, u - 2:u - 1]))
                    dve.wait_ge(pv, u - 1)
                    V.tensor_scalar(ot[:, t, h * 64:(h + 1) * 64], po[u % 2][:, 0:64], den[:, u - 2:u - 1], None,
                                    ALU.mult).then_inc(od, 1)
            for t in range(4):
                dve.wait_ge(o_T, t + 1)
                V.tensor_copy(mixT[:, 4:8, 128 * t:128 * t + 128],
                              (psc + ptr)[t][:, :].rearrange("p (f n) -> p f n", f=4)).then_inc(o_c, 1)

        @block.scalar
        def _(act):
            for u in range(n + 1):
                if u < n:
                    h, t = units[u]
                    w = (t + 1) * 128
                    act.wait_ge(mxd, u + 1)
                    if u >= 3:
                        act.wait_ge(tr, u - 2)
                    nc.scalar.activation(Pm[u % 3][:, 0:w], psc[u % 3][:, 0:w], ACT.Exp, bias=nb[:, u:u + 1],
                                         scale=scale, accum_out=den[:, u:u + 1]).then_inc(ex, 1)
                if u >= 1:
                    h, t = units[u - 1]
                    act.wait_ge(tr, u)
                    if u >= 3:
                        act.wait_ge(pv, u - 2)
                    nc.scalar.activation(PT[(u - 1) % 2][:, 0:(t + 1) * 128], ptr[(u - 1) % 2][:, 0:(t + 1) * 128],
                                         ACT.Copy).then_inc(ptc, 1)


def attend_sample(nc, C, qkT, vt, mixT, cache):
    scale = 64 ** -0.5
    with Scope(nc, "as") as s:
        NBUF, ring, loads, kvl = cache.RING, cache.ring, cache.LOADS, cache.loaded
        KT = [qkT[:, 0:4, 0:512], qkT[:, 4:8, 0:512]] + [s.sb(f"KT{b}", [128, 4, 512]) for b in range(2)]
        PT = vt[:, 0:4, :].rearrange("p t (r n) -> p (t r) n", r=4)
        Q = s.sb("Q", [128, NB, 4, 32])
        Ss = [s.sb(f"S{G}", [128, 4 * 512 + NS]) for G in range(2)]
        own, ownT = s.sb("own", [128, 32]), s.sb("ownT", [32, 128])
        gs, rk, gt8, eq8, pen = s.sb("gs", [128, 8]), s.sb("rk", [128, 8]), s.sb("gt8", [128, 8, 8]), s.sb("eq8", [128, 8, 8]), s.sb("pen", [128, 8])
        nb, den = s.sb("nb", [128, 2]), s.sb("den", [128, 2])
        Oh, wh = KT[2][:, 0, :], KT[2][:, 1, 0:8]
        ptk = [s.ps(f"k{i}") for i in range(4)]
        pss = [s.ps(f"s{i}") for i in range(2)]
        po, pw = s.ps("o"), s.ps("w")
        (dv, k_T, kcp, kcp2, scored, sccp, q_r, soft, exs, pT, pTc, ownr, ownTr, ownc, pvd, oh_r, o_t,
         o_c, kvused) = (s.sem(x) for x in (
             "dve_steps", "K_T", "K_act", "K_dve", "scored", "s_copied", "Q_ready",
             "softmax_in", "exps", "P_T", "P_copied", "own_ready", "own_T", "own_copied", "pv", "O_ready", "O_T",
             "O_copied", "kv_used"))
        BANKS = (0, 2, 1, 3)
        block = s.block()

        @block.gpsimd
        def _(pool):
            for n in range(NBUF, len(loads)):
                m = n - NBUF + 1
                if loads[n - NBUF][1] == "k":
                    pool.wait_ge(k_T, 16 * sum(q[1] == "k" for q in loads[:m]))
                else:
                    pool.wait_ge(kvused, sum(q[1] == "v" for q in loads[:m]))
                cache.load(n)

        @block.tensor
        def _(pe):
            pe.wait_ge(q_r, 1)
            nk = 0
            for n, (G, kind, pq) in enumerate(loads):
                pe.wait_ge(kvl[n % NBUF], 64 * (n // NBUF + 1))
                if kind == "k":
                    for b in range(4):
                        for c in BANKS:
                            if nk:
                                pe.wait_ge(kcp if c < 2 else kcp2, 2 * nk - 1 + c % 2)
                            for r in range(4):
                                last = nc.tensor.transpose(ptk[c][:, r * 128:(r + 1) * 128],
                                                           ring[n % NBUF][b][:, r * 512 + c * 128:r * 512 + (c + 1) * 128],
                                                           C("ident"))
                            last.then_inc(k_T, 1)
                        nk += 1
                    pe.wait_ge(kcp, 2 * nk)
                    pe.wait_ge(kcp2, 2 * nk)
                    ns = G * 5 + pq
                    if ns >= 2:
                        pe.wait_ge(sccp, ns - 1)
                    for c in range(4):
                        for b in range(4):
                            last = nc.tensor.matmul(pss[ns % 2][32 * b:32 * b + 32, :], Q[:, 4 * G + b, c, :],
                                                    KT[b][:, c, :], start=(c == 0), stop=(c == 3),
                                                    tile_position=(0, 32 * b))
                    last.then_inc(scored, 1)
                    if pq == 3:
                        ns += 1
                        pe.wait_ge(sccp, ns - 1)
                        for b in range(4):
                            for c in range(4):
                                tok = 512 + 4 * (4 * G + b)
                                last = nc.tensor.matmul(pss[ns % 2][32 * b:32 * b + 32, 0:NS], Q[:, 4 * G + b, c, :],
                                                        qkT[:, 4 + c, tok:tok + NS], start=(c == 0), stop=(c == 3),
                                                        tile_position=(0, 32 * b))
                        last.then_inc(scored, 1)
                else:
                    if pq == 0:
                        pe.wait_ge(exs, G + 1)
                        for q in range(4):
                            for r in range(4):
                                last = nc.tensor.transpose(ptk[q][:, r * 128:(r + 1) * 128],
                                                           Ss[G][:, q * 512 + r * 128:q * 512 + (r + 1) * 128],
                                                           C("ident"))
                            last.then_inc(pT, 1)
                        pe.wait_ge(ownr, G + 1)
                        if G:
                            pe.wait_ge(o_c, G)
                        nc.tensor.transpose(pw[0:32, 0:128], own[:, :], C("ident")).then_inc(ownTr, 1)
                        pe.wait_ge(pTc, 4 * G + 4)
                        if G:
                            pe.wait_ge(oh_r, G)
                    for r in range(4):
                        for b in range(4):
                            last = nc.tensor.matmul(po[32 * b:32 * b + 32, :], PT[:, 4 * pq + r, 32 * b:32 * b + 32],
                                                    ring[n % NBUF][b][:, r * 512:(r + 1) * 512],
                                                    start=(pq == 0 and r == 0), stop=False, tile_position=(0, 32 * b),
                                                    skip_group_check=True)
                    last.then_inc(kvused, 1)
                    if pq == 3:
                        pe.wait_ge(ownc, G + 1)
                        for b in range(4):
                            last = nc.tensor.matmul(po[32 * b:32 * b + 32, :], ownT[:, 32 * b:32 * b + 32],
                                                    vt[0:32, 4, :], start=False, stop=True, tile_position=(0, 32 * b),
                                                    skip_group_check=True)
                        last.then_inc(pvd, 1)
                        pe.wait_ge(oh_r, G + 1)
                        for c in range(4):
                            last = nc.tensor.matmul(pw[:, 128 + 16 * c:144 + 16 * c], Oh[:, c * 128:(c + 1) * 128],
                                                    C("sumh"), start=True, stop=True)
                        last.then_inc(o_t, 1)

        @block.scalar
        def _(act):
            def keys(G):
                for pq in range(4):
                    for b in range(4):
                        nk = 16 * G + 4 * pq + b
                        if nk >= 4:
                            act.wait_ge(scored, G * 5 + pq)
                        for c in range(2):
                            act.wait_ge(k_T, 4 * nk + BANKS.index(c) + 1)
                            nc.scalar.activation(KT[b][:, c, :], ptk[c][:, :], ACT.Copy).then_inc(kcp, 1)

            def exps(G):
                act.wait_ge(soft, G + 1)
                nc.scalar.activation(Ss[G][:, :], Ss[G][:, :], ACT.Exp, bias=nb[:, G:G + 1], scale=scale,
                                     accum_out=den[:, G:G + 1]).then_inc(exs, 1)

            def probs(G):
                for q in range(4):
                    act.wait_ge(pT, 4 * G + q + 1)
                    if G and q == 0:
                        act.wait_ge(pvd, G)
                    nc.scalar.activation(PT[:, 4 * q:4 * q + 4, :].rearrange("p r n -> p (r n)"), ptk[q][:, :],
                                         ACT.Copy).then_inc(pTc, 1)
                act.wait_ge(ownTr, G + 1)
                nc.scalar.activation(ownT[:, :], pw[0:32, 0:128], ACT.Copy).then_inc(ownc, 1)

            keys(0)
            exps(0)
            keys(1)
            exps(1)
            probs(0)
            probs(1)

        @block.vector
        def _(dve):
            c, V = Count(dve, dv), nc.vector
            lt8 = C("lt8").rearrange("p (n m) -> p n m", n=8)

            def keys(G):
                for pq in range(4):
                    ns = G * 5 + pq
                    for b in range(4):
                        nk = 16 * G + 4 * pq + b
                        if nk >= 4:
                            dve.wait_ge(scored, ns)
                        for f in (2, 3):
                            dve.wait_ge(k_T, 4 * nk + BANKS.index(f) + 1)
                            V.tensor_copy(KT[b][:, f, :], ptk[f][:, :]).then_inc(kcp2, 1)
                    dve.wait_ge(scored, ns + 1)
                    V.tensor_copy(Ss[G][:, 512 * pq:512 * pq + 512], pss[ns % 2][:, :]).then_inc(sccp, 1)
                    dve.wait_ge(sccp, ns + 1)
                    sv = Ss[G][:, 512 * pq:512 * pq + 512].rearrange("p (r b x) -> p b r x", r=4, b=2)
                    c.step(V.tensor_reduce(gs[:, 2 * pq:2 * pq + 2], sv, AX.XY, ALU.add))

            def penalties(G):
                S, ns = Ss[G], 5 * G + 4
                dve.wait_ge(scored, ns + 1)
                V.tensor_tensor(S[:, 2048:2052], pss[ns % 2][:, 0:NS], C("ownneg"), ALU.add).then_inc(sccp, 1)
                rank(V, c, rk[:, :], gs[:, :], gt8[:, :, :], eq8[:, :, :], lt8)
                c.step(V.tensor_scalar(pen[:, :], rk[:, :], 2.5, NEG, ALU.is_gt, ALU.mult))
                for q in range(4):
                    for bl in range(2):
                        v3 = S[:, 512 * q:512 * q + 512].rearrange("p (r b x) -> p b r x", r=4, b=2)[:, bl, :, :]
                        c.add(V.tensor_scalar(v3, v3, pen[:, 2 * q + bl:2 * q + bl + 1], None, ALU.add))
                c.wait()
                dve.wait_ge(sccp, ns + 1)
                c.step(V.reduce_max(nb[:, G:G + 1], S[:, :], AX.X))
                V.tensor_scalar(nb[:, G:G + 1], nb[:, G:G + 1], -scale, None, ALU.mult).then_inc(soft, 1)

            def outputs(G):
                dve.wait_ge(exs, G + 1)
                c.add(V.reciprocal(den[:, G:G + 1], den[:, G:G + 1]))
                V.tensor_tensor(own[:, :].rearrange("p (b k) -> p b k", k=NS),
                                Ss[G][:, 2048:2052].unsqueeze(1).to_broadcast([128, NB, NS]),
                                C(f"ownb{G}").rearrange("p (b k) -> p b k", k=NS), ALU.mult).then_inc(ownr, 1)
                c.wait()
                c.step(V.tensor_scalar(wh, C("hmask"), den[:, G:G + 1], None, ALU.mult))
                dve.wait_ge(pvd, G + 1)
                V.tensor_tensor(Oh.rearrange("p (h d) -> p h d", h=8), po[:, :].rearrange("p (h d) -> p h d", h=8),
                                wh.unsqueeze(2).to_broadcast([128, 8, 64]), ALU.mult).then_inc(oh_r, 1)
                dve.wait_ge(o_t, G + 1)
                V.tensor_copy(mixT[:, 4:8, 512 + 16 * G:528 + 16 * G],
                              pw[:, 128:192].rearrange("p (f n) -> p f n", f=4)).then_inc(o_c, 1)

            c.step(V.memset(Q[:, :, :, :], 0.0))
            for f in range(4):
                for h in range(2):
                    r = slice(64 * h, 64 * h + 64)
                    last = V.tensor_copy(Q[r, :, f, 4 * (2 * f + h):4 * (2 * f + h) + 4],
                                         qkT[r, f, 512:544].rearrange("p (b s) -> p b s", s=NS))
            last.then_inc(q_r, 1)
            for G in range(2):
                keys(G)
                penalties(G)
            for G in range(2):
                outputs(G)


IN = ["x_prompt", "x_sample", "state_gla", "state_ssm", "state_conv", "state_pool", "cache_k", "cache_v",
      "page_table", "ab_w_in", "ab_w_gate2", "ab_b_gate", "ab_gla_norm", "ab_conv_w", "ab_conv_b", "ab_dt_bias",
      "ab_a_log", "ab_d_skip", "ab_ssm_norm", "ab_w_out", "cd_w_in", "cd_w_pool", "cd_pool_scale", "cd_w_out",
      "moe_w_coarse", "moe_b_coarse", "moe_w_fine", "moe_b_fine", "moe_w_gate_up", "moe_w_down", "ln_g", "ln_b"]
OUT = [("y_p", (1, SEQ, D)), ("y_s", (NB, NS, D)), ("gla_p", (1, 4, 64, 128)), ("ssm_p", (1, 8, 64, 64)),
       ("conv_p", (1, 3, 768)), ("pool_p", (1, PBUF, 512)), ("k_p", (1, SEQ, 8, 64)), ("v_p", (1, SEQ, 8, 64)),
       ("gla_s", (NB, 4, 64, 128)), ("ssm_s", (NB, 8, 64, 64)), ("conv_s", (NB, 3, 768)),
       ("pool_s", (NB, PBUF, 512)), ("k_s", (NB, NS, 8, 64)), ("v_s", (NB, NS, 8, 64))]


def clear_rows(nc, yo, yd, cleared):
    with Scope(nc, "clear") as s:
        zeros = s.sem("zeros")
        block = s.block()

        @block.vector
        def _(dve):
            nc.vector.memset(yo[:, 0, :], 0.0).then_inc(zeros, 1)

        @block.sync
        def _(sp):
            sp.wait_ge(zeros, 1)
            for i in range((NROW - NE * SLOT) // 128):
                at = NE * SLOT + 128 * i
                sp.dma_start(yd[at:at + 128, :], yo[:, 0, :]).then_inc(cleared, 16)


def build(nc, A, cols, ncols):
    xd = nc.dram_tensor("token_rows", [NTOK, D], F32).ap()
    yd = nc.dram_tensor("expert_rows", [NROW, D], F32).ap()
    cleared = nc.alloc_semaphore("extra_rows_cleared")
    names = [f"{n}_stored" for n in ("abg", "abc", "abd", "pl", "n11")] + [f"cache_loaded{i}" for i in range(Cache.RING)]
    for l in range(2):
        names += [f"{n}{l}_rows{i}" for n in "efg" for i in range(2)]
        names += [f"{n}{l}_gathered{i}" for n in "fg" for i in range(3)] + [f"n{l}1_y_in{i}" for i in range(5)]
    Scope.used, Scope.kept = [], {n: nc.alloc_semaphore(n) for n in names}
    with Scope(nc, "top") as S:
        X = S.sb("X", [128, 5, D])
        consts = S.sb("consts", [128, ncols])
        xT = S.sb("xT", [128, KD, NTOK])
        wr = [S.sb(f"wr{l}", [128, KD, 36]) for l in range(2)]
        br = [S.sb(f"br{l}", [128, 36]) for l in range(2)]
        lg = S.sb("lg", [128, 5, 36])

        def C(name):
            return consts[:, cols[name][0]:cols[name][1]]

        pages = S.sb("pages", [128, NB * NPG // 4], I32)

        with Scope(nc, "in") as s:
            table = s.sb("table", [128, NB * NPG], I32)
            quads = s.sb("quads", [128, NB * NPG // 4])
            loaded, routers, paged, dv = (s.sem(x) for x in ("loaded", "routers", "paged", "dve_steps"))
            block = s.block()

            @block.sync
            def _(sp):
                sp.dma_start(table[:, :], A["page_table"].rearrange("b n -> (b n)").partition_broadcast(128))\
                  .then_inc(paged, 16)
                sp.dma_start(consts[:, :], A["consts"]).then_inc(paged, 16)
                for t in range(4):
                    sp.dma_start(X[:, t, :], A["x_prompt"][0, tok0(t):tok0(t) + 128, :]).then_inc(loaded, 16)
                sp.dma_start(X[0:32, 4, :], A["x_sample"].rearrange("b s d -> (b s) d")).then_inc(loaded, 16)
                for l in range(2):
                    sp.dma_start(wr[l][:, :, 0:4], A["moe_w_coarse"][l].rearrange("(k p) g -> p k g", p=128))\
                      .then_inc(routers, 16)
                    for g in range(4):
                        sp.dma_start(wr[l][:, :, 4 + 8 * g:12 + 8 * g],
                                     A["moe_w_fine"][l, g].rearrange("(k p) e -> p k e", p=128)).then_inc(routers, 16)
                    sp.dma_start(br[l][:, 0:4], A["moe_b_coarse"][l].partition_broadcast(128)).then_inc(routers, 16)
                    sp.dma_start(br[l][:, 4:36], A["moe_b_fine"][l].rearrange("g e -> (g e)").partition_broadcast(128))\
                      .then_inc(routers, 16)
                sp.wait_ge(loaded, 16 * 5)
                sp.wait_ge(routers, 16 * 14)

            @block.vector
            def _(dve):
                c, V = Count(dve, dv), nc.vector
                dve.wait_ge(paged, 32)
                for g in range(4):
                    r = slice(32 * g, 32 * g + 32)
                    c.add(V.tensor_copy(quads[r, :], table[r, :].rearrange("p (n g) -> p n g", g=4)[:, :, g]))
                c.wait()
                c.step(V.tensor_scalar(quads[:, :], quads[:, :], 32.0, C("p32"), ALU.mult, ALU.add))
                c.step(V.tensor_copy(pages[:, :], quads[:, :]))

        transpose_stage(nc, "xt", C, X, xT)
        for l in range(2):
            if l == 0:
                with Scope(nc, "mix") as s:
                    yo = s.sb("yo", [128, 5, 1024])
                    clear_rows(nc, yo, yd, cleared)
                    mixer_ab(nc, A, C, xT, yo, cleared)
                    transpose_stage(nc, "abt", C, yo, xT)
            else:
                reset_stage(nc)
                mixer_cd(nc, A, C, xT, pages)
            reset_stage(nc)
            with Scope(nc, f"m{l}") as M:
                E = Experts(nc, A, M, l)
                finish_stage(nc, f"n{l}0", C, X, A["ln_g"][l, 0], A["ln_b"][l, 0],
                             proj=(xT, A["cd_w_out" if l else "ab_w_out"]), xT=xT, router=(wr[l], br[l], lg), rows=xd,
                             ahead=E)
                route(nc, f"r{l}", C, lg, xT, E)
                expert_stage(nc, f"e{l}", C, E, xT, xd, yd, range(NE // 2))
                expert_stage(nc, f"f{l}", C, E, xT, xd, yd, range(NE // 2, NE // 2 + 1))
                expert_stage(nc, f"g{l}", C, E, xT, xd, yd, range(NE // 2 + 1, NPAIR))
                finish_stage(nc, f"n{l}1", C, X, A["ln_g"][l, 1], A["ln_b"][l, 1],
                             experts=(yd, E), xT=None if l else xT,
                             out=(A["y_p"], A["y_s"]) if l else None)


def kernel(**inputs):
    import concourse.bacc as bacc
    import concourse.bass_utils as bass_utils

    nc = bacc.Bacc("TRN2", target_bir_lowering=False, num_devices=1)
    table, cols = constants()
    arrays = {n: np.ascontiguousarray(inputs[n]) for n in IN}
    arrays["consts"] = table
    A = {}
    feed = {}
    for n, a in arrays.items():
        A[n] = nc.dram_tensor("in_" + n, a.shape, mybir.dt.from_np(a.dtype), kind="ExternalInput").ap()
        feed["in_" + n] = a
    for n, shape in OUT:
        A[n] = nc.dram_tensor("out_" + n, shape, F32, kind="ExternalOutput").ap()
    build(nc, A, cols, table.shape[1])
    r = bass_utils.run_bass_kernel_spmd(nc, [feed], core_ids=[0])
    return tuple(r.results[0]["out_" + n] for n, _ in OUT)
```

```python
from contextlib import ExitStack

import numpy as np

import concourse.bass as bass
from concourse import mybir

F32 = mybir.dt.float32
I32 = mybir.dt.int32
ALU = mybir.AluOpType
ACT = mybir.ActivationFunctionType
AX = mybir.AxisListType

D = 1024
KD = D // 128
SEQ, NB, NS = 512, 8, 4
NTOK = SEQ + NB * NS
TILES = [(t, 128) for t in range(4)] + [(4, NB * NS)]
ORDER = TILES[4:] + TILES[:4]
ALPHA = 4 ** 0.25
LN_EPS, RMS_EPS = 1e-5, 1e-6
PAST, PAGE, NPG = 2048, 128, 16
WINDOWS = (2, 4, 8, 16)
PBUF = 15
NEG = -1e30
NE, SLOT, DE = 32, 64, 256
NPAIR = (NE + (2 * NTOK - NE) // SLOT + 1) // 2
NTILE = 2 * NPAIR
NROW = NTILE * SLOT


def constants():
    p = np.arange(128)
    j, i = p[:, None], p[None, :]
    parts = {}
    parts["ident"] = np.eye(128)
    for name, c in (("p", 64), ("s", NS)):
        same = j // c == i // c
        parts["tri_" + name] = same & (j <= i)
        parts["suf_" + name] = same & (j > i)
        parts["neg_" + name] = np.where(same & (j <= i), 0.0, NEG)
    parts["ones"] = np.ones((128, 128))
    parts["before"] = j < i
    parts["causal"] = np.where(i <= j, 0.0, NEG)
    parts["cmask"] = p[:, None] // 64 == np.arange(2)
    parts["bmask"] = p[:, None] // NS == np.arange(NB)
    parts["lt8"] = np.broadcast_to((np.arange(8)[:, None] > np.arange(8)[None, :]).reshape(1, 64), (128, 64))
    cnt = np.zeros((4, 16))
    for g, w in enumerate(WINDOWS):
        cnt[g, :PBUF] = 1.0 / np.minimum(w, np.arange(PBUF) + 1)
    parts["invcnt"] = np.broadcast_to(cnt.reshape(1, 64), (128, 64))
    parts["pidx"] = p[:, None]
    parts["p32"] = p[:, None] % 32
    parts["iota"] = np.broadcast_to(p[None, :], (128, 128))
    parts["m128"] = np.broadcast_to(128 * np.arange(NPAIR + 1)[None, :], (128, NPAIR + 1))
    tok = p[:, None] + 128 * np.arange(5)
    parts["valid"] = tok < NTOK
    parts["tokid"] = np.where(tok < NTOK, tok, 0)
    parts["m64"] = np.broadcast_to(SLOT * np.arange(1, 9)[None, :], (128, 8))
    parts["e64"] = np.broadcast_to(SLOT * np.arange(NE)[None, :], (128, NE))
    parts["tile"] = np.broadcast_to(np.arange(NTILE - NE)[None, :], (128, NTILE - NE))
    parts["ownneg"] = np.where(np.arange(NS)[None, :] <= p[:, None] % NS, 0.0, NEG)
    for g in range(2):
        parts[f"ownb{g}"] = np.repeat(p[:, None] // 32 + 4 * g == np.arange(NB)[None, :], NS, axis=1)
    parts["hmask"] = (p[:, None] // NS) % 8 == np.arange(8)
    parts["sumh"] = ((p[:, None] // 32) * NS + p[:, None] % NS) == np.arange(16)[None, :]
    half = 8
    inv = (np.float32(500000.0) ** (-np.arange(half, dtype=np.float32) / np.float32(half))).astype(np.float32)
    pos = np.concatenate([np.arange(SEQ), PAST + np.tile(np.arange(NS), NB), np.zeros(96)]).astype(np.float32)
    ang = (pos[:, None] * inv[None, :]).astype(np.float32)
    rope = np.concatenate([np.cos(ang), np.sin(ang)], axis=1).astype(np.float32)
    parts["rope"] = rope.reshape(5, 128, 16).transpose(1, 0, 2).reshape(128, 80)
    at, cols, out = 0, {}, []
    for name, a in parts.items():
        a = np.asarray(a, np.float32).reshape(128, -1)
        cols[name] = (at, at + a.shape[1])
        at += a.shape[1]
        out.append(a)
    return np.ascontiguousarray(np.concatenate(out, axis=1)), cols


class Count:

    def __init__(self, eng, sem):
        self.eng, self.sem, self.n = eng, sem, 0

    def add(self, ins):
        ins.then_inc(self.sem, 1)
        self.n += 1

    def wait(self):
        self.eng.wait_ge(self.sem, self.n)

    def step(self, ins):
        self.add(ins)
        self.wait()


class Scope(ExitStack):
    used, kept = [], {}

    def __init__(self, nc, name):
        super().__init__()
        self.nc, self.name = nc, name

    def sb(self, name, shape, dt=F32):
        return self.enter_context(self.nc.sbuf_tensor(f"{self.name}_{name}", shape, dt))

    def ps(self, name, cols=512):
        return self.enter_context(self.nc.psum_tensor(f"{self.name}_psum_{name}", [128, cols], F32))

    def sem(self, name):
        if f"{self.name}_{name}" in self.kept:
            return self.kept[f"{self.name}_{name}"]
        sem = self.enter_context(self.nc.semaphore(f"{self.name}_{name}"))
        self.used.append(sem.num)
        return sem

    def block(self):
        return self.enter_context(self.nc.Block())


def tok0(t):
    return 128 * t


def reset_stage(nc):
    nums, Scope.used = sorted(set(Scope.used)), []
    with Scope(nc, "reset") as s:
        block = s.block()

        @block.sync
        def _(sp):
            start = nums[0]
            for a, b in zip(nums, nums[1:] + [None]):
                if b != a + 1:
                    sp.sem_clear(range(start, a + 1))
                    start = b


def transpose_stage(nc, name, C, src, dst, chunks=KD):
    units = [(t, P, h) for t, P in TILES for h in range(chunks // 4)]
    with Scope(nc, name) as s:
        ps = [s.ps(f"p{i}") for i in range(4)]
        transposed, by_act, by_dve = s.sem("transposed"), s.sem("by_act"), s.sem("by_dve")
        block = s.block()

        @block.tensor
        def _(pe):
            for u, (t, P, h) in enumerate(units):
                if u >= 4:
                    pe.wait_ge(by_dve if u % 2 else by_act, u // 2 - 1)
                for c in range(4):
                    last = nc.tensor.transpose(ps[u % 4][:, c * P:(c + 1) * P],
                                               src[:P, t, (4 * h + c) * 128:(4 * h + c + 1) * 128],
                                               C("ident")[:P, :P])
                last.then_inc(transposed, 1)

        def out_in(u):
            t, P, h = units[u]
            return (dst[:, 4 * h:4 * h + 4, tok0(t):tok0(t) + P],
                    ps[u % 4][:, :4 * P].rearrange("p (c n) -> p c n", c=4))

        @block.scalar
        def _(act):
            for u in range(0, len(units), 2):
                act.wait_ge(transposed, u + 1)
                o, i = out_in(u)
                nc.scalar.activation(o, i, ACT.Copy).then_inc(by_act, 1)

        @block.vector
        def _(dve):
            for u in range(1, len(units), 2):
                dve.wait_ge(transposed, u + 1)
                o, i = out_in(u)
                nc.vector.tensor_copy(o, i).then_inc(by_dve, 1)


def sum_in_quarters(nc, out, N, lhsT, rhs):
    w = N // 4
    for k in range(KD):
        for q in range(4):
            last = nc.tensor.matmul(out[32 * q:32 * q + 32, 0:w], lhsT(k), rhs(k)[:, q * w:(q + 1) * w],
                                    start=(k == 0), stop=(k == KD - 1), tile_position=(0, 32 * q))
    return last


class Job:

    def __init__(self, piece, M, N, lhsT, rhs, by, copy, emit=None, after=()):
        self.emit, self.after = emit, after
        self.piece, self.M, self.N, self.lhsT, self.rhs, self.by, self.copy = piece, M, N, lhsT, rhs, by, copy
        self.quarters = M == 32 and N == 512 and not emit

    def copied(self, ps):
        if not self.quarters:
            return self.copy(ps[:self.M, :self.N], slice(0, self.N))
        for q in range(4):
            last = self.copy(ps[32 * q:32 * q + 32, 0:128], slice(128 * q, 128 * q + 128))
        return last


def project_stage(nc, name, w_dram, pieces, width, xT, jobs_of, nbuf=3, ahead=None, store=None, act_at={}, dve_at={}):
    with Scope(nc, name) as s:
        ring = [s.sb(f"w{i}", [128, KD, width]) for i in range(nbuf)]
        ps = [s.ps(f"p{i}") for i in range(8)]
        loaded = [s.sem(f"loaded{i}") for i in range(nbuf)]
        summed, by_act, by_dve = s.sem("summed"), s.sem("by_act"), s.sem("by_dve")
        jobs = [j for n in range(len(pieces)) for j in jobs_of(n, ring[n % nbuf])]
        done = {"act": by_act, "dve": by_dve}
        last_of = [max(i for i, j in enumerate(jobs) if j.piece == n) for n in range(len(pieces))]

        def wait_copied(eng, i):
            by = jobs[i].by
            eng.wait_ge(done[by], sum(q.by == by for q in jobs[:i + 1]))

        block = s.block()

        if ahead:
            @block.gpsimd
            def _(pool):
                ahead(pool)

        @block.sync
        def _(sp):
            for n, (a, b) in enumerate(pieces):
                if n >= nbuf:
                    sp.wait_ge(summed, last_of[n - nbuf] + 1)
                sp.dma_start(ring[n % nbuf][:, :, 0:b - a],
                             w_dram.rearrange("(k p) n -> p k n", p=128)[:, :, a:b]).then_inc(loaded[n % nbuf], 16)
            if store:
                store(sp, lambda i: wait_copied(sp, i))

        @block.tensor
        def _(pe):
            for i, j in enumerate(jobs):
                if i == 0 or jobs[i - 1].piece != j.piece:
                    pe.wait_ge(loaded[j.piece % nbuf], 16 * (j.piece // nbuf + 1))
                if i >= 8:
                    wait_copied(pe, i - 8)
                for needed in j.after:
                    wait_copied(pe, needed)
                if j.emit:
                    last = j.emit(ps[i % 8])
                elif j.quarters:
                    last = sum_in_quarters(nc, ps[i % 8], j.N, j.lhsT, j.rhs)
                else:
                    for k in range(KD):
                        last = nc.tensor.matmul(ps[i % 8][:j.M, :j.N], j.lhsT(k), j.rhs(k),
                                                start=(k == 0), stop=(k == KD - 1))
                last.then_inc(summed, 1)

        @block.scalar
        def _(act):
            for i, j in enumerate(jobs):
                if j.by == "act":
                    act.wait_ge(summed, i + 1)
                    j.copied(ps[i % 8]).then_inc(by_act, 1)
                if i in act_at:
                    act_at[i](act, lambda needed: wait_copied(act, needed))

        @block.vector
        def _(dve):
            for i, j in enumerate(jobs):
                if j.by == "dve":
                    dve.wait_ge(summed, i + 1)
                    j.copied(ps[i % 8]).then_inc(by_dve, 1)
                if i in dve_at:
                    dve_at[i](dve, lambda needed: wait_copied(dve, needed))


def finish_stage(nc, name, C, X, lng, lnb, proj=None, experts=None, xT=None, router=None, rows=None, out=None,
                 ahead=None):
    with Scope(nc, name) as s:
        gb = s.sb("gb", [128, 2, D])
        st, mv = s.sb("st", [128, 5, 2, 6]), s.sb("mv", [128, 5, 2])
        rstd, nmr = s.sb("rstd", [128, 5]), s.sb("nmr", [128, 5])
        if proj:
            mixT, w_dram = proj
            w = ahead.w_out
            pp = [s.ps(f"p{i}") for i in range(4)]
        else:
            y_dram, E = experts
            y = [w[:, 0:2 * D].rearrange("p (k n) -> p k n", k=2) for w in E.wg[0:5]]
            weighed = s.sem("weighed")
        if xT is not None:
            pt = [s.ps(f"t{i}") for i in range(2)]
        if router:
            wr, br, lg = router
            pl = [s.ps(f"l{i}") for i in range(2)]
        (gb_in, summed, added, dv, var_in, root, mean_in, normed, final, T_in, T_out, logits, logit_c) = (
            s.sem(x) for x in ("gb_in", "summed", "added", "dve_steps", "var_in", "root", "mean_in", "normed",
                               "final", "T_in", "T_out", "logits", "logits_copied"))
        w_in = [s.sem(f"w_in{h}") for h in range(2)] if proj else None
        y_in = [s.sem(f"y_in{i}") for i in range(5)] if experts else None
        stored = s.sem("stored") if out else s.sem("rows_stored")
        block = s.block()

        @block.sync
        def _(sp):
            if proj:
                for h in range(2):
                    sp.dma_start(w[h][:, :, :], w_dram.rearrange("(k p) n -> p k n", p=128)[:, :, 512 * h:512 * h + 512])\
                      .then_inc(w_in[h], 16)
            sp.dma_start(gb[:, 0, :], lng.partition_broadcast(128)).then_inc(gb_in, 16)
            sp.dma_start(gb[:, 1, :], lnb.partition_broadcast(128)).then_inc(gb_in, 16)
            if ahead:
                ahead.fill(sp, range(ahead.RING - 1))
            for i, (t, P) in enumerate(ORDER):
                if ahead and i == 3:
                    sp.wait_ge(summed, 5)
                    ahead.fill(sp, range(ahead.RING - 1, ahead.RING))
                if rows is not None:
                    sp.wait_ge(final, i + 1)
                    sp.dma_start(rows[tok0(t):tok0(t) + P, :], X[:P, t, :]).then_inc(stored, 16)
                elif out:
                    sp.wait_ge(final, i + 1)
                    dst = out[0][0, tok0(t):tok0(t) + P, :] if t < 4 else out[1].rearrange("b s d -> (b s) d")
                    sp.dma_start(dst, X[:P, t, :]).then_inc(stored, 16)
            if rows is not None or out:
                sp.wait_ge(stored, 16 * 5)

        if experts:
            @block.gpsimd
            def _(pool):
                for t, P in ORDER:
                    for k in range(2):
                        nc.gpsimd.indirect_dma_start(out=y[t][:P, k, :], out_offset=None, in_=y_dram,
                                                     in_offset=bass.IndirectOffsetOnAxis(ap=E.posi[:P, k, t:t + 1], axis=0))\
                            .then_inc(y_in[t], 16)

        if proj or xT is not None:
            @block.tensor
            def _(pe):
                def project(i, t, P):
                    if i >= 2:
                        pe.wait_ge(added, i - 1)
                    for h in range(2):
                        if i == 0:
                            pe.wait_ge(w_in[h], 16)
                        if t == 4:
                            last = sum_in_quarters(nc, pp[h], 512, lambda k: mixT[:, k, 512:544],
                                                   lambda k: w[h][:, k, :])
                            continue
                        for k in range(KD):
                            last = nc.tensor.matmul(pp[2 * (i % 2) + h][:P, :], mixT[:, k, tok0(t):tok0(t) + P],
                                                    w[h][:, k, :], start=(k == 0), stop=(k == KD - 1))
                    last.then_inc(summed, 1)

                def flip(i, t, P):
                    pe.wait_ge(final, i + 1)
                    if i >= 1:
                        pe.wait_ge(T_out, i)
                    for c in range(KD):
                        last = nc.tensor.transpose(pt[c // 4][:, (c % 4) * P:(c % 4 + 1) * P],
                                                   X[:P, t, c * 128:(c + 1) * 128], C("ident")[:P, :P])
                    last.then_inc(T_in, 1)

                def route(i, t, P):
                    pe.wait_ge(T_out, i + 1)
                    if i >= 2:
                        pe.wait_ge(logit_c, i - 1)
                    for k in range(KD):
                        last = nc.tensor.matmul(pl[i % 2][:P, 0:36], xT[:, k, tok0(t):tok0(t) + P], wr[:, k, :],
                                                start=(k == 0), stop=(k == KD - 1))
                    last.then_inc(logits, 1)

                for i in range(7):
                    if proj and i < 5:
                        project(i, *ORDER[i])
                    if xT is not None and 1 <= i <= 5:
                        flip(i - 1, *ORDER[i - 1])
                    if router and i >= 2:
                        route(i - 2, *ORDER[i - 2])

        @block.vector
        def _(dve):
            c, V = Count(dve, dv), nc.vector

            def add(i, t, P):
                x = X[:P, t, :]
                if proj:
                    dve.wait_ge(summed, i + 1)
                    for h in range(2):
                        sums = [(pp[2 * (i % 2) + h][:P, :], x[:, 512 * h:512 * h + 512])]
                        if t == 4:
                            sums = [(pp[h][32 * q:32 * q + 32, 0:128],
                                     x[:, 512 * h + 128 * q:512 * h + 128 * q + 128]) for q in range(4)]
                        for f, part in sums:
                            last = V.scalar_tensor_tensor(out=part, in0=part, scalar=ALPHA, in1=f,
                                                          op0=ALU.mult, op1=ALU.add)
                else:
                    y0, y1 = y[t][:P, 0, :], y[t][:P, 1, :]
                    dve.wait_ge(y_in[t], 32)
                    dve.wait_ge(weighed, i + 1)
                    c.step(V.scalar_tensor_tensor(out=y0, in0=y1, scalar=E.gate[:P, 1, t:t + 1], in1=y0,
                                                  op0=ALU.mult, op1=ALU.add))
                    last = V.scalar_tensor_tensor(out=x, in0=x, scalar=ALPHA, in1=y0, op0=ALU.mult, op1=ALU.add)
                last.then_inc(added, 1)
                dve.wait_ge(added, i + 1)
                for h in range(2):
                    c.add(V.bn_stats(st[:P, t, h, :], x[:, h * 512:(h + 1) * 512]))
                c.wait()
                c.step(V.bn_aggr(mv[:P, t, :], st[:P, t, :, :].rearrange("p a b -> p (a b)")))
                V.tensor_scalar(rstd[:P, t:t + 1], mv[:P, t, 1:2], LN_EPS, None, ALU.add).then_inc(var_in, 1)

            def scale(i, t, P):
                dve.wait_ge(root, i + 1)
                c.step(V.reciprocal(rstd[:P, t:t + 1], rstd[:P, t:t + 1]))
                V.tensor_scalar(nmr[:P, t:t + 1], mv[:P, t, 0:1], rstd[:P, t:t + 1], -1.0, ALU.mult, ALU.mult)\
                 .then_inc(mean_in, 1)

            def affine(i, t, P):
                dve.wait_ge(normed, i + 1)
                if i == 0:
                    dve.wait_ge(gb_in, 32)
                c.step(V.tensor_tensor(X[:P, t, :], X[:P, t, :], gb[:P, 0, :], ALU.mult))
                V.tensor_tensor(X[:P, t, :], X[:P, t, :], gb[:P, 1, :], ALU.add).then_inc(final, 1)

            def logit(i, t, P):
                dve.wait_ge(logits, i + 1)
                V.tensor_tensor(lg[:P, t, :], pl[i % 2][:P, 0:36], br[:P, :], ALU.add).then_inc(logit_c, 1)

            if router:
                c.step(V.memset(lg[:, :, :], 0.0))
            for i in range(6):
                if i < 5:
                    add(i, *ORDER[i])
                if experts and i >= 1:
                    affine(i - 1, *ORDER[i - 1])
                if i < 5:
                    scale(i, *ORDER[i])
                if proj and i < 5:
                    affine(i, *ORDER[i])
                if router and i >= 1:
                    logit(i - 1, *ORDER[i - 1])

        @block.scalar
        def _(act):
            def weigh(i, t, P):
                act.wait_ge(y_in[t], 32)
                nc.scalar.activation(y[t][:P, 0, :], y[t][:P, 0, :], ACT.Copy, scale=E.gate[:P, 0, t:t + 1])\
                  .then_inc(weighed, 1)

            if experts:
                weigh(0, *ORDER[0])
            for i in range(6):
                if experts and i < 4:
                    weigh(i + 1, *ORDER[i + 1])
                if i < 5:
                    t, P = ORDER[i]
                    act.wait_ge(var_in, i + 1)
                    nc.scalar.activation(rstd[:P, t:t + 1], rstd[:P, t:t + 1], ACT.Sqrt).then_inc(root, 1)
                    act.wait_ge(mean_in, i + 1)
                    nc.scalar.activation(X[:P, t, :], X[:P, t, :], ACT.Identity, bias=nmr[:P, t:t + 1],
                                         scale=rstd[:P, t:t + 1]).then_inc(normed, 1)
                if xT is not None and i >= 1:
                    t, P = ORDER[i - 1]
                    act.wait_ge(T_in, i)
                    for h in range(2):
                        last = nc.scalar.activation(xT[:, 4 * h:4 * h + 4, tok0(t):tok0(t) + P],
                                                    pt[h][:, :4 * P].rearrange("p (c n) -> p c n", c=4), ACT.Copy)
                    last.then_inc(T_out, 1)




class MixerInputs:

    def __init__(self, nc, A, s):
        self.convst = s.sb("convst", [NB * 3, 768])
        self.taps = s.sb("taps", [5, 768])
        self.wg2 = s.sb("wg2", [16, 256])
        self.bg = s.sb("bg", [128, 264])
        self.heads = s.sb("heads", [128, 16])
        self.norms = s.sb("norms", [128, 640])
        self.loads = [(self.convst[:, :], A["state_conv"].rearrange("b i n -> (b i) n")),
                      (self.taps[0:4, :], A["ab_conv_w"]),
                      (self.taps[4:5, :], A["ab_conv_b"].rearrange("(a n) -> a n", a=1)),
                      (self.wg2[:, :], A["ab_w_gate2"]),
                      (self.bg[:, 0:256], A["ab_b_gate"].partition_broadcast(128)),
                      (self.bg[:, 256:264], A["ab_dt_bias"].partition_broadcast(128)),
                      (self.heads[:, 0:8], A["ab_a_log"].partition_broadcast(128)),
                      (self.heads[:, 8:16], A["ab_d_skip"].partition_broadcast(128)),
                      (self.norms[:, 0:128], A["ab_gla_norm"].partition_broadcast(128)),
                      (self.norms[:, 128:640], A["ab_ssm_norm"].partition_broadcast(128))]


def mixer_ab(nc, A, C, xT, yo, yd, cleared, I):
    with Scope(nc, "ab") as L:
        v = L.sb("v", [128, 5, 512])
        rs = L.sb("rs", [128, 5, 512])
        zs = L.sb("zs", [128, 5, 512])
        qT = L.sb("qT", [128, 2, NTOK])
        kT = L.sb("kT", [128, 2, NTOK])
        soft = L.sb("soft", [128, 5, 264])
        xbcC = L.sb("xbcC", [128, 6, NTOK])
        las = L.sb("las", [128, 5, 8])
        lam = L.sb("lam", [128, 4, 2, 8])
        lams = L.sb("lams", [32, NB, 8])

        with Scope(nc, "abw") as W:
            xbcP = W.sb("xbcP", [128, 6, 3 + SEQ])
            xbcS = W.sb("xbcS", [128, 6, NB, 3 + NS])
            cw = W.sb("cw", [128, 6, 5])
            logit = W.sb("logit", [128, 5, 264])
            prepare_ab(nc, C, I, yo, xbcP, xbcS, cw, logit)
            project_ab(nc, A, C, W, xT, I, yo, yd, cleared, v, rs, zs, qT, kT, soft, xbcC, las, lam, lams,
                       xbcP, xbcS, cw, logit)

        with Scope(nc, "abz") as L2:
            scan_ab(nc, A, C, L2, xT, yo, cleared, v, rs, zs, qT, kT, soft, xbcC, las, lam, lams, I.heads, I.norms)


def prepare_ab(nc, C, I, yo, xbcP, xbcS, cw, logit):
    with Scope(nc, "abp") as s:
        pc = s.ps("pc")
        flipped, dv = s.sem("flipped"), s.sem("dve_steps")
        block = s.block()

        @block.tensor
        def _(pe):
            for f in range(6):
                nc.tensor.transpose(pc[:, f * 24:(f + 1) * 24], I.convst[:, f * 128:(f + 1) * 128],
                                    C("ident")[:24, :24])
                last = nc.tensor.transpose(pc[:, 144 + f * 5:149 + f * 5], I.taps[:, f * 128:(f + 1) * 128],
                                           C("ident")[:5, :5])
            last.then_inc(flipped, 1)

        @block.vector
        def _(dve):
            c, V = Count(dve, dv), nc.vector
            c.add(V.memset(yo[:, 0, :], 0.0))
            c.add(V.memset(xbcP[:, :, 0:3], 0.0))
            c.add(V.memset(logit[:, 4, :], 0.0))
            dve.wait_ge(flipped, 1)
            c.add(V.tensor_copy(cw[:, :, :], pc[:, 144:174].rearrange("p (f i) -> p f i", f=6)))
            c.step(V.tensor_copy(xbcS[:, :, :, 0:3], pc[:, 0:144].rearrange("p (f b i) -> p f b i", f=6, b=NB)))

        @block.scalar
        def _(act):
            nc.scalar.activation(I.heads[:, 0:8], I.heads[:, 0:8], ACT.Exp)


def project_ab(nc, A, C, W, xT, I, yo, yd, cleared, v, rs, zs, qT, kT, soft, xbcC, las, lam, lams, xbcP, xbcS, cw, logit):
    gT = W.sb("gT", [16, NTOK])
    ends = W.sb("ends", [128, 6, 3 + NB * 3])
    newst = W.sb("newst", [32, 2, 768])
    stored = W.kept["abi_stored"]
    dv, ac, ends_in, log_in = (W.sem(x) for x in ("dve_steps", "act_steps", "ends_ready", "log_ready"))
    pieces = [(2064, 2448), (2448, 2840), (1536, 2064), (0, 512), (512, 1024), (1024, 1536)]
    jobs = []
    at = {}

    def jobs_of(n, w):
        first = len(jobs)

        def feat(c0, M, prompt, sample, scale=1.0):
            jobs.append(Job(n, M, 512, lambda k: w[:, k, c0:c0 + M], lambda k: xT[:, k, 0:512], "act",
                            lambda p, cols: nc.scalar.activation(prompt, p, ACT.Copy, scale=scale)))
            jobs.append(Job(n, M, 32, lambda k: w[:, k, c0:c0 + M], lambda k: xT[:, k, 512:544], "dve",
                            lambda p, cols: nc.vector.tensor_scalar(
                                sample, p.rearrange("p (b s) -> p b s", s=NS) if len(sample.shape) == 3 else p,
                                scale, None, ALU.mult)))

        def tok(c0, N, dst, func=None, bias=None):
            for t, P in TILES:
                def copy(p, cols, t=t, P=P):
                    if func is not None:
                        return nc.scalar.activation(dst[:P, t, cols], p, func)
                    if bias is not None:
                        return nc.vector.tensor_tensor(dst[:P, t, cols], p, bias[:P, cols], ALU.add)
                    return nc.vector.tensor_copy(dst[:P, t, cols], p)
                jobs.append(Job(n, P, N, lambda k, t=t, P=P: xT[:, k, tok0(t):tok0(t) + P],
                                lambda k: w[:, k, c0:c0 + N], "dve" if func is None else "act", copy))

        if n < 2:
            for f in range(3):
                ff = 3 * n + f
                at["conv", ff] = len(jobs)
                feat(f * 128, 128, xbcP[:, ff, 3:515], xbcS[:, ff, :, 3:7])
            if n == 1:
                tok(384, 8, logit[:, :, 256:264], bias=I.bg[:, 256:264])
        elif n == 2:
            at["g"] = len(jobs)
            feat(0, 16, gT[:, 0:512], gT[:, 512:544])
            at["ends"] = len(jobs)
            for rows, c0, of in ((3, 0, 0), (24, 3, 1)):
                for h in range(2):
                    def flip(ps, rows=rows, c0=c0, h=h, of=of):
                        if (of, h) == (0, 0):
                            nc.tensor.wait_ge(ends_in, 1)
                        for f in range(3):
                            last = nc.tensor.transpose(ps[0:rows, f * 128:(f + 1) * 128],
                                                       ends[:, 3 * h + f, c0:c0 + rows], C("ident"))
                        return last
                    jobs.append(Job(n, rows, 384, None, None, "dve", lambda p, cols, rows=rows, h=h, of=of:
                                    nc.vector.tensor_copy(newst[0:rows, of, h * 384:(h + 1) * 384], p), emit=flip))
            tok(16, 512, zs, ACT.Silu)
            for t, P in TILES:
                jobs.append(Job(n, P, 256, None, None, "dve", lambda p, cols, t=t, P=P:
                                nc.vector.scalar_tensor_tensor(out=logit[:P, t, 0:256], in0=p, scalar=-1.0,
                                                               in1=I.bg[:P, 0:256], op0=ALU.mult, op1=ALU.subtract),
                                emit=lambda ps, t=t, P=P: nc.tensor.matmul(ps[:P, 0:256], gT[:, tok0(t):tok0(t) + P],
                                                                           I.wg2[:, :], start=True, stop=True),
                                after=(at["g"], at["g"] + 1)))
            at["logits"] = len(jobs) - 1
        elif n == 3:
            for f in range(2):
                feat(f * 128, 128, qT[:, f, 0:512], qT[:, f, 512:544], 64 ** -0.5)
                feat(256 + f * 128, 128, kT[:, f, 0:512], kT[:, f, 512:544])
        elif n == 4:
            tok(0, 512, v)
        else:
            tok(0, 512, rs, ACT.Silu)
        return jobs[first:]

    steps = {}

    def convolve(f):
        def run(dve, copied):
            c, V = steps.setdefault("dve", Count(dve, dv)), nc.vector
            copied(at["conv", f])
            copied(at["conv", f] + 1)
            outs = [(xbcC[:, f, 0:512], lambda i: xbcP[:, f, i:i + 512]),
                    (xbcC[:, f, 512:544].rearrange("p (b s) -> p b s", s=NS), lambda i: xbcS[:, f, :, i:i + NS])]
            for o, src in outs:
                c.add(V.tensor_scalar(o, src(0), cw[:, f, 0:1], cw[:, f, 4:5], ALU.mult, ALU.add))
            for i in range(1, 4):
                for o, src in outs:
                    dve.wait_ge(dv, c.n - 1)
                    c.add(V.scalar_tensor_tensor(out=o, in0=src(i), scalar=cw[:, f, i:i + 1], in1=o,
                                                 op0=ALU.mult, op1=ALU.add))
            if f == 5:
                c.wait()
                V.tensor_copy(ends[:, :, 0:3], xbcP[:, :, 512:515])
                V.tensor_copy(ends[:, :, 3:27].rearrange("p f (b i) -> p f b i", b=NB), xbcS[:, :, :, 4:7])\
                 .then_inc(ends_in, 1)
        return run

    def activate(act, copied):
        act.wait_ge(ends_in, 1)
        for f in range(6):
            nc.scalar.activation(xbcC[:, f, :], xbcC[:, f, :], ACT.Silu)

    def logs(act, copied):
        c = Count(act, ac)
        for i in range(at["logits"] - 4, at["logits"] + 1):
            copied(i)
        c.step(nc.scalar.activation(soft[:, :, :], logit[:, :, :], ACT.Abs))
        c.step(nc.scalar.activation(soft[:, :, :], soft[:, :, :], ACT.Exp, scale=-1.0))
        nc.scalar.activation(soft[:, :, :], soft[:, :, :], ACT.Ln, bias=1.0).then_inc(log_in, 1)

    def decays(dve, copied):
        c, V = steps["dve"], nc.vector
        dve.wait_ge(log_in, 1)
        c.step(V.scalar_tensor_tensor(out=soft[:, :, :], in0=logit[:, :, :], scalar=0.0, in1=soft[:, :, :],
                                      op0=ALU.max, op1=ALU.add))
        c.add(V.tensor_scalar(soft[:, :, 0:256], soft[:, :, 0:256], -1.0 / 16, None, ALU.mult))
        c.step(V.scalar_tensor_tensor(out=las[:, :, :], in0=soft[:, :, 256:264], scalar=-1.0,
                                      in1=I.heads[:, 0:8].unsqueeze(1).to_broadcast([128, 5, 8]),
                                      op0=ALU.mult, op1=ALU.mult))
        for cc in range(2):
            c.add(V.tensor_scalar(lam[:, :, cc, :], las[:, 0:4, :], C("cmask")[:, cc:cc + 1], None, ALU.mult))
        for b in range(NB):
            c.add(V.tensor_scalar(lams[:, b, :], las[0:32, 4, :], C("bmask")[0:32, b:b + 1], None, ALU.mult))

    def store(sp, copied):
        for i in range(4):
            copied(at["ends"] + i)
        sp.dma_start(A["conv_p"][0, :, :], newst[0:3, 0, :]).then_inc(stored, 16)
        sp.dma_start(A["conv_s"].rearrange("b i n -> (b i) n"), newst[0:24, 1, :]).then_inc(stored, 16)
        for row in range(NE * SLOT, NROW, 128):
            sp.dma_start(yd[row:row + 128, :], yo[:, 0, :]).then_inc(cleared, 16)
        sp.wait_ge(stored, 32)

    project_stage(nc, "abi", A["ab_w_in"], pieces, 528, xT, jobs_of, nbuf=2, store=store,
                  dve_at={3: convolve(0), 5: convolve(1), 7: convolve(2), 9: convolve(3), 11: convolve(4),
                          13: convolve(5), 36: decays},
                  act_at={23: activate, 33: logs})


def scan_ab(nc, A, C, L, xT, yo, cleared, v, rs, zs, qT, kT, soft, xbcC, las, lam, lams, heads, norms):
    eb = L.sb("eb", [128, 2, NTOK])
    kend = L.sb("kend", [128, 5, 256])
    xs = L.sb("xs", [128, 5, 512])
    btok = L.sb("btok", [128, 5, 128])
    xdd = L.sb("xdd", [128, 5, 512])
    ecum = L.sb("ecum", [128, 5, 16])
    elh = L.sb("elh", [128, 16, 4])
    ycs = L.sb("ycs", [128, 5, 512])
    G0 = L.sb("G0", [128, 2, NB, 128])
    raw = L.sb("raw", [128, NB, 2, 128])
    ld_g, ld_s = L.sem("ld_g"), L.sem("ld_s")
    ms = L.sb("ms", [128, 5, 5])
    sq = soft[:, :, :].rearrange("p t n -> p (t n)")[:, 0:512]
    BT, CT = xbcC[:, 4, :], xbcC[:, 5, :]

    def gate_y(c, V, t, P):
        y, x = yo[:P, t, 512:1024], xs[:P, t, :]
        x3 = x.rearrange("p (h d) -> p h d", h=8)
        c.add(V.tensor_tensor(x3, x3, heads[:P, 8:16].unsqueeze(2).to_broadcast([P, 8, 64]), ALU.mult))
        c.step(V.tensor_tensor(y, y, ycs[:P, t, :], ALU.add))
        c.step(V.tensor_tensor(y, y, x, ALU.add))
        return V.tensor_tensor(y, y, zs[:P, t, :], ALU.mult)

    def square(t, P, a, b, col):
        return nc.scalar.activation(sq[:P, 0:b - a], yo[:P, t, a:b], ACT.Square, accum_out=ms[:P, t, col:col + 1])

    with Scope(nc, "abs") as s:
        enb = s.sb("enb", [128, 2, 128])
        qd, kd = qT, kT
        ncum = s.sb("ncum", [128, 8])
        esuf = s.sb("esuf", [128, 256])
        el = s.sb("el", [128, 64])
        xdts = [s.sb(f"xdt{i}", [128, 512]) for i in range(2)]
        W = s.sb("W", [128, 8, 128])
        At = s.sb("At", [128, 4, 128])
        pa, pb, px, pB, pr0, pr1, po, py = (s.ps(x) for x in ("pa", "pb", "px", "pB", "pr0", "pr1", "po", "py"))
        (based, summed, dv, exps, cneg, decayed, wexp, ready, att, masked, outs, copied) = (s.sem(x) for x in (
            "based", "summed", "dve_steps", "exps", "cneg", "decayed", "wexp", "ready", "att", "masked", "outs",
            "copied"))
        block = s.block()

        @block.sync
        def _(sp):
            for f in range(2):
                sp.dma_start(G0[:, f, :, :], A["state_gla"][:, 2 * f:2 * f + 2, :, :].rearrange("b h k v -> (h k) b v"))\
                  .then_inc(ld_g, 16)
            for g in range(2):
                for u in range(2):
                    h = 4 * g + 2 * u
                    sp.dma_start(raw[:, :, u, 64 * g:64 * g + 64],
                                 A["state_ssm"][:, h:h + 2, :, :].rearrange("b h p n -> (h p) b n")).then_inc(ld_s, 16)

        @block.tensor
        def _(pe):
            def base(t, P):
                m = "p" if t < 4 else "s"
                tri, suf = C("tri_" + m)[:P, :P], C("suf_" + m)[:P, :P]
                tk = slice(tok0(t), tok0(t) + P)
                if t:
                    pe.wait_ge(ready, t)
                for f in range(2):
                    nc.tensor.matmul(pa[:, f * 128:f * 128 + P], soft[:P, t, f * 128:(f + 1) * 128], tri,
                                     start=True, stop=True)
                nc.tensor.matmul(pa[:P, 256:512], suf, soft[:P, t, 0:256], start=True, stop=True)
                nc.tensor.matmul(pb[:P, 0:8], tri, las[:P, t, :], start=True, stop=True)
                nc.tensor.matmul(pb[:P, 8:16], suf, las[:P, t, :], start=True, stop=True)
                n = 16 if t < 4 else 64
                rhs = (lam[:, t, :, :] if t < 4 else lams[:, :, :]).rearrange("p c h -> p (c h)")
                nc.tensor.matmul(pb[:, 16:16 + n], C("ones")[:P, :], rhs, start=True, stop=True)
                for f in range(2):
                    nc.tensor.transpose(pb[:P, 256 + f * 128:256 + (f + 1) * 128], kT[:, f, tk], C("ident"))
                for f in range(4):
                    nc.tensor.transpose(px[:P, f * 128:(f + 1) * 128], xbcC[:, f, tk], C("ident"))
                nc.tensor.transpose(pB[:P, 256:384], BT[:, tk], C("ident")).then_inc(based, 1)

            def rows(t, P):
                m = "p" if t < 4 else "s"
                tri, neg = C("tri_" + m)[:P, :P], C("neg_" + m)[:P, :P]
                tk = slice(tok0(t), tok0(t) + P)
                if t:
                    pe.wait_ge(masked, t)
                for h in range(8):
                    pr = (pr0, pr1)[h // 4][:P, (h % 4) * 128:(h % 4) * 128 + P]
                    nc.tensor.matmul(pr, las[:P, t, h:h + 1].to_broadcast([P, P]), tri, start=True, stop=False)
                    nc.tensor.matmul(pr, C("ident")[:P, :P], neg, start=False, stop=True)
                pe.wait_ge(based, t + 1)
                pe.wait_ge(decayed, t + 1)
                if t:
                    pe.wait_ge(copied, t)
                for g in range(2):
                    last = nc.tensor.matmul((pB, po)[g][:P, 0:P], BT[64 * g:64 * g + 64, tk],
                                            CT[64 * g:64 * g + 64, tk], start=True, stop=True)
                last.then_inc(summed, 1)

            base(*TILES[0])
            rows(*TILES[0])
            for t, P in TILES:
                tk, xdt = slice(tok0(t), tok0(t) + P), xdts[t % 2]
                pe.wait_ge(wexp, t + 1)
                pe.wait_ge(decayed, t + 1)
                for h in range(4):
                    r = slice(64 * (h % 2), 64 * (h % 2) + 64)
                    last = nc.tensor.matmul((pr0, pr1)[h % 2][:P, (h // 2) * 128:(h // 2) * 128 + P],
                                            kd[r, h // 2, tk], qd[r, h // 2, tk],
                                            start=True, stop=True)
                last.then_inc(att, 1)
                if t < 4:
                    base(*TILES[t + 1])
                pe.wait_ge(ready, t + 1)
                pe.wait_ge(masked, t + 1)
                for h in range(4):
                    last = nc.tensor.matmul(po[:P, h * 128:(h + 1) * 128], At[:P, h, :P], v[:P, t, h * 128:(h + 1) * 128],
                                            start=True, stop=True)
                for h in range(8):
                    last = nc.tensor.matmul(py[:P, h * 64:(h + 1) * 64], W[:P, h, :P], xdt[:P, h * 64:(h + 1) * 64],
                                            start=True, stop=True)
                last.then_inc(outs, 1)
                if t < 4:
                    rows(*TILES[t + 1])

        @block.scalar
        def _(act):
            for t, P in TILES:
                tk = slice(tok0(t), tok0(t) + P)
                if t:
                    act.wait_ge(ready, t)
                act.wait_ge(based, t + 1)
                b = pa[:, 0:256].rearrange("p (f n) -> p f n", f=2)[:, :, :P]
                nc.scalar.activation(eb[:, :, tk], b, ACT.Exp)
                nc.scalar.activation(enb[:, :, :P], b, ACT.Exp, scale=-1.0)
                nc.scalar.activation(esuf[:P, :], pa[:P, 256:512], ACT.Exp)
                nc.scalar.activation(ecum[:P, t, :], pb[:P, 0:16], ACT.Exp)
                n = 16 if t < 4 else 64
                nc.scalar.activation(el[:, 0:n], pb[:, 16:16 + n], ACT.Exp).then_inc(exps, 1)
                act.wait_ge(summed, t + 1)
                act.wait_ge(cneg, t + 1)
                if t:
                    act.wait_ge(outs, t)
                for h in range(8):
                    last = nc.scalar.activation(W[:P, h, :P], (pr0, pr1)[h // 4][:P, (h % 4) * 128:(h % 4) * 128 + P],
                                                ACT.Exp, bias=ncum[:P, h:h + 1])
                last.then_inc(wexp, 1)

        @block.vector
        def _(dve):
            c = Count(dve, dv)
            dve.wait_ge(cleared, 16 * (NROW - NE * SLOT) // 128)
            c.add(nc.vector.memset(yo[:, 4, :], 0.0))
            c.step(nc.vector.memset(ycs[:, 4, :], 0.0))
            c.add(nc.vector.memset(xs[:, 4, :], 0.0))
            c.step(nc.vector.memset(ecum[:, 4, :], 0.0))

            def decay(t, P):
                tk, xdt = slice(tok0(t), tok0(t) + P), xdts[t % 2]
                dve.wait_ge(based, t + 1)
                c.add(nc.vector.tensor_copy(xs[:P, t, :], px[:P, :]))
                c.add(nc.vector.tensor_copy(btok[:P, t, :], pB[:P, 256:384]))
                c.wait()
                dt = soft[:P, t, 256:264].unsqueeze(2).to_broadcast([P, 8, 64])
                c.step(nc.vector.tensor_tensor(xdt[:P, :].rearrange("p (h d) -> p h d", h=8),
                                               xs[:P, t, :].rearrange("p (h d) -> p h d", h=8), dt, ALU.mult))
                dve.wait_ge(exps, t + 1)
                nc.vector.tensor_scalar(ncum[:P, :], pb[:P, 0:8], -1.0, None, ALU.mult).then_inc(cneg, 1)
                nc.vector.tensor_tensor(qd[:, :, tk], qT[:, :, tk], eb[:, :, tk], ALU.mult)
                nc.vector.tensor_tensor(kd[:, :, tk], kT[:, :, tk], enb[:, :, :P], ALU.mult).then_inc(decayed, 1)
                c.add(nc.vector.tensor_tensor(kend[:P, t, :], pb[:P, 256:512], esuf[:P, :], ALU.mult))
                c.add(nc.vector.tensor_tensor(xdd[:P, t, :].rearrange("p (h d) -> p h d", h=8),
                                              xdt[:P, :].rearrange("p (h d) -> p h d", h=8),
                                              ecum[:P, t, 8:16].unsqueeze(2).to_broadcast([P, 8, 64]), ALU.mult))
                for g in range(2):
                    n, at = (2, 2 * t) if t < 4 else (8, 8)
                    c.add(nc.vector.tensor_copy(elh[64 * g:64 * g + 64, at:at + n, :],
                                                el[64 * g:64 * g + 64, 0:8 * n]
                                                .rearrange("p (c h) -> p c h", h=8)[:, :, 4 * g:4 * g + 4]))

            decay(*TILES[0])
            for t, P in TILES:
                dve.wait_ge(wexp, t + 1)
                for g in range(2):
                    last = nc.vector.tensor_tensor(W[:P, 4 * g:4 * g + 4, :P], W[:P, 4 * g:4 * g + 4, :P],
                                                   (pB, po)[g][:P, 0:P].unsqueeze(1).to_broadcast([P, 4, P]),
                                                   ALU.mult)
                last.then_inc(ready, 1)
                dve.wait_ge(att, t + 1)
                m = C("tri_p" if t < 4 else "tri_s")[:P, :P].unsqueeze(1).to_broadcast([P, 2, P])
                for hh in range(2):
                    last = nc.vector.tensor_tensor(At[:P, :, :P].rearrange("p (f h) n -> p h f n", h=2)[:, hh, :, :],
                                                   (pr0, pr1)[hh][:P, 0:256].rearrange("p (h n) -> p h n", h=2)[:, :, :P],
                                                   m, ALU.mult)
                last.then_inc(masked, 1)
                if t < 4:
                    decay(*TILES[t + 1])
                dve.wait_ge(outs, t + 1)
                c.add(nc.vector.tensor_copy(yo[:P, t, 0:512], po[:P, :]))
                nc.vector.tensor_copy(yo[:P, t, 512:1024], py[:P, :]).then_inc(copied, 1)

    qd = qT
    with Scope(nc, "abc") as s:
        Sg = s.sb("Sg", [128, 9, 256])
        Ss = xT[:, :, :].rearrange("p k n -> p (k n)")[:, 0:9 * 256].rearrange("p (c n) -> p c n", c=9)
        stT = s.sb("stT", [128, 2, 128])
        pu = [s.ps(f"pu{i}") for i in range(4)]
        po = [s.ps(f"po{i}") for i in range(4)]
        upd, dv, states, inter, added, gated, squared, T_ready, T_done, stored = (s.sem(x) for x in (
            "upd", "dve_steps", "states", "inter", "added", "gated", "squared", "T_ready", "T_done", "stored"))
        block = s.block()

        @block.scalar
        def _(act):
            act.wait_ge(dv, 3)
            for t in range(4):
                act.wait_ge(added, 2 * t + 1)
                for h in range(4):
                    square(t, 128, 128 * h, 128 * h + 128, h).then_inc(squared, 1)
                    act.wait_ge(squared, 5 * t + h + 1)
                act.wait_ge(gated, t + 1)
                square(t, 128, 512, 1024, 4).then_inc(squared, 1)
                act.wait_ge(squared, 5 * t + 5)

        @block.tensor
        def _(pe):
            for ch in range(8):
                t, r = ch // 2, slice(64 * (ch % 2), 64 * (ch % 2) + 64)
                if ch >= 4:
                    pe.wait_ge(states, ch - 3)
                for h in range(4):
                    nc.tensor.matmul(pu[ch % 4][64 * (h % 2):64 * (h % 2) + 64, (h // 2) * 128:(h // 2) * 128 + 128],
                                     kend[r, t, h * 64:(h + 1) * 64], v[r, t, h * 128:(h + 1) * 128],
                                     start=True, stop=True)
                for g in range(2):
                    last = nc.tensor.matmul(pu[ch % 4][64 * g:64 * g + 64, 256:512], btok[r, t, g * 64:(g + 1) * 64],
                                            xdd[r, t, g * 256:(g + 1) * 256], start=True, stop=True)
                last.then_inc(upd, 1)
            for t in range(4):
                pe.wait_ge(states, 2 * t + 1)
                if t >= 1:
                    pe.wait_ge(added, 2 * t)
                for ch in (2 * t, 2 * t + 1):
                    o = slice(64 * (ch % 2), 64 * (ch % 2) + 64)
                    tk = slice(64 * ch, 64 * ch + 64)
                    for h in range(4):
                        r = slice(64 * (h % 2), 64 * (h % 2) + 64)
                        nc.tensor.matmul(po[h % 2][o, (h // 2) * 128:(h // 2 + 1) * 128], qd[r, h // 2, tk],
                                         Sg[r, ch, (h // 2) * 128:(h // 2) * 128 + 128], start=True, stop=True)
                    for g in range(2):
                        r = slice(64 * g, 64 * g + 64)
                        last = nc.tensor.matmul(po[2 + g][o, 0:256], CT[r, tk], Ss[r, ch, :],
                                                start=True, stop=True)
                last.then_inc(inter, 1)
            pe.wait_ge(states, 8)
            for u in range(2):
                last = nc.tensor.transpose(pu[0][:, u * 128:(u + 1) * 128], Ss[:, 8, u * 128:(u + 1) * 128], C("ident"))
            last.then_inc(T_ready, 1)

        @block.vector
        def _(dve):
            c = Count(dve, dv)
            c.add(nc.vector.memset(ms[:, :, :], 1.0))
            c.add(nc.vector.memset(Sg[:, 0, :], 0.0))
            c.step(nc.vector.memset(Ss[:, 0, :], 0.0))
            for ch in range(8):
                dve.wait_ge(upd, ch + 1)
                c.step(nc.vector.tensor_tensor(Ss[:, ch + 1, :].rearrange("p (h d) -> p h d", h=4),
                                               Ss[:, ch, :].rearrange("p (h d) -> p h d", h=4),
                                               elh[:, ch, :].unsqueeze(2).to_broadcast([128, 4, 64]), ALU.mult))
                c.add(nc.vector.tensor_tensor(Ss[:, ch + 1, :], Ss[:, ch + 1, :], pu[ch % 4][:, 256:512], ALU.add))
                for f in range(2):
                    col = slice(f * 128, f * 128 + 128)
                    last = nc.vector.scalar_tensor_tensor(out=Sg[:, ch + 1, col], in0=Sg[:, ch, col],
                                                          scalar=eb[:, f, 64 * ch + 63:64 * ch + 64],
                                                          in1=pu[ch % 4][:, col], op0=ALU.mult, op1=ALU.add)
                last.then_inc(states, 1)
                dve.wait_ge(states, ch + 1)
            for t in range(4):
                dve.wait_ge(inter, t + 1)
                for hh in range(2):
                    o3 = yo[:, t, 0:512].rearrange("p (f h d) -> p h f d", f=2, h=2)[:, hh, :, :]
                    last = nc.vector.tensor_tensor(o3, o3, po[hh][:, 0:256].rearrange("p (f d) -> p f d", f=2), ALU.add)
                last.then_inc(added, 1)
                for g in range(2):
                    last = nc.vector.tensor_tensor(
                        ycs[:, t, 256 * g:256 * g + 256].rearrange("p (h d) -> p h d", h=4),
                        po[2 + g][:, 0:256].rearrange("p (h d) -> p h d", h=4),
                        ecum[:, t, 4 * g:4 * g + 4].unsqueeze(2).to_broadcast([128, 4, 64]), ALU.mult)
                last.then_inc(added, 1)
                dve.wait_ge(added, 2 * t + 2)
                gate_y(c, nc.vector, t, 128).then_inc(gated, 1)
            dve.wait_ge(T_ready, 1)
            nc.vector.tensor_copy(stT[:, :, :], pu[0][:, 0:256].rearrange("p (u n) -> p u n", u=2)).then_inc(T_done, 1)

        @block.sync
        def _(sp):
            sp.wait_ge(states, 8)
            for f in range(2):
                sp.dma_start(A["gla_p"][0, 2 * f:2 * f + 2, :, :].rearrange("h k v -> (h k) v"),
                             Sg[:, 8, f * 128:(f + 1) * 128]).then_inc(stored, 16)
            sp.wait_ge(T_done, 1)
            for g in range(2):
                for u in range(2):
                    h = 4 * g + 2 * u
                    sp.dma_start(A["ssm_p"][0, h:h + 2, :, :].rearrange("h p n -> (h p) n"),
                                 stT[:, u, 64 * g:64 * g + 64]).then_inc(stored, 16)
            sp.wait_ge(stored, 16 * 6)

    with Scope(nc, "abd") as s:
        S0 = s.sb("S0", [128, NB, 256])
        vm = xT[0:32, :, 0:512]
        oTs = s.sb("oTs", [128, 4, 32])
        yTs = s.sb("yTs", [128, 4, 32])
        ps = [s.ps(f"p{i}") for i in range(8)]
        (gated, squared, tr, tr_out, vmask, inter, evac, back, added, upd, dv, new_g, new_s, xmask, trb, fin, stored,
         mm) = (s.sem(x) for x in (
             "gated", "squared", "tr", "tr_out", "vmask", "inter", "evac", "back", "added", "upd", "dve_steps", "new_g",
             "new_s", "xmask", "trb", "fin", "stored", "updated_s"))
        block = s.block()

        @block.sync
        def _(sp):
            sp.wait_ge(new_g, 1)
            for f in range(2):
                sp.dma_start(A["gla_s"][:, 2 * f:2 * f + 2, :, :].rearrange("b h k v -> (h k) b v"), G0[:, f, :, :])\
                  .then_inc(stored, 16)
            sp.wait_ge(fin, 4)
            for g in range(2):
                for u in range(2):
                    h = 4 * g + 2 * u
                    sp.dma_start(A["ssm_s"][:, h:h + 2, :, :].rearrange("b h p n -> (h p) b n"),
                                 raw[:, :, u, 64 * g:64 * g + 64]).then_inc(stored, 16)

        @block.scalar
        def _(act):
            act.wait_ge(gated, 1)
            for h in range(4):
                square(4, 32, 128 * h, 128 * h + 128, h).then_inc(squared, 1)
                act.wait_ge(squared, h + 1)
            square(4, 32, 512, 1024, 4)

        @block.tensor
        def _(pe):
            pe.wait_ge(ld_s, 64)
            for i in range(4):
                for b in (2 * i, 2 * i + 1):
                    for u in range(2):
                        last = nc.tensor.transpose(ps[i][:, (b % 2) * 256 + u * 128:(b % 2) * 256 + (u + 1) * 128],
                                                   raw[:, b, u, :], C("ident"))
                last.then_inc(tr, 1)
            pe.wait_ge(ld_g, 32)
            for h in range(4):
                r = slice(64 * (h % 2), 64 * (h % 2) + 64)
                for b in range(NB):
                    nc.tensor.matmul(ps[4 + h % 2][:, (h // 2) * 32 + 4 * b:(h // 2) * 32 + 4 * b + 4], G0[r, h // 2, b, :],
                                     qd[r, h // 2, 512 + 4 * b:516 + 4 * b], start=True, stop=True)
            pe.wait_ge(tr_out, 4)
            for j in range(4):
                r = slice(64 * (j // 2), 64 * (j // 2) + 64)
                for b in range(NB):
                    last = nc.tensor.matmul(ps[6 + j // 2][:, (j % 2) * 32 + 4 * b:(j % 2) * 32 + 4 * b + 4],
                                            S0[r, b, (j % 2) * 128:(j % 2) * 128 + 128],
                                            CT[r, 512 + 4 * b:516 + 4 * b], start=True, stop=True)
            last.then_inc(inter, 1)
            pe.wait_ge(evac, 1)
            for h in range(4):
                nc.tensor.matmul(ps[6][:32, h * 128:(h + 1) * 128], oTs[:, h, :], C("ident"), start=True, stop=True)
            for h in range(4):
                last = nc.tensor.matmul(ps[7][:32, h * 128:(h + 1) * 128], yTs[:, h, :], C("ident"),
                                        start=True, stop=True)
            last.then_inc(back, 1)
            pe.wait_ge(vmask, 1)
            for h in range(4):
                for q in range(2):
                    last = nc.tensor.matmul(ps[2 * (h // 2) + q][64 * (h % 2):64 * (h % 2) + 64, :],
                                            kend[:32, 4, h * 64:(h + 1) * 64],
                                            vm[:, 4 * q:4 * q + 4, h * 128:(h + 1) * 128], start=True, stop=True)
            last.then_inc(upd, 1)
            pe.wait_ge(xmask, 1)
            for g in range(2):
                for q in range(4):
                    last = nc.tensor.matmul(ps[4 + q][64 * g:64 * g + 64, :], btok[:32, 4, g * 64:(g + 1) * 64],
                                            vm[:, 2 * q:2 * q + 2, g * 256:(g + 1) * 256], start=True, stop=True)
            last.then_inc(mm, 1)
            pe.wait_ge(new_s, 1)
            for i in range(4):
                for b in (2 * i, 2 * i + 1):
                    for u in range(2):
                        last = nc.tensor.transpose(ps[i][:, (b % 2) * 256 + u * 128:(b % 2) * 256 + (u + 1) * 128],
                                                   S0[:, b, u * 128:(u + 1) * 128], C("ident"))
                last.then_inc(trb, 1)

        @block.vector
        def _(dve):
            c = Count(dve, dv)
            for b in range(NB):
                last = nc.vector.tensor_scalar(vm[:, b, :], v[:32, 4, :], C("bmask")[:32, b:b + 1], None, ALU.mult)
            last.then_inc(vmask, 1)
            for i in range(4):
                dve.wait_ge(tr, i + 1)
                nc.vector.tensor_copy(S0[:, 2 * i:2 * i + 2, :], ps[i][:, :].rearrange("p (b n) -> p b n", b=2))\
                  .then_inc(tr_out, 1)
            for o_gate, P, n in ((rs[:, 0:4, :], 128, 16), (rs[:32, 4:5, :], 32, 4)):
                g3 = o_gate.rearrange("p t (h d) -> p (t h) d", h=4)
                c.add(nc.vector.tensor_tensor(g3, g3, norms[:P, 0:128].unsqueeze(1).to_broadcast([P, n, 128]),
                                              ALU.mult))
            dve.wait_ge(inter, 1)
            for q in range(2):
                nc.vector.tensor_copy(oTs[:, :, :].rearrange("p (f h) n -> p h f n", h=2)[:, q, :, :],
                                      ps[4 + q][:, 0:64].rearrange("p (h n) -> p h n", h=2))
                last = nc.vector.tensor_copy(yTs[:, 2 * q:2 * q + 2, :],
                                             ps[6 + q][:, 0:64].rearrange("p (h n) -> p h n", h=2))
            last.then_inc(evac, 1)
            dve.wait_ge(back, 1)
            c.add(nc.vector.tensor_tensor(yo[:32, 4, 0:512], yo[:32, 4, 0:512], ps[6][:32, :], ALU.add))
            c.step(nc.vector.tensor_tensor(ycs[:32, 4, :].rearrange("p (h d) -> p h d", h=8),
                                           ps[7][:32, :].rearrange("p (h d) -> p h d", h=8),
                                           ecum[:32, 4, 0:8].unsqueeze(2).to_broadcast([32, 8, 64]), ALU.mult))
            for f in range(2):
                ebl = eb[:, f, 512:544].rearrange("p (b s) -> p b s", s=NS)[:, :, NS - 1:NS].to_broadcast([128, NB, 128])
                c.add(nc.vector.tensor_tensor(G0[:, f, :, :], G0[:, f, :, :], ebl, ALU.mult))
            c.add(nc.vector.tensor_tensor(S0[:, :, :].rearrange("p b (h d) -> p (b h) d", h=4),
                                          S0[:, :, :].rearrange("p b (h d) -> p (b h) d", h=4),
                                          elh[:, 8:16, :].rearrange("p b h -> p (b h)").unsqueeze(2)
                                          .to_broadcast([128, 32, 64]), ALU.mult))
            c.wait()
            dve.wait_ge(upd, 1)
            for b in range(NB):
                last = nc.vector.tensor_scalar(vm[:, b, :], xdd[:32, 4, :], C("bmask")[:32, b:b + 1], None, ALU.mult)
            last.then_inc(xmask, 1)
            for f in range(2):
                for q in range(2):
                    rows = G0[:, f, 4 * q:4 * q + 4, :].rearrange("p b n -> p (b n)")
                    last = nc.vector.tensor_tensor(rows, rows, ps[2 * f + q][:, :], ALU.add)
            last.then_inc(new_g, 1)
            dve.wait_ge(mm, 1)
            for q in range(4):
                rows = S0[:, 2 * q:2 * q + 2, :].rearrange("p b n -> p (b n)")
                last = nc.vector.tensor_tensor(rows, rows, ps[4 + q][:, :], ALU.add)
            last.then_inc(new_s, 1)
            gate_y(c, nc.vector, 4, 32).then_inc(gated, 1)
            for i in range(4):
                dve.wait_ge(trb, i + 1)
                nc.vector.tensor_copy(raw[:, 2 * i:2 * i + 2, :, :].rearrange("p b u n -> p (b u n)"), ps[i][:, :])\
                  .then_inc(fin, 1)

    with Scope(nc, "abe") as s:
        pt = [[s.ps(f"t{i}{h}") for h in range(2)] for i in range(2)]
        dv, var_ready, root, inverse, scaled, normed, flipped, by_act, by_dve = (s.sem(x) for x in (
            "dve_steps", "var_ready", "root", "inverse", "scaled", "normed", "flipped", "by_act", "by_dve"))
        block = s.block()

        @block.tensor
        def _(pe):
            for t, P in TILES:
                pe.wait_ge(normed, t + 1)
                if t >= 2:
                    pe.wait_ge(by_act, t - 1)
                    pe.wait_ge(by_dve, t - 1)
                for h in range(2):
                    for c in range(4):
                        last = nc.tensor.transpose(pt[t % 2][h][:, c * P:(c + 1) * P],
                                                   yo[:P, t, (4 * h + c) * 128:(4 * h + c + 1) * 128],
                                                   C("ident")[:P, :P])
                    last.then_inc(flipped, 1)

        def out_in(t, P, h):
            return (xT[:, 4 * h:4 * h + 4, tok0(t):tok0(t) + P],
                    pt[t % 2][h][:, :4 * P].rearrange("p (c n) -> p c n", c=4))

        @block.sync
        def _(sp):
            sp.wait_ge(L.kept["abd_stored"], 16 * 6)

        @block.vector
        def _(dve):
            c, V = Count(dve, dv), nc.vector
            c.add(V.tensor_scalar(ms[:, :, 0:4], ms[:, :, 0:4], 1.0 / 128, RMS_EPS, ALU.mult, ALU.add))
            V.tensor_scalar(ms[:, :, 4:5], ms[:, :, 4:5], 1.0 / 512, RMS_EPS, ALU.mult, ALU.add).then_inc(var_ready, 1)
            dve.wait_ge(root, 1)
            V.reciprocal(ms[:, :, :], ms[:, :, :]).then_inc(inverse, 1)
            dve.wait_ge(inverse, 1)
            for i in range(len(TILES) + 1):
                if i < len(TILES):
                    t, P = TILES[i]
                    o, y = yo[:P, t, 0:512], yo[:P, t, 512:1024]
                    V.scalar_tensor_tensor(out=y, in0=y, scalar=ms[:P, t, 4:5], in1=norms[:P, 128:640],
                                           op0=ALU.mult, op1=ALU.mult)
                    dve.wait_ge(scaled, t + 1)
                    V.tensor_tensor(o, o, rs[:P, t, :], ALU.mult).then_inc(normed, 1)
                if i >= 1:
                    t, P = TILES[i - 1]
                    dve.wait_ge(flipped, 2 * t + 2)
                    V.tensor_copy(*out_in(t, P, 1)).then_inc(by_dve, 1)

        @block.scalar
        def _(act):
            act.wait_ge(var_ready, 1)
            act.wait_ge(dv, 1)
            nc.scalar.activation(ms[:, :, :], ms[:, :, :], ACT.Sqrt).then_inc(root, 1)
            act.wait_ge(inverse, 1)
            for i in range(len(TILES) + 1):
                if i < len(TILES):
                    t, P = TILES[i]
                    for h in range(4):
                        oh = yo[:P, t, 128 * h:128 * h + 128]
                        last = nc.scalar.activation(oh, oh, ACT.Copy, scale=ms[:P, t, h:h + 1])
                    last.then_inc(scaled, 1)
                if i >= 1:
                    t, P = TILES[i - 1]
                    act.wait_ge(flipped, 2 * t + 1)
                    nc.scalar.activation(*out_in(t, P, 0), ACT.Copy).then_inc(by_act, 1)


def rank(V, c, dst, val, gt, eq, lt):
    lead, n = list(val.shape[:-1]), val.shape[-1]
    full = lead + [n, n]
    ax = len(lead)
    m_val, n_val = val.unsqueeze(ax).to_broadcast(full), val.unsqueeze(ax + 1).to_broadcast(full)
    c.add(V.tensor_tensor(gt, m_val, n_val, ALU.is_gt))
    c.step(V.tensor_tensor(eq, m_val, n_val, ALU.is_equal))
    c.step(V.tensor_tensor(eq, eq, lt, ALU.mult))
    c.step(V.tensor_tensor(gt, gt, eq, ALU.add))
    c.step(V.tensor_reduce(dst, gt, AX.X, ALU.add))


class Experts:

    RING = 3

    def __init__(self, nc, A, M, l):
        self.posi = M.sb("posi", [128, 2, 5], I32)
        self.gate = M.sb("gate", [128, 2, 5])
        self.tokof = M.sb("tokof", [128, NPAIR], I32)
        self.widx = M.sb("widx", [128, NTILE - NE], I32)
        self.extra = M.sb("extra", [1, 1], I32)
        self.wg = [M.sb(f"wg{i}", [128, KD * 2 * DE]) for i in range(2 * self.RING)]
        self.wd = [M.sb(f"wd{i}", [128, 2 * D]) for i in range(2 * self.RING)]
        self.w_out = [w[:, :].rearrange("p (k n) -> p k n", k=KD) for w in self.wg[-2:]]
        self.loaded = [M.sem(f"weights{i}") for i in range(self.RING)]
        self.w_gu = A["moe_w_gate_up"].rearrange("l g e (p j) f -> (l g e p) (j f)", p=128)
        self.w_dn = A["moe_w_down"].rearrange("l g e (p j) d -> (l g e p) (j d)", p=128)
        self.l = l

    def load(self, eng, i, multiplied=None, projected=None):
        n = self.RING
        for used, dst, src in ((multiplied, self.wg, self.w_gu), (projected, self.wd, self.w_dn)):
            if used is not None:
                eng.wait_ge(used, i - n + 1)
            for a in range(2):
                row = (self.l * NE + 2 * i + a) * 128
                eng.dma_start(dst[2 * (i % n) + a][:, :], src[row:row + 128, :]).then_inc(self.loaded[i % n], 16)

    def fill(self, eng, pairs):
        for i in pairs:
            self.load(eng, i)


def route(nc, name, C, lg, xT, E):
    l, posi, gate, tokof, widx = E.l, E.posi, E.gate, E.tokof, E.widx
    with Scope(nc, name) as s:
        gt4, eq4 = s.sb("gt4", [128, 5, 4, 4]), s.sb("eq4", [128, 5, 4, 4])
        gt8, eq8 = s.sb("gt8", [128, 5, 8, 8]), s.sb("eq8", [128, 5, 8, 8])
        r4, r8 = s.sb("r4", [128, 5, 4]), s.sb("r8", [128, 5, 8])
        mx, dif, ssum, pgrp = s.sb("mx", [128, 5]), s.sb("dif", [128, 5, 5]), s.sb("ssum", [128, 5]), s.sb("pg", [128, 5])
        sel, sel4 = s.sb("sel", [128, 5, 8]), s.sb("sel4", [128, 5, 8, 4])
        oh = s.sb("oh", [128, 2, 5, 8])
        pick = s.sb("pick", [128, 5, 8])
        v2 = s.sb("v2", [128, 5])
        As = s.sb("As", [128, 2, 5, 32])
        A12 = s.sb("A12", [128, 6, 32])
        earlier = s.sb("earlier", [128, 6, 32])
        rk = s.sb("rk", [128, 6, 32])
        cmp8 = s.sb("cmp8", [128, 32, 8])
        tiles, sc = s.sb("tiles", [128, 32]), s.sb("sc", [128, 2, 32])
        pos = s.sb("pos", [128, 10])
        big = s.sb("big", [128, NTILE - NE, 32])
        ex = s.sb("ex", [128, NTILE - NE])
        low, away = s.sb("low", [128, 5, 32]), s.sb("away", [128, 2, 32])
        ge = s.sb("ge", [128, 10, NPAIR + 1])
        ci = s.sb("ci", [128, 10, NPAIR])
        rr = s.sb("rr", [128, 2, 10])
        ohr = xT[:, :, :].rearrange("p k n -> p (k n)")[:, 0:1280].rearrange("p (a n) -> p a n", a=10)
        pr, pt = s.ps("r"), s.ps("t")
        (dv, ex_in, ex_out, asg, sums, ranks, onehots, toks) = (s.sem(x) for x in (
            "dve_steps", "exp_in", "exp_out", "assigned", "sums", "ranks", "onehots", "toks"))
        block = s.block()

        @block.tensor
        def _(pe):
            pe.wait_ge(asg, 1)
            nc.tensor.matmul(pr[:, 0:192], C("before"), A12[:, :, :].rearrange("p t e -> p (t e)"),
                             start=True, stop=False)
            pe.wait_ge(sums, 1)
            nc.tensor.matmul(pr[:, 0:192], C("ones"), earlier[:, :, :].rearrange("p t e -> p (t e)"),
                             start=False, stop=True).then_inc(ranks, 1)
            pe.wait_ge(onehots, 1)
            for n in range(10):
                last = nc.tensor.matmul(pt[:, 0:NPAIR], ohr[:, n, :], ci[:, n, :], start=(n == 0), stop=(n == 9))
            last.then_inc(toks, 1)

        @block.scalar
        def _(act):
            act.wait_ge(ex_in, 1)
            nc.scalar.activation(dif[:, :, :], dif[:, :, :], ACT.Exp).then_inc(ex_out, 1)

        @block.vector
        def _(dve):
            c, V = Count(dve, dv), nc.vector
            lt8 = C("lt8").rearrange("p (n m) -> p n m", n=8)
            lc = lg[:, :, 0:4]
            rank(V, c, r4[:, :, :], lc, gt4[:, :, :, :], eq4[:, :, :, :],
                 lt8[:, 0:4, 0:4].unsqueeze(1).to_broadcast([128, 5, 4, 4]))
            c.add(V.tensor_scalar(r4[:, :, :], r4[:, :, :], 0.0, None, ALU.is_equal))
            c.step(V.tensor_reduce(mx[:, :], lc, AX.X, ALU.max))
            c.add(V.tensor_tensor(dif[:, :, 0:4], lc, mx[:, :].unsqueeze(2).to_broadcast([128, 5, 4]), ALU.subtract))
            c.step(V.tensor_tensor(sel4[:, :, :, :],
                                   lg[:, :, 4:36].rearrange("p t (g e) -> p t e g", g=4),
                                   r4[:, :, :].unsqueeze(2).to_broadcast([128, 5, 8, 4]), ALU.mult))
            c.step(V.tensor_reduce(sel[:, :, :], sel4[:, :, :, :], AX.X, ALU.add))
            rank(V, c, r8[:, :, :], sel[:, :, :], gt8[:, :, :, :], eq8[:, :, :, :],
                 lt8.unsqueeze(1).to_broadcast([128, 5, 8, 8]))
            for k in range(2):
                c.add(V.tensor_scalar(oh[:, k, :, :], r8[:, :, :], float(k), None, ALU.is_equal))
            c.step(V.tensor_reduce(mx[:, :], sel[:, :, :], AX.X, ALU.max))
            c.step(V.tensor_tensor(pick[:, :, :], sel[:, :, :], oh[:, 1, :, :], ALU.mult))
            c.step(V.tensor_reduce(v2[:, :], pick[:, :, :], AX.X, ALU.add))
            V.tensor_tensor(dif[:, :, 4], v2[:, :], mx[:, :], ALU.subtract).then_inc(ex_in, 1)
            for k in range(2):
                c.add(V.tensor_tensor(As[:, k, :, :].rearrange("p t (g e) -> p t g e", g=4),
                                      r4[:, :, :].unsqueeze(3).to_broadcast([128, 5, 4, 8]),
                                      oh[:, k, :, :].unsqueeze(2).to_broadcast([128, 5, 4, 8]), ALU.mult))
            c.wait()
            for k in range(2):
                c.add(V.tensor_tensor(As[:, k, :, :], As[:, k, :, :],
                                      C("valid").unsqueeze(2).to_broadcast([128, 5, 32]), ALU.mult))
            c.wait()
            c.add(V.memset(A12[:, 5, :], 0.0))
            c.add(V.memset(earlier[:, 0, :], 0.0))
            c.step(V.tensor_tensor(A12[:, 0:5, :], As[:, 0, :, :], As[:, 1, :, :], ALU.add))
            V.tensor_copy(earlier[:, 1, :], A12[:, 0, :]).then_inc(asg, 1)
            dve.wait_ge(asg, 1)
            for t in range(1, 4):
                c.step(V.tensor_tensor(earlier[:, t + 1, :], earlier[:, t, :], A12[:, t, :], ALU.add))
            V.tensor_tensor(earlier[:, 5, :], earlier[:, 4, :], A12[:, 4, :], ALU.add).then_inc(sums, 1)
            dve.wait_ge(ex_out, 1)
            c.add(V.tensor_reduce(ssum[:, :], dif[:, :, 0:4], AX.X, ALU.add))
            c.step(V.tensor_scalar(pgrp[:, :], dif[:, :, 4], 1.0, None, ALU.add))
            c.step(V.tensor_tensor(ssum[:, :], ssum[:, :], pgrp[:, :], ALU.mult))
            c.step(V.reciprocal(gate[:, 0, :], ssum[:, :]))
            c.add(V.tensor_tensor(gate[:, 1, :], gate[:, 0, :], dif[:, :, 4], ALU.mult))
            dve.wait_ge(ranks, 1)
            c.step(V.tensor_copy(rk[:, :, :], pr[:, 0:192].rearrange("p (t e) -> p t e", t=6)))
            c.step(V.tensor_tensor(cmp8[:, :, :], rk[:, 5, :].unsqueeze(2).to_broadcast([128, 32, 8]),
                                   C("m64").unsqueeze(1).to_broadcast([128, 32, 8]), ALU.is_gt))
            c.step(V.tensor_reduce(tiles[:, :], cmp8[:, :, :], AX.X, ALU.add))
            c.step(V.tensor_copy(sc[:, 0, :], tiles[:, :]))
            cur = 0
            for sh in (1, 2, 4, 8, 16):
                c.add(V.tensor_copy(sc[:, 1 - cur, 0:sh], sc[:, cur, 0:sh]))
                c.step(V.tensor_tensor(sc[:, 1 - cur, sh:32], sc[:, cur, sh:32], sc[:, cur, 0:32 - sh], ALU.add))
                cur = 1 - cur
            ends = sc[:, cur, :]
            c.add(V.tensor_copy(E.extra[:, :], ends[0:1, 31:32]))
            c.add(V.tensor_tensor(big[:, :, :], ends.unsqueeze(1).to_broadcast([128, NTILE - NE, 32]),
                                  C("tile").unsqueeze(2).to_broadcast([128, NTILE - NE, 32]), ALU.is_le))
            c.step(V.tensor_tensor(tiles[:, :], ends, tiles[:, :], ALU.subtract))
            c.add(V.tensor_reduce(ex[:, :], big[:, :, :], AX.X, ALU.add))
            c.step(V.tensor_scalar(away[:, 0, :], tiles[:, :], float(SLOT), float(SLOT * (NE - 1)), ALU.mult, ALU.add))
            c.add(V.tensor_scalar(ex[:, :], ex[:, :], NE - 1.0, 128.0, ALU.min, ALU.mult))
            c.add(V.tensor_scalar(low[:, :, :], rk[:, 0:5, :], SLOT - 0.5, None, ALU.is_lt))
            c.step(V.tensor_tensor(away[:, 1, :], C("e64"), away[:, 0, :], ALU.subtract))
            c.add(V.tensor_scalar(widx[:, :], ex[:, :], C("pidx"), float(l * NE * 128), ALU.add, ALU.add))
            c.step(V.tensor_tensor(low[:, :, :], low[:, :, :], away[:, 1, :].unsqueeze(1).to_broadcast([128, 5, 32]),
                                   ALU.mult))
            c.step(V.tensor_tensor(rk[:, 0:5, :], rk[:, 0:5, :], away[:, 0, :].unsqueeze(1).to_broadcast([128, 5, 32]),
                                   ALU.add))
            c.step(V.tensor_tensor(rk[:, 0:5, :], rk[:, 0:5, :], low[:, :, :], ALU.add))
            for k in range(2):
                c.add(V.tensor_tensor(As[:, k, :, :], As[:, k, :, :], rk[:, 0:5, :], ALU.mult))
            c.wait()
            c.step(V.tensor_reduce(pos[:, :], As[:, :, :, :].rearrange("p k t e -> p (k t) e"), AX.X, ALU.add))
            c.add(V.tensor_copy(posi[:, :, :].rearrange("p k t -> p (k t)"), pos[:, :]))
            c.step(V.tensor_tensor(ge[:, :, :], pos[:, :].unsqueeze(2).to_broadcast([128, 10, NPAIR + 1]),
                                   C("m128").unsqueeze(1).to_broadcast([128, 10, NPAIR + 1]), ALU.is_ge))
            c.add(V.tensor_tensor(ci[:, :, :], ge[:, :, 0:NPAIR], ge[:, :, 1:NPAIR + 1], ALU.subtract))
            c.step(V.tensor_reduce(rr[:, 0, :], ge[:, :, 1:NPAIR + 1], AX.X, ALU.add))
            c.step(V.scalar_tensor_tensor(out=rr[:, 1, :], in0=rr[:, 0, :], scalar=-128.0, in1=pos[:, :],
                                          op0=ALU.mult, op1=ALU.add))
            for k in range(2):
                c.add(V.tensor_tensor(ci[:, 5 * k:5 * k + 5, :], ci[:, 5 * k:5 * k + 5, :],
                                      C("tokid").unsqueeze(2).to_broadcast([128, 5, NPAIR]), ALU.mult))
            c.wait()
            V.tensor_tensor(ohr[:, :, :], rr[:, 1, :].unsqueeze(2).to_broadcast([128, 10, 128]),
                            C("iota").unsqueeze(1).to_broadcast([128, 10, 128]), ALU.is_equal).then_inc(onehots, 1)
            dve.wait_ge(toks, 1)
            c.step(V.tensor_copy(tokof[:, :], pt[:, 0:NPAIR]))


def expert_stage(nc, name, C, E, xT, xd, yd, pairs):
    NR = E.RING
    n, first = len(pairs), 2 * pairs[0] - NE
    extra = first >= 0
    with Scope(nc, name) as s:
        wg, wd = E.wg, E.wd
        xg = [s.sb(f"xg{i}", [128, D]) for i in range(2)]
        xgT = [xT[:, :, 128 * i:128 * i + 128] for i in range(2)]
        sg, hh, hT = xT[:, 0, 256:256 + DE], xT[:, 1, 256:256 + DE], xT[:, 2:4, 256:384]
        Y = [s.sb(f"Y{i}", [128, D]) for i in range(2)]
        px = [s.ps(f"x{i}") for i in range(2)]
        pg = [s.ps(f"g{i}") for i in range(2)]
        ph = s.ps("h")
        py = [s.ps(f"y{i}") for i in range(2)]
        wl = [s.sem(f"gathered{i}") for i in range(NR)] if extra else E.loaded
        xl = [s.sem(f"rows{i}") for i in range(2)]
        ys = [s.sem(f"kept{i}") for i in range(2)]
        (xt, xta, xtd, gu, sl, hr, ht, htc, dn, ya, ydv) = (s.sem(x) for x in (
            "x_T", "x_act", "x_dve", "gate_up", "silu", "hidden", "h_T", "h_copied", "down", "y_act", "y_dve"))
        block = s.block()

        def when(eng, run):
            if not extra:
                return run(eng)
            tiles = eng.value_load(E.extra[0:1, 0:1], min_val=0, max_val=NTILE - NE)
            with eng.If(tiles > first):
                run(eng)

        def free(eng, i):
            if i >= NR:
                eng.wait_ge(gu, i - NR + 1)
                eng.wait_ge(dn, i - NR + 1)

        @block.gpsimd
        def _(pool):
            def rows(i):
                if i >= 2:
                    pool.wait_ge(xt, i - 1)
                at = pairs[i]
                nc.gpsimd.indirect_dma_start(out=xg[i % 2][:, :], out_offset=None, in_=xd,
                                             in_offset=bass.IndirectOffsetOnAxis(ap=E.tokof[:, at:at + 1], axis=0))\
                    .then_inc(xl[i % 2], 16)

            def run(pool):
                rows(0)
                for i in range(n):
                    if i + 1 < n:
                        rows(i + 1)
                    if extra:
                        free(pool, i)
                        for a in range(2):
                            at = bass.IndirectOffsetOnAxis(ap=E.widx[:, first + 2 * i + a:first + 2 * i + a + 1], axis=0)
                            for dst, src in ((wg, E.w_gu), (wd, E.w_dn)):
                                nc.gpsimd.indirect_dma_start(out=dst[2 * (i % NR) + a][:, :], out_offset=None,
                                                             in_=src, in_offset=at).then_inc(wl[i % NR], 16)
            when(pool, run)

        @block.sync
        def _(sp):
            def store(i):
                sp.wait_ge(ya, i + 1)
                sp.wait_ge(ydv, i + 1)
                at = 128 * pairs[i]
                sp.dma_start(yd[at:at + 128, :], Y[i % 2][:, :]).then_inc(ys[i % 2], 16)

            def run(sp):
                for i in range(n):
                    if not extra and i >= NR:
                        E.load(sp, i, gu, dn)
                    if i >= NR:
                        store(i - NR)
                for i in range(max(n - NR, 0), n):
                    store(i)
                for i in range(min(n, 2)):
                    sp.wait_ge(ys[i], 16 * ((n - i + 1) // 2))
            when(sp, run)

        @block.tensor
        def _(pe):
            def x_T(i):
                pe.wait_ge(xl[i % 2], 16 * (i // 2 + 1))
                if i >= 1:
                    pe.wait_ge(xta, i)
                    pe.wait_ge(xtd, i)
                xv = xg[i % 2][:, :].rearrange("r (p j) -> r j p", j=KD)
                for j in range(KD):
                    last = nc.tensor.transpose(px[j // 4][:, (j % 4) * 128:(j % 4) * 128 + 128], xv[:, j, :], C("ident"))
                last.then_inc(xt, 1)

            def gate_up(i):
                pe.wait_ge(wl[i % NR], 64 * (i // NR + 1))
                pe.wait_ge(xta, i + 1)
                pe.wait_ge(xtd, i + 1)
                if i >= 2:
                    pe.wait_ge(hr, i - 1)
                for j in range(KD):
                    for a in range(2):
                        last = nc.tensor.matmul(pg[i % 2][64 * a:64 * a + 64, :], xgT[i % 2][:, j, 64 * a:64 * a + 64],
                                                wg[2 * (i % NR) + a][:, j * 512:(j + 1) * 512],
                                                start=(j == 0), stop=(j == KD - 1))
                last.then_inc(gu, 1)

            def h_T(i):
                pe.wait_ge(hr, i + 1)
                if i >= 1:
                    pe.wait_ge(htc, i)
                hv = hh.rearrange("r (p j) -> r j p", j=2)
                for j in range(2):
                    last = nc.tensor.transpose(ph[:, j * 128:(j + 1) * 128], hv[:, j, :], C("ident"))
                last.then_inc(ht, 1)

            def down(i):
                pe.wait_ge(htc, i + 1)
                if i >= 1:
                    pe.wait_ge(ya, i)
                    pe.wait_ge(ydv, i)
                for n2 in range(2):
                    for j in range(2):
                        for a in range(2):
                            last = nc.tensor.matmul(py[n2][64 * a:64 * a + 64, :], hT[:, j, 64 * a:64 * a + 64],
                                                    wd[2 * (i % NR) + a][:, j * D + n2 * 512:j * D + (n2 + 1) * 512],
                                                    start=(j == 0), stop=(j == 1))
                last.then_inc(dn, 1)

            def run(pe):
                x_T(0)
                for i in range(n + 1):
                    if i < n:
                        gate_up(i)
                    if i >= 1:
                        h_T(i - 1)
                    if i + 1 < n:
                        x_T(i + 1)
                    if i >= 1:
                        down(i - 1)
            when(pe, run)

        def copy_x(i, half, eng, sem):
            eng.wait_ge(xt, i + 1)
            if i >= 2:
                eng.wait_ge(gu, i - 1)
            dst, src = xgT[i % 2][:, 4 * half:4 * half + 4, :], px[half][:, :].rearrange("p (j n) -> p j n", j=4)
            ins = nc.scalar.activation(dst, src, ACT.Copy) if half == 0 else nc.vector.tensor_copy(dst, src)
            ins.then_inc(sem, 1)

        def copy_y(i, half, eng, sem):
            eng.wait_ge(dn, i + 1)
            if i >= 2:
                eng.wait_ge(ys[i % 2], 16 * (i // 2))
            dst = Y[i % 2][:, 512 * half:512 * half + 512]
            ins = nc.scalar.activation(dst, py[half][:, :], ACT.Copy) if half == 0 else \
                nc.vector.tensor_copy(dst, py[half][:, :])
            ins.then_inc(sem, 1)

        @block.scalar
        def _(act):
            def run(act):
                copy_x(0, 0, act, xta)
                for i in range(n + 1):
                    if i < n:
                        act.wait_ge(gu, i + 1)
                        if i >= 1:
                            act.wait_ge(hr, i)
                        nc.scalar.activation(sg, pg[i % 2][:, 0:DE], ACT.Silu).then_inc(sl, 1)
                    if i >= 1:
                        act.wait_ge(ht, i)
                        if i >= 2:
                            act.wait_ge(dn, i - 1)
                        nc.scalar.activation(hT, ph[:, 0:256].rearrange("p (j n) -> p j n", j=2), ACT.Copy)\
                            .then_inc(htc, 1)
                    if i + 1 < n:
                        copy_x(i + 1, 0, act, xta)
                    if i >= 1:
                        copy_y(i - 1, 0, act, ya)
            when(act, run)

        @block.vector
        def _(dve):
            def run(dve):
                copy_x(0, 1, dve, xtd)
                for i in range(n + 1):
                    if i < n:
                        dve.wait_ge(sl, i + 1)
                        if i >= 1:
                            dve.wait_ge(ht, i)
                        nc.vector.tensor_tensor(hh, sg, pg[i % 2][:, DE:2 * DE], ALU.mult).then_inc(hr, 1)
                    if i + 1 < n:
                        copy_x(i + 1, 1, dve, xtd)
                    if i >= 1:
                        copy_y(i - 1, 1, dve, ydv)
            when(dve, run)


class Cache:

    LOADS = [(G, kind, pq) for kind in "kv" for G in range(2) for pq in range(4)]
    RING = 3

    def __init__(self, nc, A, L, pages):
        self.nc, self.pages = nc, pages
        self.ring = []
        self.grow(L, self.RING - 1)
        self.loaded = [L.kept[f"cache_loaded{i}"] for i in range(self.RING)]
        self.views = {k: A["cache_" + k].rearrange("n (c r) h d -> (n c) (r h d)", r=4) for k in "kv"}

    def grow(self, s, n):
        for i in range(len(self.ring), len(self.ring) + n):
            self.ring.append([s.sb(f"kv{i}{b}", [128, 4 * 512]) for b in range(4)])

    def load(self, n):
        G, kind, pq = self.LOADS[n]
        for b in range(4):
            at = (4 * G + b) * 4 + pq
            self.nc.gpsimd.indirect_dma_start(out=self.ring[n % self.RING][b][:, :], out_offset=None,
                                              in_=self.views[kind],
                                              in_offset=bass.IndirectOffsetOnAxis(ap=self.pages[:, at:at + 1], axis=0))\
                .then_inc(self.loaded[n % self.RING], 16)


class Pooling:

    def __init__(self, L, F, qkT):
        self.free = qkT[:, :, :].rearrange("p k n -> p (k n)")
        self.at = 0
        self.uP = F.sb("uP", [128, 4, PBUF + SEQ])
        self.uS = F.sb("uS", [128, 4, NB, PBUF + NS])
        self.newS = F.sb("newS", [128, 4, NB * PBUF])
        self.Df = self.take(4 * NTOK).rearrange("p (g n) -> p g n", g=4)
        self.scale = self.take(4)
        self.st = self.take(512)[:NB * PBUF, :]
        self.scales = self.take(128)[:4, :]
        self.sP = [self.take(PBUF + SEQ) for i in range(2)]
        self.sS = [self.take(NB * (PBUF + NS)).rearrange("p (b s) -> p b s", b=NB) for i in range(2)]

    def take(self, n):
        self.at += n
        assert self.at <= KD * NTOK
        return self.free[:, self.at - n:self.at]


def pool_window(V, c, C, p, g):
    uP, uS, Df, w = p.uP, p.uS, p.Df, WINDOWS[g]
    sp_, ss_ = uP[:, g, :], uS[:, g, :, :]
    width, i = 1, 0
    while width < w:
        n = PBUF + SEQ - width
        sP, sS = p.sP[i], p.sS[i]
        c.add(V.tensor_tensor(sP[:, width:], sp_[:, width:], sp_[:, 0:n], ALU.add))
        c.add(V.tensor_copy(sP[:, 0:width], sp_[:, 0:width]))
        c.add(V.tensor_tensor(sS[:, :, width:], ss_[:, :, width:], ss_[:, :, 0:PBUF + NS - width], ALU.add))
        c.step(V.tensor_copy(sS[:, :, 0:width], ss_[:, :, 0:width]))
        sp_, ss_ = sP, sS
        width, i = 2 * width, 1 - i
    inv = C("invcnt")[:, 16 * g:16 * g + PBUF]
    c.add(V.tensor_tensor(Df[:, g, 0:PBUF], sp_[:, PBUF:2 * PBUF], inv, ALU.mult))
    c.add(V.scalar_tensor_tensor(out=Df[:, g, PBUF:512], in0=sp_[:, 2 * PBUF:], scalar=1.0 / w,
                                 in1=uP[:, g, 2 * PBUF:], op0=ALU.mult, op1=ALU.subtract))
    c.add(V.scalar_tensor_tensor(out=Df[:, g, 512:544].rearrange("p (b s) -> p b s", s=NS),
                                 in0=ss_[:, :, PBUF:], scalar=1.0 / w, in1=uS[:, g, :, PBUF:],
                                 op0=ALU.mult, op1=ALU.subtract))
    c.wait()
    c.step(V.tensor_tensor(Df[:, g, 0:PBUF], Df[:, g, 0:PBUF], uP[:, g, PBUF:2 * PBUF], ALU.subtract))


def rotate(V, c, C, qk, p, t, P):
    r = [p.sP[0][:P, 128 * i:128 * i + 128].rearrange("p (h d) -> p h d", h=16) for i in range(4)]
    w = qk[:P, t, :].rearrange("p (h d) -> p h d", d=64)
    x1, x2 = w[:, :, 0:8], w[:, :, 8:16]
    cos, sin = (C("rope")[:P, 16 * t + 8 * i:16 * t + 8 * i + 8].unsqueeze(1).to_broadcast([P, 16, 8])
                for i in range(2))
    for dst, x, f in ((r[0], x1, cos), (r[1], x2, sin), (r[2], x2, cos), (r[3], x1, sin)):
        c.add(V.tensor_tensor(dst, x, f, ALU.mult))
    c.wait()
    c.add(V.tensor_tensor(x1, r[0], r[1], ALU.subtract))
    c.step(V.tensor_tensor(x2, r[2], r[3], ALU.add))


def mixer_cd(nc, A, C, xT, pages):
    mixT = xT
    with Scope(nc, "cd") as L:
        vt = L.sb("vt", [128, 5, 512])
        qkT = L.sb("qkT", [128, KD, NTOK])
        cache = Cache(nc, A, L, pages)
        with Scope(nc, "cdp") as F:
            qk = F.sb("qk", [128, 5, 1024])
            p = Pooling(L, F, qkT)
            project_cd(nc, A, C, F, xT, p, qk, vt, cache)
            store_and_pool(nc, A, C, qk, vt, p, mixT)
            transpose_stage(nc, "cdq", C, qk, qkT)
        cache.grow(L, 1)
        attend_prompt(nc, C, qkT, vt, mixT, cache)
        attend_sample(nc, C, qkT, vt, mixT, cache)


def project_cd(nc, A, C, F, xT, p, qk, vt, cache):
    state_in = F.kept["cdi_state_loaded"]
    dv = F.sem("dve_steps")
    jobs = []

    def jobs_of(n, w):
        first = len(jobs)
        if n == 0:
            for f in range(4):
                jobs.append(Job(n, 128, 512, lambda k, f=f: w[:, k, f * 128:f * 128 + 128],
                                lambda k: xT[:, k, 0:512], "act",
                                lambda s, cols, f=f: nc.scalar.activation(p.uP[:, f, PBUF:], s, ACT.Copy)))
                jobs.append(Job(n, 128, 32, lambda k, f=f: w[:, k, f * 128:f * 128 + 128],
                                lambda k: xT[:, k, 512:544], "dve",
                                lambda s, cols, f=f: nc.vector.tensor_copy(
                                    p.uS[:, f, :, PBUF:], s.rearrange("p (b s) -> p b s", s=NS))))

            def flip(ps):
                nc.tensor.wait_ge(state_in, 32)
                for g in range(4):
                    nc.tensor.transpose(ps[:, g * 120:(g + 1) * 120], p.st[:, g * 128:(g + 1) * 128],
                                        C("ident")[:120, :120])
                return nc.tensor.transpose(ps[:, 480:484], p.scales, C("ident")[:4, :4])

            def copy_state(s, cols):
                nc.vector.tensor_copy(p.scale, s[:, 480:484])
                return nc.vector.tensor_copy(p.uS[:, :, :, 0:PBUF],
                                             s[:, 0:480].rearrange("p (g b i) -> p g b i", g=4, b=NB))
            jobs.append(Job(n, 128, 484, None, None, "dve", copy_state, emit=flip))
            return jobs[first:]
        for t, P in TILES:
            def copy(s, cols, t=t, P=P):
                dst = (vt[:P, t, :] if n == 3 else qk[:P, t, (n - 1) * 512:n * 512])[:, cols]
                if t % 2:
                    return nc.scalar.activation(dst, s, ACT.Copy)
                return nc.vector.tensor_copy(dst, s)
            jobs.append(Job(n, P, 512, lambda k, t=t, P=P: xT[:, k, tok0(t):tok0(t) + P],
                            lambda k: w[:, k, 0:512], "act" if t % 2 else "dve", copy))
        return jobs[first:]

    steps = {}

    def clear(dve, copied):
        steps["c"] = Count(dve, dv)
        steps["c"].step(nc.vector.memset(p.uP[:, :, 0:PBUF], 0.0))

    def window(g):
        def run(dve, copied):
            c = steps["c"]
            copied(8)
            copied(2 * g)
            copied(2 * g + 1)
            pool_window(nc.vector, c, C, p, g)
            if g == 3:
                c.step(nc.vector.tensor_copy(p.newS[:, :, :].rearrange("p g (b i) -> p g b i", b=NB),
                                             p.uS[:, :, :, NS:]))
        return run

    def rotations(ts):
        def run(dve, copied):
            for t in ts:
                copied(9 + t)
                copied(14 + t)
                rotate(nc.vector, steps["c"], C, qk, p, t, TILES[t][1])
        return run

    def ahead(pool):
        pool.dma_start(p.st, A["state_pool"].rearrange("b i c -> (b i) c")).then_inc(state_in, 16)
        pool.dma_start(p.scales, A["cd_pool_scale"].rearrange("(g d) -> g d", d=128)).then_inc(state_in, 16)
        for n in range(cache.RING - 1):
            cache.load(n)

    project_stage(nc, "cdi", A["cd_w_in"], [(512 * i, 512 * i + 512) for i in range(4)], 512, xT, jobs_of, nbuf=2,
                  ahead=ahead, dve_at={0: clear, 9: window(0), 11: window(1), 13: window(2), 15: window(3),
                                       20: rotations((0, 1)), 21: rotations((2, 3)), 22: rotations((4,))})


def store_and_pool(nc, A, C, qk, vt, p, mixT):
    with Scope(nc, "pl") as s:
        wp = s.sb("wp", [128, 4, 128])
        outs = s.sb("outs", [128, 2, 512])
        pnp, pns = s.ps("np"), s.ps("ns")
        pm = [s.ps(f"m{i}") for i in range(4)]
        loaded, act_c, stored, new_T, new_o, mixed = (s.sem(x) for x in (
            "loaded", "act_c", "stored", "new_T", "new_o", "mixed"))
        block = s.block()

        @block.sync
        def _(sp):
            sp.dma_start(wp[:, :, :], A["cd_w_pool"].rearrange("g c d -> c g d")).then_inc(loaded, 16)
            sp.dma_start(A["v_p"][0].rearrange("(t p) h d -> p t (h d)", p=128), vt[:, 0:4, :]).then_inc(stored, 16)
            sp.dma_start(A["v_s"].rearrange("b s h d -> (b s) (h d)"), vt[0:32, 4, :]).then_inc(stored, 16)
            sp.dma_start(A["k_p"][0].rearrange("(t p) h d -> p t (h d)", p=128), qk[:, 0:4, 512:1024]).then_inc(stored, 16)
            sp.dma_start(A["k_s"].rearrange("b s h d -> (b s) (h d)"), qk[0:32, 4, 512:1024]).then_inc(stored, 16)
            sp.wait_ge(new_o, 1)
            sp.dma_start(A["pool_p"][0], outs[0:PBUF, 0, :]).then_inc(stored, 16)
            sp.dma_start(A["pool_s"].rearrange("b i c -> (b i) c"), outs[0:NB * PBUF, 1, :]).then_inc(stored, 16)
            sp.wait_ge(stored, 16 * 6)

        @block.tensor
        def _(pe):
            for g in range(4):
                nc.tensor.transpose(pnp[:PBUF, g * 128:(g + 1) * 128], p.uP[:, g, SEQ:SEQ + PBUF], C("ident"))
            for g in range(4):
                last = nc.tensor.transpose(pns[:NB * PBUF, g * 128:(g + 1) * 128], p.newS[:, g, :], C("ident"))
            last.then_inc(new_T, 1)
            pe.wait_ge(loaded, 16)
            for g in range(4):
                if g >= 2:
                    pe.wait_ge(mixed, g - 1)
                a, b = pm[2 * (g % 2)], pm[2 * (g % 2) + 1]
                nc.tensor.matmul(a[:, :], wp[:, g, :], p.Df[:, g, 0:512], start=True, stop=True)
                nc.tensor.matmul(b[:, 0:32], wp[:, g, :], p.Df[:, g, 512:544], start=True, stop=True).then_inc(act_c, 1)

        @block.scalar
        def _(act):
            for g in range(4):
                act.wait_ge(act_c, g + 1)
                a, b = pm[2 * (g % 2)], pm[2 * (g % 2) + 1]
                nc.scalar.activation(mixT[:, g, 0:512], a[:, :], ACT.Copy, scale=p.scale[:, g:g + 1])
                nc.scalar.activation(mixT[:, g, 512:544], b[:, 0:32], ACT.Copy, scale=p.scale[:, g:g + 1])\
                  .then_inc(mixed, 1)

        @block.vector
        def _(dve):
            dve.wait_ge(new_T, 1)
            nc.vector.tensor_copy(outs[0:PBUF, 0, :], pnp[:PBUF, :])
            nc.vector.tensor_copy(outs[0:NB * PBUF, 1, :], pns[:NB * PBUF, :]).then_inc(new_o, 1)


def attend_prompt(nc, C, qkT, vt, mixT, cache):
    units = [(h, t) for h in range(8) for t in range(4)]
    scale = 64 ** -0.5
    with Scope(nc, "ap") as s:
        Pm = [s.sb(f"P{i}", [128, 512]) for i in range(3)]
        PT = [s.sb(f"PT{i}", [128, 512]) for i in range(2)]
        nb = s.sb("nb", [128, len(units)])
        den = s.sb("den", [128, len(units)])
        ot = s.sb("ot", [128, 4, 512])
        psc = [s.ps(f"s{i}") for i in range(3)]
        ptr = [s.ps(f"t{i}") for i in range(2)]
        po = [s.ps(f"o{i}") for i in range(2)]
        (sc, dv, mxd, ex, tr, ptc, pv, od, o_T, o_c) = (s.sem(x) for x in (
            "scores", "dve_steps", "max_ready", "exps", "P_T", "P_copied", "pv", "o_ready", "o_T", "o_copied"))
        block = s.block()
        n = len(units)

        @block.gpsimd
        def _(pool):
            cache.load(cache.RING - 1)

        @block.tensor
        def _(pe):
            for u in range(n + 2):
                if u < n:
                    h, t = units[u]
                    r, w = slice(64 * (h % 2), 64 * (h % 2) + 64), (t + 1) * 128
                    if u >= 3:
                        pe.wait_ge(ex, u - 2)
                    nc.tensor.matmul(psc[u % 3][:, 0:w], qkT[r, h // 2, 128 * t:128 * t + 128],
                                     qkT[r, 4 + h // 2, 0:w], start=True, stop=True).then_inc(sc, 1)
                if 1 <= u <= n:
                    h, t = units[u - 1]
                    pe.wait_ge(ex, u)
                    if u >= 3:
                        pe.wait_ge(ptc, u - 2)
                    for k in range(t + 1):
                        last = nc.tensor.transpose(ptr[(u - 1) % 2][:, 128 * k:128 * k + 128],
                                                   Pm[(u - 1) % 3][:, 128 * k:128 * k + 128], C("ident"))
                    last.then_inc(tr, 1)
                if u >= 2:
                    h, t = units[u - 2]
                    pe.wait_ge(ptc, u - 1)
                    if u >= 4:
                        pe.wait_ge(od, u - 3)
                    for k in range(t + 1):
                        last = nc.tensor.matmul(po[u % 2][:, 0:64], PT[u % 2][:, 128 * k:128 * k + 128],
                                                vt[:, k, h * 64:(h + 1) * 64], start=(k == 0), stop=(k == t))
                    last.then_inc(pv, 1)
            pe.wait_ge(od, n)
            for t in range(4):
                for f in range(4):
                    last = nc.tensor.transpose((psc + ptr)[t][:, f * 128:(f + 1) * 128],
                                               ot[:, t, f * 128:(f + 1) * 128], C("ident"))
                last.then_inc(o_T, 1)

        @block.vector
        def _(dve):
            c, V = Count(dve, dv), nc.vector
            for u in range(n + 2):
                if u < n:
                    h, t = units[u]
                    w = (t + 1) * 128
                    dve.wait_ge(sc, u + 1)
                    c.step(V.tensor_tensor(psc[u % 3][:, 128 * t:w], psc[u % 3][:, 128 * t:w], C("causal"), ALU.add))
                    c.step(V.reduce_max(nb[:, u:u + 1], psc[u % 3][:, 0:w], AX.X))
                    V.tensor_scalar(nb[:, u:u + 1], nb[:, u:u + 1], -scale, None, ALU.mult).then_inc(mxd, 1)
                if u >= 2:
                    h, t = units[u - 2]
                    dve.wait_ge(ex, u - 1)
                    c.step(V.reciprocal(den[:, u - 2:u - 1], den[:, u - 2:u - 1]))
                    dve.wait_ge(pv, u - 1)
                    V.tensor_scalar(ot[:, t, h * 64:(h + 1) * 64], po[u % 2][:, 0:64], den[:, u - 2:u - 1], None,
                                    ALU.mult).then_inc(od, 1)
            for t in range(4):
                dve.wait_ge(o_T, t + 1)
                V.tensor_copy(mixT[:, 4:8, 128 * t:128 * t + 128],
                              (psc + ptr)[t][:, :].rearrange("p (f n) -> p f n", f=4)).then_inc(o_c, 1)

        @block.scalar
        def _(act):
            for u in range(n + 1):
                if u < n:
                    h, t = units[u]
                    w = (t + 1) * 128
                    act.wait_ge(mxd, u + 1)
                    if u >= 3:
                        act.wait_ge(tr, u - 2)
                    nc.scalar.activation(Pm[u % 3][:, 0:w], psc[u % 3][:, 0:w], ACT.Exp, bias=nb[:, u:u + 1],
                                         scale=scale, accum_out=den[:, u:u + 1]).then_inc(ex, 1)
                if u >= 1:
                    h, t = units[u - 1]
                    act.wait_ge(tr, u)
                    if u >= 3:
                        act.wait_ge(pv, u - 2)
                    nc.scalar.activation(PT[(u - 1) % 2][:, 0:(t + 1) * 128], ptr[(u - 1) % 2][:, 0:(t + 1) * 128],
                                         ACT.Copy).then_inc(ptc, 1)


def attend_sample(nc, C, qkT, vt, mixT, cache):
    scale = 64 ** -0.5
    with Scope(nc, "as") as s:
        NBUF, ring, loads, kvl = cache.RING, cache.ring, cache.LOADS, cache.loaded
        KT = [qkT[:, 0:4, 0:512], qkT[:, 4:8, 0:512]] + [s.sb(f"KT{b}", [128, 4, 512]) for b in range(2)]
        PT = vt[:, 0:4, :].rearrange("p t (r n) -> p (t r) n", r=4)
        Q = s.sb("Q", [128, NB, 4, 32])
        Ss = [s.sb(f"S{G}", [128, 4 * 512 + NS]) for G in range(2)]
        own, ownT = s.sb("own", [128, 32]), s.sb("ownT", [32, 128])
        gs, rk, gt8, eq8 = s.sb("gs", [128, 16]), s.sb("rk", [128, 8]), s.sb("gt8", [128, 8, 8]), s.sb("eq8", [128, 8, 8])
        nb, den = s.sb("nb", [128, 2]), s.sb("den", [128, 2])
        Oh, wh = KT[2][:, 0, :], [KT[2][:, 1, 8 * G:8 * G + 8] for G in range(2)]
        ptk = [s.ps(f"k{i}") for i in range(4)]
        pss = [s.ps(f"s{i}") for i in range(2)]
        po, pw = s.ps("o"), s.ps("w")
        (dv, k_T, kcp, kcp2, scored, sccp, q_r, soft, exs, pT, pTc, ownr, ownTr, ownc, pvd, oh_r, o_t,
         o_c, kvused) = (s.sem(x) for x in (
             "dve_steps", "K_T", "K_act", "K_dve", "scored", "s_copied", "Q_ready",
             "softmax_in", "exps", "P_T", "P_copied", "own_ready", "own_T", "own_copied", "pv", "O_ready", "O_T",
             "O_copied", "kv_used"))
        BANKS = (0, 2, 1, 3)
        block = s.block()

        @block.gpsimd
        def _(pool):
            for n in range(NBUF, len(loads)):
                m = n - NBUF + 1
                if loads[n - NBUF][1] == "k":
                    pool.wait_ge(k_T, 16 * sum(q[1] == "k" for q in loads[:m]))
                else:
                    pool.wait_ge(kvused, sum(q[1] == "v" for q in loads[:m]))
                cache.load(n)

        @block.tensor
        def _(pe):
            pe.wait_ge(q_r, 1)
            nk = 0
            for n, (G, kind, pq) in enumerate(loads):
                pe.wait_ge(kvl[n % NBUF], 64 * (n // NBUF + 1))
                if kind == "k":
                    for b in range(4):
                        for c in BANKS:
                            if nk:
                                pe.wait_ge(kcp if c < 2 else kcp2, 2 * nk - 1 + c % 2)
                            for r in range(4):
                                last = nc.tensor.transpose(ptk[c][:, r * 128:(r + 1) * 128],
                                                           ring[n % NBUF][b][:, r * 512 + c * 128:r * 512 + (c + 1) * 128],
                                                           C("ident"))
                            last.then_inc(k_T, 1)
                        nk += 1
                    pe.wait_ge(kcp, 2 * nk)
                    pe.wait_ge(kcp2, 2 * nk)
                    ns = G * 5 + pq
                    if ns >= 2:
                        pe.wait_ge(sccp, ns - 1)
                    for c in range(4):
                        for b in range(4):
                            last = nc.tensor.matmul(pss[ns % 2][32 * b:32 * b + 32, :], Q[:, 4 * G + b, c, :],
                                                    KT[b][:, c, :], start=(c == 0), stop=(c == 3),
                                                    tile_position=(0, 32 * b))
                    last.then_inc(scored, 1)
                    if pq == 3:
                        ns += 1
                        pe.wait_ge(sccp, ns - 1)
                        for b in range(4):
                            for c in range(4):
                                tok = 512 + 4 * (4 * G + b)
                                last = nc.tensor.matmul(pss[ns % 2][32 * b:32 * b + 32, 0:NS], Q[:, 4 * G + b, c, :],
                                                        qkT[:, 4 + c, tok:tok + NS], start=(c == 0), stop=(c == 3),
                                                        tile_position=(0, 32 * b))
                        last.then_inc(scored, 1)
                else:
                    if pq == 0:
                        pe.wait_ge(exs, G + 1)
                        for q in range(4):
                            for r in range(4):
                                last = nc.tensor.transpose(ptk[q][:, r * 128:(r + 1) * 128],
                                                           Ss[G][:, q * 512 + r * 128:q * 512 + (r + 1) * 128],
                                                           C("ident"))
                            last.then_inc(pT, 1)
                        pe.wait_ge(ownr, G + 1)
                        if G:
                            pe.wait_ge(o_c, G)
                        nc.tensor.transpose(pw[0:32, 0:128], own[:, :], C("ident")).then_inc(ownTr, 1)
                        pe.wait_ge(pTc, 4 * G + 4)
                        if G:
                            pe.wait_ge(oh_r, G)
                    for r in range(4):
                        for b in range(4):
                            last = nc.tensor.matmul(po[32 * b:32 * b + 32, :], PT[:, 4 * pq + r, 32 * b:32 * b + 32],
                                                    ring[n % NBUF][b][:, r * 512:(r + 1) * 512],
                                                    start=(pq == 0 and r == 0), stop=False, tile_position=(0, 32 * b),
                                                    skip_group_check=True)
                    last.then_inc(kvused, 1)
                    if pq == 3:
                        pe.wait_ge(ownc, G + 1)
                        for b in range(4):
                            last = nc.tensor.matmul(po[32 * b:32 * b + 32, :], ownT[:, 32 * b:32 * b + 32],
                                                    vt[0:32, 4, :], start=False, stop=True, tile_position=(0, 32 * b),
                                                    skip_group_check=True)
                        last.then_inc(pvd, 1)
                        pe.wait_ge(oh_r, G + 1)
                        for c in range(4):
                            last = nc.tensor.matmul(pw[:, 128 + 16 * c:144 + 16 * c], Oh[:, c * 128:(c + 1) * 128],
                                                    C("sumh"), start=True, stop=True)
                        last.then_inc(o_t, 1)

        @block.scalar
        def _(act):
            def keys(G, after_row=None, run=None):
                for pq in range(4):
                    for b in range(4):
                        nk = 16 * G + 4 * pq + b
                        if nk >= 4:
                            act.wait_ge(scored, G * 5 + pq)
                        for c in range(2):
                            act.wait_ge(k_T, 4 * nk + BANKS.index(c) + 1)
                            nc.scalar.activation(KT[b][:, c, :], ptk[c][:, :], ACT.Copy).then_inc(kcp, 1)
                        if 4 * pq + b == after_row:
                            run()

            def exps(G):
                act.wait_ge(soft, G + 1)
                nc.scalar.activation(Ss[G][:, :], Ss[G][:, :], ACT.Exp, bias=nb[:, G:G + 1], scale=scale,
                                     accum_out=den[:, G:G + 1]).then_inc(exs, 1)

            def probs(G):
                for q in range(4):
                    act.wait_ge(pT, 4 * G + q + 1)
                    if G and q == 0:
                        act.wait_ge(pvd, G)
                    nc.scalar.activation(PT[:, 4 * q:4 * q + 4, :].rearrange("p r n -> p (r n)"), ptk[q][:, :],
                                         ACT.Copy).then_inc(pTc, 1)
                act.wait_ge(ownTr, G + 1)
                nc.scalar.activation(ownT[:, :], pw[0:32, 0:128], ACT.Copy).then_inc(ownc, 1)

            keys(0)
            keys(1, 5, lambda: exps(0))
            probs(0)
            exps(1)
            probs(1)

        @block.vector
        def _(dve):
            c, V = Count(dve, dv), nc.vector
            lt8 = C("lt8").rearrange("p (n m) -> p n m", n=8)

            def keys(G, between=None):
                for pq in range(4):
                    ns = G * 5 + pq
                    for b in range(4):
                        nk = 16 * G + 4 * pq + b
                        if nk >= 4:
                            dve.wait_ge(scored, ns)
                        for f in (2, 3):
                            dve.wait_ge(k_T, 4 * nk + BANKS.index(f) + 1)
                            V.tensor_copy(KT[b][:, f, :], ptk[f][:, :]).then_inc(kcp2, 1)
                        if between and 4 * pq + b < len(between):
                            between[4 * pq + b]()
                    dve.wait_ge(scored, ns + 1)
                    V.tensor_copy(Ss[G][:, 512 * pq:512 * pq + 512], pss[ns % 2][:, :]).then_inc(sccp, 1)
                    dve.wait_ge(sccp, ns + 1)
                    sv = Ss[G][:, 512 * pq:512 * pq + 512].rearrange("p (r b x) -> p b r x", r=4, b=2)
                    c.step(V.tensor_reduce(gs[:, 8 * G + 2 * pq:8 * G + 2 * pq + 2], sv, AX.XY, ALU.add))

            def own_scores(G):
                ns = 5 * G + 4
                dve.wait_ge(scored, ns + 1)
                V.tensor_tensor(Ss[G][:, 2048:2052], pss[ns % 2][:, 0:NS], C("ownneg"), ALU.add).then_inc(sccp, 1)

            def choose(G):
                rank(V, c, rk[:, :], gs[:, 8 * G:8 * G + 8], gt8[:, :, :], eq8[:, :, :], lt8)
                c.step(V.tensor_scalar(rk[:, :], rk[:, :], 2.5, NEG, ALU.is_gt, ALU.mult))

            def penalize(G):
                S = Ss[G]
                for q in range(4):
                    for bl in range(2):
                        v3 = S[:, 512 * q:512 * q + 512].rearrange("p (r b x) -> p b r x", r=4, b=2)[:, bl, :, :]
                        c.add(V.tensor_scalar(v3, v3, rk[:, 2 * q + bl:2 * q + bl + 1], None, ALU.add))
                c.wait()

            def maxima(G):
                S = Ss[G]
                dve.wait_ge(sccp, 5 * G + 5)
                c.step(V.reduce_max(nb[:, G:G + 1], S[:, :], AX.X))
                V.tensor_scalar(nb[:, G:G + 1], nb[:, G:G + 1], -scale, None, ALU.mult).then_inc(soft, 1)

            def weights(G):
                dve.wait_ge(exs, G + 1)
                if G:
                    dve.wait_ge(ownTr, G)
                c.add(V.reciprocal(den[:, G:G + 1], den[:, G:G + 1]))
                V.tensor_tensor(own[:, :].rearrange("p (b k) -> p b k", k=NS),
                                Ss[G][:, 2048:2052].unsqueeze(1).to_broadcast([128, NB, NS]),
                                C(f"ownb{G}").rearrange("p (b k) -> p b k", k=NS), ALU.mult).then_inc(ownr, 1)
                c.wait()
                c.step(V.tensor_scalar(wh[G], C("hmask"), den[:, G:G + 1], None, ALU.mult))

            def outputs(G):
                dve.wait_ge(pvd, G + 1)
                V.tensor_tensor(Oh.rearrange("p (h d) -> p h d", h=8), po[:, :].rearrange("p (h d) -> p h d", h=8),
                                wh[G].unsqueeze(2).to_broadcast([128, 8, 64]), ALU.mult).then_inc(oh_r, 1)
                dve.wait_ge(o_t, G + 1)
                V.tensor_copy(mixT[:, 4:8, 512 + 16 * G:528 + 16 * G],
                              pw[:, 128:192].rearrange("p (f n) -> p f n", f=4)).then_inc(o_c, 1)

            c.step(V.memset(Q[:, :, :, :], 0.0))
            for f in range(4):
                for h in range(2):
                    r = slice(64 * h, 64 * h + 64)
                    last = V.tensor_copy(Q[r, :, f, 4 * (2 * f + h):4 * (2 * f + h) + 4],
                                         qkT[r, f, 512:544].rearrange("p (b s) -> p b s", s=NS))
            last.then_inc(q_r, 1)
            keys(0)
            own_scores(0)
            keys(1, between=[lambda: choose(0), lambda: penalize(0), lambda: maxima(0)])
            own_scores(1)
            weights(0)
            choose(1)
            penalize(1)
            maxima(1)
            outputs(0)
            weights(1)
            outputs(1)


IN = ["x_prompt", "x_sample", "state_gla", "state_ssm", "state_conv", "state_pool", "cache_k", "cache_v",
      "page_table", "ab_w_in", "ab_w_gate2", "ab_b_gate", "ab_gla_norm", "ab_conv_w", "ab_conv_b", "ab_dt_bias",
      "ab_a_log", "ab_d_skip", "ab_ssm_norm", "ab_w_out", "cd_w_in", "cd_w_pool", "cd_pool_scale", "cd_w_out",
      "moe_w_coarse", "moe_b_coarse", "moe_w_fine", "moe_b_fine", "moe_w_gate_up", "moe_w_down", "ln_g", "ln_b"]
OUT = [("y_p", (1, SEQ, D)), ("y_s", (NB, NS, D)), ("gla_p", (1, 4, 64, 128)), ("ssm_p", (1, 8, 64, 64)),
       ("conv_p", (1, 3, 768)), ("pool_p", (1, PBUF, 512)), ("k_p", (1, SEQ, 8, 64)), ("v_p", (1, SEQ, 8, 64)),
       ("gla_s", (NB, 4, 64, 128)), ("ssm_s", (NB, 8, 64, 64)), ("conv_s", (NB, 3, 768)),
       ("pool_s", (NB, PBUF, 512)), ("k_s", (NB, NS, 8, 64)), ("v_s", (NB, NS, 8, 64))]


def load_stage(nc, A, C, consts, X, I, wr, br, pages):
    with Scope(nc, "in") as s:
        table = s.sb("table", [128, NB * NPG], I32)
        quads = s.sb("quads", [128, NB * NPG // 4])
        loaded, routers, small, paged, dv = (s.sem(x) for x in ("loaded", "routers", "small", "paged", "dve_steps"))
        block = s.block()

        @block.sync
        def _(sp):
            sp.dma_start(table[:, :], A["page_table"].rearrange("b n -> (b n)").partition_broadcast(128))\
              .then_inc(paged, 16)
            sp.dma_start(consts[:, :], A["consts"]).then_inc(paged, 16)
            for t in range(4):
                sp.dma_start(X[:, t, :], A["x_prompt"][0, tok0(t):tok0(t) + 128, :]).then_inc(loaded, 16)
            sp.dma_start(X[0:32, 4, :], A["x_sample"].rearrange("b s d -> (b s) d")).then_inc(loaded, 16)
            for dst, src in I.loads:
                sp.dma_start(dst, src).then_inc(small, 16)
            for l in range(2):
                sp.dma_start(wr[l][:, :, 0:4], A["moe_w_coarse"][l].rearrange("(k p) g -> p k g", p=128))\
                  .then_inc(routers, 16)
                for g in range(4):
                    sp.dma_start(wr[l][:, :, 4 + 8 * g:12 + 8 * g],
                                 A["moe_w_fine"][l, g].rearrange("(k p) e -> p k e", p=128)).then_inc(routers, 16)
                sp.dma_start(br[l][:, 0:4], A["moe_b_coarse"][l].partition_broadcast(128)).then_inc(routers, 16)
                sp.dma_start(br[l][:, 4:36], A["moe_b_fine"][l].rearrange("g e -> (g e)").partition_broadcast(128))\
                  .then_inc(routers, 16)
            sp.wait_ge(loaded, 16 * 5)
            sp.wait_ge(routers, 16 * 14)
            sp.wait_ge(small, 16 * len(I.loads))

        @block.vector
        def _(dve):
            c, V = Count(dve, dv), nc.vector
            dve.wait_ge(paged, 32)
            for g in range(4):
                r = slice(32 * g, 32 * g + 32)
                c.add(V.tensor_copy(quads[r, :], table[r, :].rearrange("p (n g) -> p n g", g=4)[:, :, g]))
            c.wait()
            c.step(V.tensor_scalar(quads[:, :], quads[:, :], 32.0, C("p32"), ALU.mult, ALU.add))
            c.step(V.tensor_copy(pages[:, :], quads[:, :]))


def build(nc, A, cols, ncols):
    xd = nc.dram_tensor("token_rows", [NTOK, D], F32).ap()
    yd = nc.dram_tensor("expert_rows", [NROW, D], F32).ap()
    cleared = nc.alloc_semaphore("extra_rows_cleared")
    names = [f"{n}_stored" for n in ("abi", "abc", "abd", "pl", "n11")] + ["cdi_state_loaded"]
    names += [f"cache_loaded{i}" for i in range(Cache.RING)]
    for l in range(2):
        names += [f"{n}{l}_rows{i}" for n in "efg" for i in range(2)]
        names += [f"{n}{l}_gathered{i}" for n in "fg" for i in range(3)] + [f"n{l}1_y_in{i}" for i in range(5)]
    Scope.used, Scope.kept = [], {n: nc.alloc_semaphore(n) for n in names}
    with Scope(nc, "top") as S:
        X = S.sb("X", [128, 5, D])
        consts = S.sb("consts", [128, ncols])
        xT = S.sb("xT", [128, KD, NTOK])
        wr = [S.sb(f"wr{l}", [128, KD, 36]) for l in range(2)]
        br = [S.sb(f"br{l}", [128, 36]) for l in range(2)]
        lg = S.sb("lg", [128, 5, 36])

        def C(name):
            return consts[:, cols[name][0]:cols[name][1]]

        pages = S.sb("pages", [128, NB * NPG // 4], I32)

        with Scope(nc, "mix") as s:
            yo = s.sb("yo", [128, 5, 1024])
            I = MixerInputs(nc, A, s)
            load_stage(nc, A, C, consts, X, I, wr, br, pages)
            transpose_stage(nc, "xt", C, X, xT)
            mixer_ab(nc, A, C, xT, yo, yd, cleared, I)
        for l in range(2):
            if l == 1:
                reset_stage(nc)
                mixer_cd(nc, A, C, xT, pages)
            reset_stage(nc)
            with Scope(nc, f"m{l}") as M:
                E = Experts(nc, A, M, l)
                finish_stage(nc, f"n{l}0", C, X, A["ln_g"][l, 0], A["ln_b"][l, 0],
                             proj=(xT, A["cd_w_out" if l else "ab_w_out"]), xT=xT, router=(wr[l], br[l], lg), rows=xd,
                             ahead=E)
                route(nc, f"r{l}", C, lg, xT, E)
                expert_stage(nc, f"e{l}", C, E, xT, xd, yd, range(NE // 2))
                expert_stage(nc, f"f{l}", C, E, xT, xd, yd, range(NE // 2, NE // 2 + 1))
                expert_stage(nc, f"g{l}", C, E, xT, xd, yd, range(NE // 2 + 1, NPAIR))
                finish_stage(nc, f"n{l}1", C, X, A["ln_g"][l, 1], A["ln_b"][l, 1],
                             experts=(yd, E), xT=None if l else xT,
                             out=(A["y_p"], A["y_s"]) if l else None)


def kernel(**inputs):
    import concourse.bacc as bacc
    import concourse.bass_utils as bass_utils

    nc = bacc.Bacc("TRN2", target_bir_lowering=False, num_devices=1)
    table, cols = constants()
    arrays = {n: np.ascontiguousarray(inputs[n]) for n in IN}
    arrays["consts"] = table
    A = {}
    feed = {}
    for n, a in arrays.items():
        A[n] = nc.dram_tensor("in_" + n, a.shape, mybir.dt.from_np(a.dtype), kind="ExternalInput").ap()
        feed["in_" + n] = a
    for n, shape in OUT:
        A[n] = nc.dram_tensor("out_" + n, shape, F32, kind="ExternalOutput").ap()
    build(nc, A, cols, table.shape[1])
    r = bass_utils.run_bass_kernel_spmd(nc, [feed], core_ids=[0])
    return tuple(r.results[0]["out_" + n] for n, _ in OUT)
```
